# Optimizing a Trainium2 kernel written in Bass

```python
import math
import jax, jax.numpy as jnp
from jax import lax
import numpy as np

D_MODEL = 1024
BATCH = 1
SEQ = 128
DEPTH = 2
DEC_BATCH = 1
DEC_SEQ = 256
PAST_LEN = 128

GRID_W = 64
MIX_W = D_MODEL // 4
N_BRANCH = 4
MLSTM_HEADS = 4
MLSTM_DK = MIX_W // MLSTM_HEADS
MLSTM_DV = MIX_W // MLSTM_HEADS
NA_HEADS = 4
NA_HEAD_DIM = MIX_W // NA_HEADS
NA_WIN_R = 8
NA_WIN_C = 16
DIFF_HEADS = 4
DIFF_V_DIM = MIX_W // DIFF_HEADS
DIFF_QK_DIM = DIFF_V_DIM // 2
SSM_HEADS = 4
SSM_HEAD_DIM = MIX_W // SSM_HEADS
SSM_GROUPS = 2
SSM_STATE = 64
SSM_CONV_K = 5
SSM_CONV_CH = MIX_W + 2 * SSM_GROUPS * SSM_STATE
CHUNK = 64
Q_BLOCK = 128
N_EXPERTS = 16
EXPERT_FF = 1024
CAPACITY_FACTOR = 2
ROPE_BASE = 10000.0
EPS = 1e-6
SPLITS = (MIX_W, MIX_W, MIX_W, MIX_W, 4 * MLSTM_HEADS, MIX_W, MIX_W, MIX_W, MIX_W, MIX_W, MIX_W, MIX_W, SSM_CONV_CH, 2 * SSM_HEADS, N_BRANCH * D_MODEL)
IN_COLS = sum(SPLITS)

kernel_name = 'hybrid_diffusion_mlstm_na_diff_ssd_ec_step'

def rms_norm(x, w):
    xf = x.astype(jnp.float32)
    y = xf * lax.rsqrt(jnp.mean(xf * xf, axis=-1, keepdims=True) + EPS)
    return (y * w.astype(jnp.float32)).astype(x.dtype)

def split_cols(u):
    points, acc = [], 0
    for s in SPLITS[:-1]:
        acc += s
        points.append(acc)
    return jnp.split(u, points, axis=-1)

def to_blocks(t, size):
    b, s = t.shape[:2]
    return jnp.moveaxis(t.reshape((b, s // size, size) + t.shape[2:]), 1, 0)

def from_blocks(t):
    t = jnp.moveaxis(t, 0, 1)
    return t.reshape((t.shape[0], t.shape[1] * t.shape[2]) + t.shape[3:])

def rev(t):
    return jnp.flip(t, axis=1)

def rope_2d(x, n_tokens):
    t = jnp.arange(n_tokens)
    half = x.shape[-1] // 2
    nf = half // 2
    inv = ROPE_BASE ** (-jnp.arange(nf, dtype=jnp.float32) / nf)
    bshape = (1, n_tokens) + (1,) * (x.ndim - 3) + (nf,)

    def rot(xs, pos):
        ang = (pos.astype(jnp.float32)[:, None] * inv).reshape(bshape)
        cos, sin = jnp.cos(ang), jnp.sin(ang)
        x1, x2 = xs[..., :nf], xs[..., nf:]
        return jnp.concatenate([x1 * cos - x2 * sin, x1 * sin + x2 * cos], axis=-1)

    out = jnp.concatenate([rot(x[..., :half], t // GRID_W), rot(x[..., half:], t % GRID_W)], axis=-1)
    return out.astype(x.dtype)

def modulation(cvec, w_ada, b_ada):
    m = (jax.nn.silu(cvec) @ w_ada + b_ada)[:, None, :]
    return jnp.split(m, 6, axis=-1)

def block_attention(q, k, v, scale):
    def one(qi):
        s = jnp.einsum('bqhd,bkhd->bhqk', qi, k).astype(jnp.float32) * scale
        p = jax.nn.softmax(s, axis=-1).astype(v.dtype)
        return jnp.einsum('bhqk,bkhd->bqhd', p, v)
    return from_blocks(lax.map(one, to_blocks(q, Q_BLOCK)))

def mlstm_scan(q, k, v, ig, lf, C0, n0, m0):
    tril = jnp.tril(jnp.ones((CHUNK, CHUNK), bool))

    def step(carry, inp):
        C, n, m = carry
        qc, kc, vc, ic, fc = inp
        b = jnp.moveaxis(jnp.cumsum(fc, axis=1), 2, 1)
        it = jnp.moveaxis(ic, 2, 1)
        dmat = jnp.where(tril, b[..., :, None] - b[..., None, :] + it[..., None, :], -jnp.inf)
        g = b + m[..., None]
        mt = jnp.maximum(g, jnp.max(dmat, axis=-1))
        s = jnp.einsum('blhd,bshd->bhls', qc, kc) * jnp.exp(dmat - mt[..., None])
        w_prev = jnp.exp(g - mt)
        num = jnp.einsum('bhls,bshe->bhle', s, vc) + jnp.einsum('blhd,bhde->bhle', qc, C) * w_prev[..., None]
        den = jnp.sum(s, axis=-1) + jnp.einsum('blhd,bhd->bhl', qc, n) * w_prev
        h = num / jnp.maximum(jnp.abs(den), jnp.exp(-mt))[..., None]
        bl = b[..., -1]
        lw = bl[..., None] - b + it
        m_new = jnp.maximum(bl + m, jnp.max(lw, axis=-1))
        ws = jnp.exp(lw - m_new[..., None])
        dec = jnp.exp(bl + m - m_new)
        C_new = dec[..., None, None] * C + jnp.einsum('bhs,bshd,bshe->bhde', ws, kc, vc)
        n_new = dec[..., None] * n + jnp.einsum('bhs,bshd->bhd', ws, kc)
        return (C_new, n_new, m_new), jnp.moveaxis(h, 1, 2)

    inp = tuple(to_blocks(t, CHUNK) for t in (q, k, v, ig, lf))
    (C, n, m), hs = lax.scan(step, (C0, n0, m0), inp)
    return from_blocks(hs), (C, n, m)

def mlstm_mixer(q, k, v, o, g_pre, gate_b, norm_w, state):
    B, S, _ = q.shape
    f32 = jnp.float32
    qh = q.reshape(B, S, MLSTM_HEADS, MLSTM_DK).astype(f32)
    kh = k.reshape(B, S, MLSTM_HEADS, MLSTM_DK).astype(f32) * (MLSTM_DK ** -0.5)
    vh = v.reshape(B, S, MLSTM_HEADS, MLSTM_DV).astype(f32)
    g = g_pre.reshape(B, S, 2, 2, MLSTM_HEADS).astype(f32) + gate_b.astype(f32)
    ig = g[:, :, :, 0]
    lf = jax.nn.log_sigmoid(g[:, :, :, 1])
    if state is None:
        C0 = jnp.zeros((B, 2, MLSTM_HEADS, MLSTM_DK, MLSTM_DV), f32)
        n0 = jnp.zeros((B, 2, MLSTM_HEADS, MLSTM_DK), f32)
        m0 = jnp.zeros((B, 2, MLSTM_HEADS), f32)
    else:
        C0, n0, m0 = (s.astype(f32) for s in state)
    hf, (Cf, nf, mf) = mlstm_scan(qh, kh, vh, ig[:, :, 0], lf[:, :, 0], C0[:, 0], n0[:, 0], m0[:, 0])
    hb, (Cb, nb, mb) = mlstm_scan(rev(qh), rev(kh), rev(vh), rev(ig[:, :, 1]), rev(lf[:, :, 1]), C0[:, 1], n0[:, 1], m0[:, 1])
    h = rms_norm(hf + rev(hb), norm_w.reshape(MLSTM_HEADS, MLSTM_DV))
    out = h.reshape(B, S, MIX_W) * jax.nn.sigmoid(o.astype(f32))
    new_state = (jnp.stack([Cf, Cb], axis=1), jnp.stack([nf, nb], axis=1), jnp.stack([mf, mb], axis=1))
    return out.astype(q.dtype), new_state

def na_mixer(q, k, v, qn_w, kn_w, rpb, ctx_kv):
    B, S, _ = q.shape
    H, D = NA_HEADS, NA_HEAD_DIM
    scale = D ** -0.5
    qh = rms_norm(q.reshape(B, S, H, D), qn_w)
    kh = rms_norm(k.reshape(B, S, H, D), kn_w)
    vh = v.reshape(B, S, H, D)
    if ctx_kv is None:
        out = block_attention(qh, kh, vh, scale)
        return out.reshape(B, S, MIX_W), (kh, vh)
    k_ctx, v_ctx = ctx_kv
    rows = S // GRID_W
    wr, wc = min(NA_WIN_R, rows), NA_WIN_C
    ri, ci = jnp.arange(rows), jnp.arange(GRID_W)
    row_idx = jnp.clip(ri - wr // 2, 0, rows - wr)[:, None] + jnp.arange(wr)
    col_idx = jnp.clip(ci - wc // 2, 0, GRID_W - wc)[:, None] + jnp.arange(wc)
    dr = row_idx - ri[:, None] + (NA_WIN_R - 1)
    dc = col_idx - ci[:, None] + (NA_WIN_C - 1)
    bias = rpb[:, dr[:, None, :, None], dc[None, :, None, :]]
    qg = qh.reshape(B, rows, GRID_W, H, D)
    k_win = kh.reshape(B, rows, GRID_W, H, D)[:, row_idx][:, :, :, col_idx]
    v_win = vh.reshape(B, rows, GRID_W, H, D)[:, row_idx][:, :, :, col_idx]
    s_win = jnp.einsum('bijhd,birjwhd->bhijrw', qg, k_win).astype(jnp.float32) * scale + bias[None].astype(jnp.float32)
    s_win = s_win.reshape(B, H, rows, GRID_W, wr * wc)
    s_ctx = jnp.einsum('bijhd,bthd->bhijt', qg, k_ctx).astype(jnp.float32) * scale
    p = jax.nn.softmax(jnp.concatenate([s_win, s_ctx], axis=-1), axis=-1).astype(v.dtype)
    p_win = p[..., :wr * wc].reshape(B, H, rows, GRID_W, wr, wc)
    p_ctx = p[..., wr * wc:]
    out = jnp.einsum('bhijrw,birjwhd->bijhd', p_win, v_win) + jnp.einsum('bhijt,bthd->bijhd', p_ctx, v_ctx)
    return out.reshape(B, S, MIX_W), None

def diff_attention(q, k, v, lam):
    scale = DIFF_QK_DIM ** -0.5

    def one(qi):
        s = jnp.einsum('bqhmd,bkhmd->bhmqk', qi, k).astype(jnp.float32) * scale
        p = jax.nn.softmax(s, axis=-1)
        a = (p[:, :, 0] - lam * p[:, :, 1]).astype(v.dtype)
        return jnp.einsum('bhqk,bkhd->bqhd', a, v)
    return from_blocks(lax.map(one, to_blocks(q, Q_BLOCK)))

def diff_mixer(q, k, v, qn_w, kn_w, lam_vecs, norm_w, lam_init, ctx_kv):
    B, S, _ = q.shape
    H, Dq = DIFF_HEADS, DIFF_QK_DIM
    qh = rms_norm(q.reshape(B, S, H, 2, Dq), qn_w)
    kh = rms_norm(k.reshape(B, S, H, 2, Dq), kn_w)
    vh = v.reshape(B, S, H, DIFF_V_DIM)
    lv = lam_vecs.astype(jnp.float32)
    lam = jnp.exp(jnp.sum(lv[0] * lv[1])) - jnp.exp(jnp.sum(lv[2] * lv[3])) + lam_init
    if ctx_kv is None:
        o = diff_attention(qh, kh, vh, lam)
        new = (kh.reshape(B, S, H, 2 * Dq), vh)
    else:
        k_ctx, v_ctx = ctx_kv
        keys = jnp.concatenate([rope_2d(kh, S), k_ctx.reshape(B, k_ctx.shape[1], H, 2, Dq).astype(kh.dtype)], axis=1)
        vals = jnp.concatenate([vh, v_ctx.astype(vh.dtype)], axis=1)
        o = diff_attention(rope_2d(qh, S), keys, vals, lam)
        new = None
    o = rms_norm(o, norm_w) * (1.0 - lam_init)
    return o.reshape(B, S, MIX_W), new

def centred_dwconv(x, w, b):
    pad = w.shape[0] // 2
    y = lax.conv_general_dilated(x, w[:, None, :].astype(x.dtype), window_strides=(1,), padding=[(pad, pad)],
                                 dimension_numbers=('NWC', 'WIO', 'NWC'), feature_group_count=x.shape[-1])
    return y + b

def ssd_scan(x, dt, A, Bm, Cm, h0):
    tril = jnp.tril(jnp.ones((CHUNK, CHUNK), bool))
    xdt = x * dt[..., None]
    a = dt * A

    def step(h, inp):
        xc, ac, bc, cc = inp
        acum = jnp.moveaxis(jnp.cumsum(ac, axis=1), 2, 1)
        seg = jnp.where(tril, acum[..., :, None] - acum[..., None, :], -jnp.inf)
        scores = jnp.einsum('blhn,bshn->bhls', cc, bc) * jnp.exp(seg)
        y = jnp.einsum('bhls,bshp->blhp', scores, xc) + jnp.einsum('blhn,bhpn->blhp', cc, h) * jnp.moveaxis(jnp.exp(acum), 1, 2)[..., None]
        dec = jnp.exp(acum[..., -1:] - acum)
        h_new = jnp.exp(acum[..., -1])[..., None, None] * h + jnp.einsum('bhs,bshn,bshp->bhpn', dec, bc, xc)
        return h_new, y

    inp = tuple(to_blocks(t, CHUNK) for t in (xdt, a, Bm, Cm))
    h_fin, ys = lax.scan(step, h0, inp)
    return from_blocks(ys), h_fin

def ssm_mixer(z, xbc, dt_pre, conv_w, conv_b, dt_bias, a_log, d_skip, norm_w, state):
    B, S, _ = z.shape
    f32 = jnp.float32
    xbc = jax.nn.silu(centred_dwconv(xbc, conv_w, conv_b))
    xs, bm, cm = jnp.split(xbc, [MIX_W, MIX_W + SSM_GROUPS * SSM_STATE], axis=-1)
    rep = SSM_HEADS // SSM_GROUPS
    x = xs.reshape(B, S, SSM_HEADS, SSM_HEAD_DIM).astype(f32)
    bm = jnp.repeat(bm.reshape(B, S, SSM_GROUPS, SSM_STATE), rep, axis=2).astype(f32)
    cm = jnp.repeat(cm.reshape(B, S, SSM_GROUPS, SSM_STATE), rep, axis=2).astype(f32)
    dt = jax.nn.softplus(dt_pre.reshape(B, S, 2, SSM_HEADS).astype(f32) + dt_bias.astype(f32))
    A = -jnp.exp(a_log.astype(f32))
    if state is None:
        h0 = jnp.zeros((B, 2, SSM_HEADS, SSM_HEAD_DIM, SSM_STATE), f32)
    else:
        h0 = state.astype(f32)
    yf, hf = ssd_scan(x, dt[:, :, 0], A[0], bm, cm, h0[:, 0])
    yb, hb = ssd_scan(rev(x), rev(dt[:, :, 1]), A[1], rev(bm), rev(cm), h0[:, 1])
    y = yf + rev(yb) + d_skip.astype(f32)[:, None] * x
    y = rms_norm(y.reshape(B, S, MIX_W) * jax.nn.silu(z.astype(f32)), norm_w)
    return y.astype(z.dtype), jnp.stack([hf, hb], axis=1)

def expert_choice_ffn(h, w_router, w_gate, w_up, w_down):
    B, T, D = h.shape
    cap = CAPACITY_FACTOR * T // N_EXPERTS
    aff = jax.nn.softmax((h @ w_router).astype(jnp.float32), axis=-1)
    g, idx = lax.top_k(jnp.swapaxes(aff, 1, 2), cap)
    xg = jax.vmap(lambda xb, ib: xb[ib])(h, idx)
    a = jnp.einsum('becd,edf->becf', xg, w_gate)
    u = jnp.einsum('becd,edf->becf', xg, w_up)
    y = jnp.einsum('becf,efd->becd', jax.nn.silu(a) * u, w_down) * g[..., None].astype(h.dtype)
    return jax.vmap(lambda yb, ib: jnp.zeros((T, D), yb.dtype).at[ib.reshape(-1)].add(yb.reshape(-1, D)))(y, idx)

def trunk_layer(x, cvec, p, lam_init, ctx):
    B, S, _ = x.shape
    shift1, scale1, gate1, shift2, scale2, gate2 = modulation(cvec, p['w_ada'], p['b_ada'])
    h = rms_norm(x, p['norm1_w']) * (1 + scale1) + shift1
    (mq, mk, mv, mo, mg, nq, nk, nv, dq, dk, dv, sz, sxbc, sdt, gpre) = split_cols(h @ p['w_in'])
    if ctx is None:
        na_ctx, diff_ctx, m_state, s_state = None, None, None, None
    else:
        na_ctx, diff_ctx, m_state, s_state = ctx
    a_out, m_new = mlstm_mixer(mq, mk, mv, mo, mg, p['mlstm_gate_b'], p['mlstm_norm_w'], m_state)
    b_out, na_new = na_mixer(nq, nk, nv, p['na_qnorm_w'], p['na_knorm_w'], p['na_rpb'], na_ctx)
    c_out, diff_new = diff_mixer(dq, dk, dv, p['diff_qnorm_w'], p['diff_knorm_w'], p['diff_lambda'], p['diff_norm_w'], lam_init, diff_ctx)
    d_out, s_new = ssm_mixer(sz, sxbc, sdt, p['ssm_conv_w'], p['ssm_conv_b'], p['ssm_dt_bias'], p['ssm_a_log'], p['ssm_d'], p['ssm_norm_w'], s_state)
    br = jnp.stack([a_out, b_out, c_out, d_out], axis=2)
    gates = jax.nn.sigmoid(gpre.reshape(B, S, N_BRANCH, D_MODEL))
    mixed = jnp.sum(gates * jnp.einsum('bsnc,ncd->bsnd', br, p['w_branch']), axis=2)
    x = x + gate1 * (mixed @ p['w_out'])
    h2 = rms_norm(x, p['norm2_w']) * (1 + scale2) + shift2
    x = x + gate2 * expert_choice_ffn(h2, p['w_router'], p['w_gate'], p['w_up'], p['w_down'])
    return x, (na_new, diff_new, m_new, s_new)

def setup_inputs(seed: int = 0) -> dict:
    key = jax.random.key(seed)
    ks = iter(jax.random.split(key, 64))
    f32 = jnp.float32

    def nrm(shape, s=1.0):
        return s * jax.random.normal(next(ks), shape, f32)

    D = D_MODEL
    x_prompt = nrm((BATCH, SEQ, D))
    x_sample = nrm((DEC_BATCH, DEC_SEQ, D))
    cache_na_k = nrm((DEC_BATCH, DEPTH, PAST_LEN, NA_HEADS, NA_HEAD_DIM))
    cache_na_v = nrm((DEC_BATCH, DEPTH, PAST_LEN, NA_HEADS, NA_HEAD_DIM))
    cache_diff_k = nrm((DEC_BATCH, DEPTH, PAST_LEN, DIFF_HEADS, 2 * DIFF_QK_DIM))
    cache_diff_v = nrm((DEC_BATCH, DEPTH, PAST_LEN, DIFF_HEADS, DIFF_V_DIM))
    state_mlstm_C = nrm((DEC_BATCH, DEPTH, 2, MLSTM_HEADS, MLSTM_DK, MLSTM_DV), 0.5)
    state_mlstm_n = nrm((DEC_BATCH, DEPTH, 2, MLSTM_HEADS, MLSTM_DK), 0.5)
    state_mlstm_m = nrm((DEC_BATCH, DEPTH, 2, MLSTM_HEADS))
    state_ssm = nrm((DEC_BATCH, DEPTH, 2, SSM_HEADS, SSM_HEAD_DIM, SSM_STATE), 0.5)
    c = nrm((DEC_BATCH, D))
    c_ctx = nrm((D,))
    norm1_w = 1.0 + nrm((DEPTH, D), 0.02)
    norm2_w = 1.0 + nrm((DEPTH, D), 0.02)
    w_ada = nrm((DEPTH, D, 6 * D), 0.5 * D ** -0.5)
    b_ada = nrm((DEPTH, 6 * D), 0.02)
    w_in = nrm((DEPTH, D, IN_COLS), D ** -0.5)
    mlstm_gate_b = jnp.concatenate([nrm((DEPTH, 2, 1, MLSTM_HEADS), 0.1), 3.0 + nrm((DEPTH, 2, 1, MLSTM_HEADS), 0.5)], axis=2)
    mlstm_norm_w = 1.0 + nrm((DEPTH, MIX_W), 0.02)
    na_qnorm_w = 1.0 + nrm((DEPTH, NA_HEAD_DIM), 0.02)
    na_knorm_w = 1.0 + nrm((DEPTH, NA_HEAD_DIM), 0.02)
    na_rpb = nrm((DEPTH, NA_HEADS, 2 * NA_WIN_R - 1, 2 * NA_WIN_C - 1), 0.1)
    diff_qnorm_w = 1.0 + nrm((DEPTH, DIFF_QK_DIM), 0.02)
    diff_knorm_w = 1.0 + nrm((DEPTH, DIFF_QK_DIM), 0.02)
    diff_lambda = nrm((DEPTH, 4, DIFF_QK_DIM), 0.1)
    diff_norm_w = 1.0 + nrm((DEPTH, DIFF_V_DIM), 0.02)
    ssm_conv_w = nrm((DEPTH, SSM_CONV_K, SSM_CONV_CH), SSM_CONV_K ** -0.5)
    ssm_conv_b = nrm((DEPTH, SSM_CONV_CH), 0.02)
    u = jax.random.uniform(next(ks), (DEPTH, 2, SSM_HEADS), f32)
    dt0 = jnp.exp(u * (math.log(0.1) - math.log(0.001)) + math.log(0.001))
    ssm_dt_bias = dt0 + jnp.log(-jnp.expm1(-dt0))
    ssm_a_log = jnp.log(jax.random.uniform(next(ks), (DEPTH, 2, SSM_HEADS), f32, minval=1.0, maxval=16.0))
    ssm_d = 1.0 + nrm((DEPTH, SSM_HEADS), 0.1)
    ssm_norm_w = 1.0 + nrm((DEPTH, MIX_W), 0.02)
    w_branch = nrm((DEPTH, N_BRANCH, MIX_W, D), MIX_W ** -0.5)
    w_out = nrm((DEPTH, D, D), D ** -0.5)
    w_router = nrm((DEPTH, D, N_EXPERTS), D ** -0.5)
    w_gate = nrm((DEPTH, N_EXPERTS, D, EXPERT_FF), D ** -0.5)
    w_up = nrm((DEPTH, N_EXPERTS, D, EXPERT_FF), D ** -0.5)
    w_down = nrm((DEPTH, N_EXPERTS, EXPERT_FF, D), EXPERT_FF ** -0.5)
    return {'x_prompt': x_prompt, 'x_sample': x_sample, 'cache_na_k': cache_na_k, 'cache_na_v': cache_na_v,
            'cache_diff_k': cache_diff_k, 'cache_diff_v': cache_diff_v, 'state_mlstm_C': state_mlstm_C,
            'state_mlstm_n': state_mlstm_n, 'state_mlstm_m': state_mlstm_m, 'state_ssm': state_ssm,
            'c': c, 'c_ctx': c_ctx, 'norm1_w': norm1_w, 'norm2_w': norm2_w, 'w_ada': w_ada, 'b_ada': b_ada,
            'w_in': w_in, 'mlstm_gate_b': mlstm_gate_b, 'mlstm_norm_w': mlstm_norm_w, 'na_qnorm_w': na_qnorm_w,
            'na_knorm_w': na_knorm_w, 'na_rpb': na_rpb, 'diff_qnorm_w': diff_qnorm_w, 'diff_knorm_w': diff_knorm_w,
            'diff_lambda': diff_lambda, 'diff_norm_w': diff_norm_w, 'ssm_conv_w': ssm_conv_w, 'ssm_conv_b': ssm_conv_b,
            'ssm_dt_bias': ssm_dt_bias, 'ssm_a_log': ssm_a_log, 'ssm_d': ssm_d, 'ssm_norm_w': ssm_norm_w,
            'w_branch': w_branch, 'w_out': w_out, 'w_router': w_router, 'w_gate': w_gate, 'w_up': w_up, 'w_down': w_down}

def reference(x_prompt, x_sample, cache_na_k, cache_na_v, cache_diff_k, cache_diff_v, state_mlstm_C, state_mlstm_n,
              state_mlstm_m, state_ssm, c, c_ctx, norm1_w, norm2_w, w_ada, b_ada, w_in, mlstm_gate_b, mlstm_norm_w,
              na_qnorm_w, na_knorm_w, na_rpb, diff_qnorm_w, diff_knorm_w, diff_lambda, diff_norm_w, ssm_conv_w,
              ssm_conv_b, ssm_dt_bias, ssm_a_log, ssm_d, ssm_norm_w, w_branch, w_out, w_router, w_gate, w_up, w_down):
    y_prompt, y_sample = x_prompt, x_sample
    na_k_l, na_v_l, df_k_l, df_v_l, mC_l, mn_l, mm_l, ss_l = [], [], [], [], [], [], [], []
    for l in range(DEPTH):
        p = {'norm1_w': norm1_w[l], 'norm2_w': norm2_w[l], 'w_ada': w_ada[l], 'b_ada': b_ada[l], 'w_in': w_in[l],
             'mlstm_gate_b': mlstm_gate_b[l], 'mlstm_norm_w': mlstm_norm_w[l], 'na_qnorm_w': na_qnorm_w[l],
             'na_knorm_w': na_knorm_w[l], 'na_rpb': na_rpb[l], 'diff_qnorm_w': diff_qnorm_w[l],
             'diff_knorm_w': diff_knorm_w[l], 'diff_lambda': diff_lambda[l], 'diff_norm_w': diff_norm_w[l],
             'ssm_conv_w': ssm_conv_w[l], 'ssm_conv_b': ssm_conv_b[l], 'ssm_dt_bias': ssm_dt_bias[l],
             'ssm_a_log': ssm_a_log[l], 'ssm_d': ssm_d[l], 'ssm_norm_w': ssm_norm_w[l], 'w_branch': w_branch[l],
             'w_out': w_out[l], 'w_router': w_router[l], 'w_gate': w_gate[l], 'w_up': w_up[l], 'w_down': w_down[l]}
        lam_init = 0.8 - 0.6 * math.exp(-0.3 * l)
        y_prompt, (na_kv, diff_kv, m_st, s_st) = trunk_layer(y_prompt, c_ctx[None, :], p, lam_init, None)
        na_k_l.append(na_kv[0]); na_v_l.append(na_kv[1])
        df_k_l.append(diff_kv[0]); df_v_l.append(diff_kv[1])
        mC_l.append(m_st[0]); mn_l.append(m_st[1]); mm_l.append(m_st[2]); ss_l.append(s_st)
        ctx = ((cache_na_k[:, l], cache_na_v[:, l]), (cache_diff_k[:, l], cache_diff_v[:, l]),
               (state_mlstm_C[:, l], state_mlstm_n[:, l], state_mlstm_m[:, l]), state_ssm[:, l])
        y_sample, _ = trunk_layer(y_sample, c, p, lam_init, ctx)
    new_na_k = jnp.stack(na_k_l, axis=1)
    new_na_v = jnp.stack(na_v_l, axis=1)
    new_diff_k = jnp.stack(df_k_l, axis=1)
    new_diff_v = jnp.stack(df_v_l, axis=1)
    new_mlstm_C = jnp.stack(mC_l, axis=1)
    new_mlstm_n = jnp.stack(mn_l, axis=1)
    new_mlstm_m = jnp.stack(mm_l, axis=1)
    new_ssm = jnp.stack(ss_l, axis=1)
    return (y_prompt, y_sample, new_na_k, new_na_v, new_diff_k, new_diff_v, new_mlstm_C, new_mlstm_n, new_mlstm_m, new_ssm)


_drawn_inputs = setup_inputs


def setup_inputs(seed=0):
    import zlib

    import numpy as np

    out = dict(_drawn_inputs(seed))
    spreads = {}
    factors = {'cache_na_k': 3.01,
     'state_mlstm_C': 2.904,
     'state_mlstm_n': 6.664,
     'state_mlstm_m': 4.808,
     'norm2_w': 7.028,
     'mlstm_norm_w': 8.0,
     'na_qnorm_w': 8.0,
     'na_knorm_w': 2.796,
     'na_rpb': 8.0,
     'diff_qnorm_w': 8.0,
     'diff_lambda': 5.632,
     'diff_norm_w': 8.0,
     'ssm_norm_w': 8.0}
    for name, (base, spread) in spreads.items():
        noise = np.random.default_rng([zlib.crc32(name.encode()), seed]).standard_normal(out[name].shape)
        drawn = base * np.exp(spread * noise) if base else spread * noise
        out[name] = __import__('jax').numpy.asarray(drawn.astype(out[name].dtype))
    for name, factor in factors.items():
        out[name] = (out[name] * factor).astype(out[name].dtype)
    return out
```

```python
import math
from contextlib import ExitStack

import numpy as np

import concourse.bass as bass
from concourse import mybir

F32 = mybir.dt.float32
ALU = mybir.AluOpType
ACT = mybir.ActivationFunctionType
AX = mybir.AxisListType

D = 1024
KC = D // 128
L = 2
TT = 3
T = 128 * TT
NE = 16
IN_COLS = 7448
EPS = 1e-6
NEG = -1e30
RING = 4
SLOT = 4096

C_MQ, C_MV, C_MG, C_NQ, C_NV, C_DK, C_SZ, C_XBC, C_DT, C_GATE = 0, 512, 1024, 1040, 1552, 2064, 2576, 2832, 3344, 3352

ROW_WIDTHS = [("gate_b", 16), ("dt_bias", 8), ("a_log", 8), ("ssm_d", 4), ("na_qn", 64), ("na_kn", 64), ("diff_qn", 32),
              ("diff_kn", 32), ("diff_norm", 64), ("mlstm_norm", 256), ("ssm_norm", 256), ("lambda", 128), ("m0", 128)]
ROW, _at = {}, 0
for _n, _w in ROW_WIDTHS:
    ROW[_n] = (_at, _w)
    _at += _w
NROW = _at
COL_WIDTHS = [("norm1", 8), ("norm2", 8), ("b_ada", 48), ("conv_w", 20), ("conv_b", 4), ("m0", 1)]
COL, _at = {}, 0
for _n, _w in COL_WIDTHS:
    COL[_n] = (_at, _w)
    _at += _w
NCOL = _at
CST_WIDTHS = [("ident", 128), ("mask", 384), ("iota", 32), ("cos", 64), ("sin", 64), ("win", 64), ("adasel", 2),
              ("one", 1), ("eps", 1), ("mhalf", 1)]
CST, _at = {}, 0
for _n, _w in CST_WIDTHS:
    CST[_n] = (_at, _w)
    _at += _w
NCST = _at


SEEN = (((( 0, 0),), ((1, 128),), ((1, 256), (2, 384))), (((0, 0),), ((1, 128), (2, 256)), ((2, 384),)))
FILL_NA = (1, 3, 5, 7, 9)
FILL_DF = (1, 4, 7)


def constants():
    c = np.zeros((128, NCST), np.float32)

    def put(name, v):
        o, w = CST[name]
        c[:, o:o + w] = v

    p = np.arange(128)[:, None]
    q = np.arange(128)[None, :]
    put("ident", np.eye(128))
    fwd = np.where(q >= p, 0.0, NEG)
    bwd = np.where(q <= p, 0.0, NEG)
    put("mask", np.concatenate([fwd, np.zeros((128, 128)), bwd], 1))
    put("iota", np.arange(32)[None, :])
    nf = 8
    inv = 10000.0 ** (-np.arange(nf, dtype=np.float32) / np.float32(nf))
    cos, sin = np.zeros((128, 2, 2, 2, nf)), np.zeros((128, 2, 2, 2, nf))
    for tile in range(2):
        t = tile * 128 + np.arange(128)
        for half, pos in enumerate((t // 64, t % 64)):
            ang = (pos.astype(np.float32)[:, None] * inv).astype(np.float32)
            for x12 in range(2):
                cos[:, tile, half, x12] = np.cos(ang)
                sin[:, tile, half, x12] = np.sin(ang) * (-1.0 if x12 == 0 else 1.0)
    put("cos", cos.reshape(128, 64))
    put("sin", sin.reshape(128, 64))
    qc = np.arange(128) % 64
    lo = np.clip(qc - 8, 0, 48)[:, None]
    kc = np.arange(64)[None, :]
    put("win", np.where((kc >= lo) & (kc < lo + 16), 0.0, NEG))
    sel = np.zeros((128, 2))
    for g in range(4):
        for r in range(2):
            sel[32 * g + r, r] = 1.0
    put("adasel", sel)
    put("one", 1.0)
    put("eps", EPS)
    put("mhalf", -0.5)
    return c


NT = 12 + 7 + 12 + 2 + 6 * NE
N_PROJ = 23
PROJ_TILES = ((C_MQ, 512, 4), (C_NQ, 512, 7), (C_XBC, 512, 11), (C_MV, 512, 14), (C_NV, 512, 17), (C_DK, 512, 20), (C_SZ, 256, 23))
SEMS = ["ada_part", "ada_evac", "ada_sel", "mod_done", "proj_out", "proj_evac", "gpre_out", "xT_out", "xT_evac",
        "c_ready", "sq_ready", "ss_ready", "rms_ready", "h_ready", "small_used", "bm_loaded", "ctx_loaded",
        "gact_in", "gact_e", "gact_out", "gtm_ready", "growT", "rows_ready", "tmT", "tm_evac", "tm_ready", "tm_exp",
        "m_out", "pool_in", "pool_out", "conv_ready", "silu_t", "xs_ready", "xtr_out", "xtr_evac", "nan_ready", "ntr_out",
        "ntr_evac", "dfn_ready", "dtr_out", "dtr_evac", "s_out", "s_read", "p_exp", "p_ready", "pt_out", "pt_evac", "o_out", "o_evac",
        "ds_out", "d_max", "d_exp", "d_ready", "dpt_out", "dpt_evac", "do_out", "do_evac", "fill_out", "fill_evac",
        "row_out", "e_ready", "e_exp", "pm_ready", "sT_out", "num_out", "num_evac", "kt_out", "kw_ready", "st_out",
        "st_evac", "tanh_in", "tanh_out", "y_out", "y_evac", "brt_out", "brt_evac", "br_ready", "bp_out", "bp_evac",
        "mix_ready", "wo_out", "x1_ready", "rt_out", "rt_max", "rt_exp", "aff_ready", "afT", "pos_ready", "posT",
        "sel_ready", "h2t_out", "h2t_evac", "sgt_out", "sgt_evac", "xg_out", "xg_evac", "a_out", "u_out", "a_tanh", "hh_ready",
        "ht_out", "ht_evac", "yd_out", "yd_evac", "cb_out", "cb_evac", "x_ready", "yt_out", "yt_evac", "pool_init"]


def trunk_program(nc, dr, outs):
    (y_prompt, y_sample, new_na_k, new_na_v, new_diff_k, new_diff_v, new_C, new_n, new_m, new_ssm) = outs
    with ExitStack() as ctx:
        def sb(name, shape):
            return ctx.enter_context(nc.sbuf_tensor(name, shape, F32))

        sem = {n: ctx.enter_context(nc.semaphore(n)) for n in SEMS}
        landed = [ctx.enter_context(nc.semaphore(f"landed{i}")) for i in range(RING)]
        par_in = [ctx.enter_context(nc.semaphore(f"par_in{i}")) for i in range(3)]
        dve_step = ctx.enter_context(nc.semaphore("dve_step"))
        st_dma = {n: ctx.enter_context(nc.semaphore("st_" + n)) for n in ("nak", "nav", "dk", "dv", "C", "n", "m", "ssm", "y")}

        PS = ctx.enter_context(nc.psum_tensor("banks", [128, 8, 512], F32))
        ring = sb("ring", [128, RING, SLOT])
        wsm = sb("wsm", [128, KC, 24])
        wrt = sb("wrt", [128, KC, NE])
        xT = sb("xT", [128, KC, T])
        hT = sb("hT", [128, KC, T])
        cst = sb("cst", [128, NCST])
        rowp = sb("rowp", [128, NROW])
        colp = sb("colp", [128, NCOL])
        c32 = sb("c32", [128, KC, 32])
        mod = sb("mod", [128, 48, 2])
        amp = sb("amp", [128, 2, 8, 2])
        small = sb("small", [128, 536])
        WORK = 27500
        work = sb("work", [128, WORK])

        def K(name):
            o, w = CST[name]
            return cst[:, o:o + w]

        def RP(name):
            o, w = ROW[name]
            return rowp[:, o:o + w]

        def CP(name):
            o, w = COL[name]
            return colp[:, o:o + w]

        def region(base, end):
            at = [base]

            def take(shape):
                n = int(np.prod(shape))
                v = work[:, at[0]:at[0] + n]
                at[0] += n
                assert at[0] <= end, (at[0], end)
                if len(shape) == 1:
                    return v
                names = "abcd"[:len(shape)]
                spec = f"p ({' '.join(names)}) -> p {' '.join(names)}"
                return v.rearrange(spec, **{k: d for k, d in zip(names[1:], shape[1:])})
            take.at = at
            return take

        t = region(0, WORK)
        V1 = t([TT, 4, 65])
        MO = t([TT, 256])
        NAQK = t([TT, 512])
        base_nv = t.at[0]
        NV = t([TT, 256])
        DV = t([TT, 256])
        DQK = t([TT, 512])
        SZ = t([TT, 256])
        end_u = t.at[0]
        QKT = t([4, T])
        XS = t([4, T])
        base_ctx = t.at[0]
        KRAW = t([2, 256])
        KCT = t([4, 128])
        VC = t([2, 256])
        end_ctx = t.at[0] + 24
        t.at[0] = end_ctx
        base_cw = t.at[0]
        XB = t([4, 392])
        CV = t([4, 392])
        end_cw = t.at[0]
        base_pr = t.at[0]
        BM = t([2, 4, 256])
        PTS = t([2, 384])
        NAT = t([4, T])
        end_pr = t.at[0]
        ED = t([4, 384])
        EDf = ED.rearrange("p a b -> p (a b)")
        XTM = t([TT, 256])
        C0 = t([2, 2, 130])
        H0 = t([256])
        ROWS = t([3, T])
        TM = t([3, T])
        KW = ROWS[:, 1:3, :].rearrange("p a b -> p (a b)")[:, 0:512].rearrange("p (a b c) -> p a b c", a=2, b=4)
        BTM = ROWS[:, 1:3, :].rearrange("p a b -> p (a b)")[:, 512:640]
        base_gates = t.at[0]
        GATES = t([8, T])
        end_mix = t.at[0]
        r = region(base_nv, base_nv + 2 * 768)
        XDT = r([2, TT, 4, 64])
        r = region(base_ctx, end_ctx)
        NUM = r([2 * TT, 4, 65])
        r = region(base_cw, end_cw)
        W1 = r([1536])
        W2 = r([1536])
        r = region(base_pr, end_pr)
        PM = r([8, 512])
        r = region(base_pr, end_pr)
        BRT = r([8, T])
        r = region(0, end_u)
        r.at[0] = 0
        MIX = r([8, T])
        TMPB = r([2, T])
        GT = r([2, T])
        RSTD = W2[:, 0:T]
        QF = QKT.rearrange("p a b -> p (a b)")
        CN_OUT = QF[:, 0:520].rearrange("p (a b c) -> p a b c", a=2, b=4)
        SS_OUT = QF[:, 520:1032].rearrange("p (a b) -> p a b", a=8)
        MP = W1[:, 0:1024].rearrange("p (a b) -> p a b", a=2)

        m = region(0, WORK)
        XG = m([KC, NE, 2, 32])
        YS = m([4, D])
        YP = m([4, D])
        SGT = m([4, 256])
        SGP = m([4, 128])
        HH = m([2, 512])
        HTT = m([2, 4, 128])
        TH = m([512])
        SA = m([512])
        m2 = region(KC * NE * 64, KC * NE * 64 + 2 * 4 * D)
        H2M = m2([TT, D])
        SEL = m2([TT, NE, 32])
        SELG = m2([TT, NE, 32])
        POS = m2([TT, NE])
        AFF = m2([TT, NE])
        AFT = m2([T])
        WK = m2([T])
        MSK = m2([T])
        XIN = work[:, 0:TT * D].rearrange("p (a b) -> p a b", a=TT)
        YOUT = work[:, 0:TT * D].rearrange("p (a b) -> p a b", a=TT)

        sm = [0]

        def st(shape):
            n = int(np.prod(shape))
            v = small[:, sm[0]:sm[0] + n]
            sm[0] += n
            assert sm[0] <= 536, sm[0]
            if len(shape) == 1:
                return v
            names = "abcd"[:len(shape)]
            return v.rearrange(f"p ({' '.join(names)}) -> p {' '.join(names)}", **{k: d for k, d in zip(names[1:], shape[1:])})

        G1 = st([TT, 24])
        GA = st([TT, 24])
        GL = st([TT, 24])
        DTM = st([TT, 8])
        AEXP = st([8])
        WS = st([16])
        EMT = st([TT, 8])
        SS = st([TT * 24])
        RS = st([TT * 24])
        NM0 = st([1])
        MOUT = st([2])
        LAM = st([8])
        SMX = st([2, 2])
        SSUM = st([2, 2])
        SREC = st([2, 2])
        DMX = st([2, 2])
        DSUM = st([2, 2])
        DREC = st([2, 2])
        WPT = st([TT, 16])
        RMX = st([TT])
        RSUM = st([TT])
        TOP = st([8])

        ident = K("ident")
        zeros = K("iota")[:, 0:1]
        ones = K("one").broadcast_to([128, 128])

        def over(ap, axis, n):
            v = ap.unsqueeze(axis)
            shape = list(v.shape)
            shape[axis] = n
            return v.broadcast_to(shape)

        block = ctx.enter_context(nc.Block())

        @block.sync
        def _(sp):
            count = [0]

            def load(w, c0=0, width=512):
                n = count[0]
                count[0] += 1
                rows = w.shape[0] // 128
                dst = ring[:, n % RING, 0:rows * width].rearrange("p (k n) -> p k n", n=width)
                sp.dma_start(dst, w[:, c0:c0 + width].rearrange("(k p) n -> p k n", p=128)).then_inc(landed[n % RING], 16)

            def load_gate(l, n, half):
                load(dr["w_in"][l], C_GATE + D * n + 512 * half)

            def load_pair(w):
                for half in range(2):
                    load(w, 512 * half)

            for l in range(L):
                e0, f0 = NE * l, 32 * l
                for i in range(12):
                    if i >= RING:
                        sp.wait_ge(sem["ada_part"], 12 * l + i - RING + 1)
                    elif l and i == 0:
                        sp.wait_ge(sem["u_out"], e0)
                    elif l and i == 2:
                        sp.wait_ge(sem["yd_out"], e0)
                    load(dr["w_ada"][l], 512 * i)
                for i, (c0, width, _) in enumerate(PROJ_TILES):
                    if i < RING:
                        sp.wait_ge(sem["ada_part"], 12 * l + 8 + i + 1)
                    else:
                        sp.wait_ge(sem["proj_out"], N_PROJ * l + PROJ_TILES[i - RING][2])
                    load(dr["w_in"][l], c0, width)
                sp.wait_ge(sem["proj_out"], N_PROJ * l + PROJ_TILES[3][2])
                load_gate(l, 0, 0)
                sp.wait_ge(sem["proj_out"], N_PROJ * l + PROJ_TILES[4][2])
                load_gate(l, 0, 1)
                sp.wait_ge(sem["proj_out"], N_PROJ * l + PROJ_TILES[5][2])
                load(dr["w_branch"][l, 0], 0, 1024)
                sp.wait_ge(sem["proj_out"], N_PROJ * (l + 1))
                load(dr["w_branch"][l, 1], 0, 1024)
                sp.wait_ge(sem["fill_out"], f0 + 4)
                load_gate(l, 1, 0)
                sp.wait_ge(sem["fill_out"], f0 + 8)
                load_gate(l, 1, 1)
                sp.wait_ge(sem["bp_out"], f0 + 8)
                load(dr["w_branch"][l, 2], 0, 1024)
                sp.wait_ge(sem["bp_out"], f0 + 16)
                load_gate(l, 2, 0)
                sp.wait_ge(sem["fill_out"], f0 + 12)
                load_gate(l, 2, 1)
                sp.wait_ge(sem["fill_out"], f0 + 16)
                load(dr["w_branch"][l, 3], 0, 1024)
                sp.wait_ge(sem["bp_out"], f0 + 24)
                load_gate(l, 3, 0)
                sp.wait_ge(sem["fill_out"], f0 + 20)
                load_gate(l, 3, 1)
                sp.wait_ge(sem["fill_out"], f0 + 24)
                load(dr["w_out"][l], 0)
                sp.wait_ge(sem["bp_out"], f0 + 32)
                load(dr["w_out"][l], 512)
                sp.wait_ge(sem["fill_out"], f0 + 32)
                load_pair(dr["w_gate"][l, 0])
                sp.wait_ge(sem["wo_out"], 8 * (l + 1))
                load_pair(dr["w_up"][l, 0])
                sp.wait_ge(sem["a_out"], e0 + 1)
                load_pair(dr["w_gate"][l, 1])
                sp.wait_ge(sem["u_out"], e0 + 1)
                load_pair(dr["w_down"][l, 0])
                sp.wait_ge(sem["a_out"], e0 + 2)
                load_pair(dr["w_up"][l, 1])
                for e in range(2, NE):
                    sp.wait_ge(sem["yd_out"], e0 + e - 1)
                    load_pair(dr["w_gate"][l, e])
                    sp.wait_ge(sem["u_out"], e0 + e)
                    load_pair(dr["w_down"][l, e - 1])
                    sp.wait_ge(sem["a_out"], e0 + e + 1)
                    load_pair(dr["w_up"][l, e])
                sp.wait_ge(sem["yd_out"], e0 + NE - 1)
                load_pair(dr["w_down"][l, NE - 1])

        @block.gpsimd
        def _(pool):
            for l in range(L):
                if l:
                    pool.wait_ge(sem["x_ready"], l)
                pool.dma_start(rowp[:, :], dr["rowp"][l:l + 1, :].broadcast_to([128, NROW])).then_inc(par_in[1], 16)
                pool.dma_start(colp[:, :], dr["colp"][l]).then_inc(par_in[1], 16)
                pool.dma_start(wsm[:, :, 0:16], dr["w_in"][l, :, C_MG:C_MG + 16].rearrange("(k p) n -> p k n", p=128)).then_inc(par_in[1], 16)
                pool.dma_start(wsm[:, :, 16:24], dr["w_in"][l, :, C_DT:C_DT + 8].rearrange("(k p) n -> p k n", p=128)).then_inc(par_in[1], 16)
                pool.dma_start(wrt[:, :, :], dr["w_router"][l].rearrange("(k p) n -> p k n", p=128)).then_inc(par_in[1], 16)
                if l == 0:
                    pool.wait_ge(sem["xT_evac"], 6)
                pool.dma_start(KRAW[:, 0, :], dr["cache_na_k"][0, l].rearrange("t h d -> t (h d)")).then_inc(sem["ctx_loaded"], 16)
                pool.dma_start(KRAW[:, 1, :], dr["cache_diff_k"][0, l].rearrange("t h d -> t (h d)")).then_inc(sem["ctx_loaded"], 16)
                pool.dma_start(VC[:, 0, :], dr["cache_na_v"][0, l].rearrange("t h d -> t (h d)")).then_inc(sem["ctx_loaded"], 16)
                pool.dma_start(VC[:, 1, :], dr["cache_diff_v"][0, l].rearrange("t h d -> t (h d)")).then_inc(sem["ctx_loaded"], 16)
                pool.dma_start(C0[:, :, :, :], dr["c0n"][l].rearrange("p (a b c) -> p a b c", a=2, b=2)).then_inc(sem["ctx_loaded"], 16)
                pool.dma_start(H0[:, :], dr["h0t"][l]).then_inc(sem["ctx_loaded"], 16)
                for h in range(4):
                    for qr in range(4):
                        off = l * 4 * 465 + h * 465 + (7 - qr) * 31 - 48
                        src = bass.AP(dr["rpb_rev"].tensor, off, [[1, 64], [31, 4], [1, 64]])
                        dst = BM[64 * (qr % 2):64 * (qr % 2) + 64, qr // 2, h, :].rearrange("p (a b) -> p a b", a=4)
                        pool.dma_start(dst, src).then_inc(sem["bm_loaded"], 16)

                def power(i, n):
                    pool.wait_ge(sem["pool_in"], 4 * l + i + 1)
                    pool.tensor_tensor(RS[:, 0:n], SS[:, 0:n], K("mhalf").broadcast_to([128, n]), ALU.pow).then_inc(sem["pool_out"], 1)

                power(0, 72)
                pool.wait_ge(sem["nan_ready"], l + 1)
                pool.dma_start(new_na_k[0, l].rearrange("t h d -> t (h d)"), NAQK[:, 0, 256:512]).then_inc(st_dma["nak"], 16)
                pool.wait_ge(sem["proj_evac"], l * N_PROJ + 23)
                pool.dma_start(new_na_v[0, l].rearrange("t h d -> t (h d)"), NV[:, 0, :]).then_inc(st_dma["nav"], 16)
                pool.dma_start(new_diff_v[0, l].rearrange("t h d -> t (h d)"), DV[:, 0, :]).then_inc(st_dma["dv"], 16)
                pool.wait_ge(sem["dfn_ready"], l + 1)
                pool.dma_start(new_diff_k[0, l].rearrange("t h d -> t (h d)"), DQK[:, 0, 256:512]).then_inc(st_dma["dk"], 16)
                pool.wait_ge(sem["m_out"], l + 1)
                pool.dma_start(new_m[0, l, 0].rearrange("(h a) -> h a", a=1), MOUT[0:4, 0:1]).then_inc(st_dma["m"], 16)
                pool.dma_start(new_m[0, l, 1].rearrange("(h a) -> h a", a=1), MOUT[64:68, 1:2]).then_inc(st_dma["m"], 16)
                power(1, 12)
                power(2, 12)
                pool.wait_ge(sem["st_evac"], 3 * l + 2)
                for d in range(2):
                    pool.dma_start(new_C[0, l, d].rearrange("h d e -> d h e"), CN_OUT[0:64, d, :, 0:64]).then_inc(st_dma["C"], 16)
                    pool.dma_start(new_n[0, l, d].rearrange("h (d a) -> d h a", a=1), CN_OUT[0:64, d, :, 64:65], allow_slow_non_contiguous=True).then_inc(st_dma["n"], 16)
                power(3, 3)
                pool.wait_ge(sem["st_evac"], 3 * l + 3)
                pool.dma_start(new_ssm[0, l].rearrange("d h p n -> p (d h) n"), SS_OUT[0:64, :, :]).then_inc(st_dma["ssm"], 16)
            for t in range(TT):
                pool.wait_ge(sem["yt_evac"], 2 * t + 2)
                dst = y_prompt[0] if t == 0 else y_sample[0, 128 * (t - 1):128 * t, :]
                pool.dma_start(dst, YOUT[:, t, :]).then_inc(st_dma["y"], 16)
            for n, k in (("nak", 1), ("nav", 1), ("dk", 1), ("dv", 1), ("C", 2), ("n", 2), ("m", 2), ("ssm", 1)):
                pool.wait_ge(st_dma[n], 16 * k * L)
            pool.wait_ge(st_dma["y"], 16 * TT)

        @block.tensor
        def _(pe):
            def tile(n, b=512):
                pe.wait_ge(landed[n % RING], 16 * (n // RING + 1))
                a = 4096 // 512 if b == 512 else (8 if b == 256 else 2)
                return ring[:, n % RING, 0:a * b].rearrange("p (a b) -> p a b", b=b)

            pe.wait_ge(par_in[0], 16 * 3)
            for g in range(6):
                t, h = g // 2, g % 2
                for c in range(4):
                    mm = pe.transpose(PS[:, g, c * 128:(c + 1) * 128], XIN[:, t, (4 * h + c) * 128:(4 * h + c + 1) * 128], ident)
                mm.then_inc(sem["xT_out"], 1)
            pe.wait_ge(sem["xT_evac"], 6)
            pe.wait_ge(sem["c_ready"], 1)
            for l in range(L):
                n0 = l * NT
                if l:
                    pe.wait_ge(sem["x_ready"], l)

                def ada_turn(i):
                    pe.wait_ge(sem["ada_evac"], 12 * l + i + 1)
                    for j in range(4):
                        c = 4 * i + j
                        mm = pe.matmul(PS[:, 2, 2 * c:2 * c + 2], MP[:, i % 2, j * 128:(j + 1) * 128], K("adasel"), start=True, stop=True)
                    mm.then_inc(sem["ada_sel"], 1)

                for i in range(12):
                    w = tile(n0 + i)
                    if i >= 2:
                        pe.wait_ge(sem["ada_evac"], 12 * l + i - 1)
                    for k in range(KC):
                        g = k % 4
                        mm = pe.matmul(PS[32 * g:32 * g + 32, i % 2, :], c32[:, k, :], w[:, k, :], start=(k < 4), stop=(k >= 4),
                                       tile_position=(0, 32 * g))
                    mm.then_inc(sem["ada_part"], 1)
                    if i:
                        ada_turn(i - 1)
                ada_turn(11)

                def sum_squares(which, bank):
                    pe.wait_ge(sem["sq_ready"], 2 * l + which + 1)
                    for k in range(KC):
                        mm = pe.matmul(PS[:, bank, 0:T], ones, hT[:, k, :], start=(k == 0), stop=(k == KC - 1))
                    mm.then_inc(sem["ss_ready"], 1)

                sum_squares(0, 3)
                pe.wait_ge(sem["h_ready"], 2 * l + 1)

                pe.wait_ge(par_in[1], 80 * (l + 1))
                for t in range(TT):
                    for k in range(KC):
                        mm = pe.matmul(PS[:, 7, 24 * t:24 * t + 24], hT[:, k, t * 128:(t + 1) * 128], wsm[:, k, :],
                                       start=(k == 0), stop=(k == KC - 1))
                mm.then_inc(sem["gpre_out"], 1)

                po = [0]

                def out_bank():
                    j = po[0]
                    po[0] += 1
                    if j >= 4:
                        pe.wait_ge(sem["proj_evac"], l * N_PROJ + j - 3)
                    return j % 4

                def feature_major(n):
                    w = tile(n)
                    for c in range(4):
                        b = out_bank()
                        for k in range(KC):
                            mm = pe.matmul(PS[:, b, 0:T], w[:, k, c * 128:(c + 1) * 128], hT[:, k, :], start=(k == 0), stop=(k == KC - 1))
                        mm.then_inc(sem["proj_out"], 1)

                def token_major(n, width=512):
                    w = tile(n, width)
                    for t in range(TT):
                        b = out_bank()
                        for k in range(KC):
                            mm = pe.matmul(PS[:, b, 0:width], hT[:, k, t * 128:(t + 1) * 128], w[:, k, :], start=(k == 0), stop=(k == KC - 1))
                        mm.then_inc(sem["proj_out"], 1)

                def turn3(bank, src, width=128):
                    for t in range(TT):
                        mm = pe.transpose(PS[:, bank, t * 128:(t + 1) * 128], src(t), ident)
                    return mm

                n = n0 + 12
                feature_major(n)
                token_major(n + 1)
                feature_major(n + 2)
                token_major(n + 3)
                pe.wait_ge(sem["gtm_ready"], l + 1)
                turn3(4, lambda t: TM[:, 0, t * 128:(t + 1) * 128])
                turn3(5, lambda t: TM[:, 1, t * 128:(t + 1) * 128]).then_inc(sem["growT"], 1)
                token_major(n + 4)
                pe.wait_ge(sem["rows_ready"], l + 1)
                for i in range(3):
                    mm = turn3(4 + i, lambda t: ROWS[:, i, t * 128:(t + 1) * 128])
                mm.then_inc(sem["tmT"], 1)
                token_major(n + 5)
                token_major(n + 6, 256)

                pe.wait_ge(sem["xs_ready"], l + 1)
                pe.wait_ge(sem["tm_evac"], l + 1)
                for t in range(TT):
                    for c in range(2):
                        o = 256 * (t % 2) + 128 * c
                        pe.transpose(PS[:, 4 + t // 2, o:o + 128], XS[:, c, t * 128:(t + 1) * 128], ident)
                pe.transpose(PS[:, 5, 256:384], XS[:, 2, 0:128], ident).then_inc(sem["xtr_out"], 1)

                pe.wait_ge(sem["nan_ready"], l + 1)
                for t, b in ((0, 6), (1, 7), (2, 4)):
                    if t == 2:
                        pe.wait_ge(sem["xtr_evac"], l + 1)
                    for c in range(4):
                        mm = pe.transpose(PS[:, b, c * 128:(c + 1) * 128], NAQK[:, t, c * 128:(c + 1) * 128], ident)
                    mm.then_inc(sem["ntr_out"], 1)
                pe.wait_ge(sem["ctx_loaded"], 96 * (l + 1))
                for c in range(4):
                    mm = pe.transpose(PS[:, 5, c * 128:(c + 1) * 128], KRAW[:, c // 2, (c % 2) * 128:(c % 2) * 128 + 128], ident)
                mm.then_inc(sem["ntr_out"], 1)

                fills = [0]

                def fill():
                    j = fills[0]
                    fills[0] += 1
                    nb, dc = j // 8, j % 8
                    first = 19 if nb == 0 else 19 + 3 * nb + 1
                    w = tile(n0 + first + dc // 4)
                    if j >= 2:
                        pe.wait_ge(sem["fill_evac"], 32 * l + j - 1)
                    else:
                        pe.wait_ge(sem["proj_evac"], (l + 1) * N_PROJ)
                    for k in range(KC):
                        mm = pe.matmul(PS[:, j % 2, 0:T], w[:, k, (dc % 4) * 128:(dc % 4) * 128 + 128], hT[:, k, :], start=(k == 0), stop=(k == KC - 1))
                    mm.then_inc(sem["fill_out"], 1)

                units = [("p", 0), ("p", 1)] + [(t, h) for t in (1, 2) for h in range(4)]

                def na_scores(u):
                    if u >= 2:
                        pe.wait_ge(sem["s_read"], 10 * l + u - 1)
                    else:
                        pe.wait_ge(sem["proj_evac"], (l + 1) * N_PROJ)
                        pe.wait_ge(sem["ntr_evac"], 4 * (l + 1))
                    t, h = units[u]
                    b = 2 + u % 2
                    if t == "p":
                        lo = 64 * h
                        for c in range(2):
                            mm = pe.matmul(PS[:, b, c * 128:(c + 1) * 128], NAT[lo:lo + 64, c, 0:128], NAT[lo:lo + 64, 2 + c, 0:128], start=True, stop=True)
                    else:
                        lo, c = 64 * (h % 2), h // 2
                        q = NAT[lo:lo + 64, c, t * 128:(t + 1) * 128]
                        pe.matmul(PS[:, b, 0:256], q, NAT[lo:lo + 64, 2 + c, 128:384], start=True, stop=True)
                        mm = pe.matmul(PS[:, b, 256:384], q, KCT[lo:lo + 64, c, :], start=True, stop=True)
                    mm.then_inc(sem["s_out"], 1)

                def na_turn(u):
                    pe.wait_ge(sem["p_exp"], 10 * l + u + 1)
                    if u >= 2:
                        pe.wait_ge(sem["pt_evac"], 10 * l + u - 1)
                    for c in range(2 if units[u][0] == "p" else 3):
                        mm = pe.transpose(PS[:, 4 + u % 2, c * 128:(c + 1) * 128], ED[:, u % 2, c * 128:(c + 1) * 128], ident)
                    mm.then_inc(sem["pt_out"], 1)

                def na_out(u):
                    pe.wait_ge(sem["pt_evac"], 10 * l + u + 1)
                    if u >= 2:
                        pe.wait_ge(sem["o_evac"], 10 * l + u - 1)
                    t, h = units[u]
                    b = 6 + u % 2
                    if t == "p":
                        for c in range(2):
                            hh = 2 * c + h
                            mm = pe.matmul(PS[:, b, c * 64:c * 64 + 64], PTS[:, u % 2, c * 128:(c + 1) * 128], NV[:, 0, hh * 64:hh * 64 + 64], start=True, stop=True)
                    else:
                        vs = [NV[:, 1, h * 64:h * 64 + 64], NV[:, 2, h * 64:h * 64 + 64], VC[:, 0, h * 64:h * 64 + 64]]
                        for c in range(3):
                            mm = pe.matmul(PS[:, b, 0:64], PTS[:, u % 2, c * 128:(c + 1) * 128], vs[c], start=(c == 0), stop=(c == 2))
                    mm.then_inc(sem["o_out"], 1)

                for i in range(12):
                    if i < 10:
                        na_scores(i)
                    if i in FILL_NA:
                        fill()
                    if 1 <= i <= 10:
                        na_turn(i - 1)
                    if i >= 2:
                        na_out(i - 2)

                pe.wait_ge(sem["dfn_ready"], l + 1)
                pe.wait_ge(sem["s_read"], 10 * (l + 1))
                for t in range(TT):
                    for c in range(4):
                        mm = pe.transpose(PS[:, 2 + t, c * 128:(c + 1) * 128], DQK[:, t, c * 128:(c + 1) * 128], ident)
                    mm.then_inc(sem["dtr_out"], 1)
                dunits = [(t, h) for t in range(TT) for h in range(4)]

                def df_scores(u):
                    t, h = dunits[u]
                    if u >= 2:
                        pe.wait_ge(sem["d_exp"], 12 * l + u - 1)
                    else:
                        pe.wait_ge(sem["dtr_evac"], 3 * (l + 1))
                    for mp in range(2):
                        b = 2 + 2 * (u % 2) + mp
                        lo, c = 32 * ((2 * h + mp) % 4), (2 * h + mp) // 4
                        q = NAT[lo:lo + 32, c, t * 128:(t + 1) * 128]
                        if t == 0:
                            mm = pe.matmul(PS[:, b, 0:128], q, NAT[lo:lo + 32, 2 + c, 0:128], start=True, stop=True, tile_position=(lo, 0))
                        else:
                            pe.matmul(PS[:, b, 0:256], q, NAT[lo:lo + 32, 2 + c, 128:384], start=True, stop=True, tile_position=(lo, 0))
                            mm = pe.matmul(PS[:, b, 256:384], q, KCT[lo:lo + 32, 2 + c, :], start=True, stop=True, tile_position=(lo, 0))
                    mm.then_inc(sem["ds_out"], 1)

                def df_turn(u):
                    pe.wait_ge(sem["d_ready"], 12 * l + u + 1)
                    if u:
                        pe.wait_ge(sem["dpt_evac"], 12 * l + u)
                    else:
                        pe.wait_ge(sem["o_evac"], 10 * (l + 1))
                    for c in range(1 if dunits[u][0] == 0 else 3):
                        mm = pe.transpose(PS[:, 6, c * 128:(c + 1) * 128], ED[:, 2 * (u % 2), c * 128:(c + 1) * 128], ident)
                    mm.then_inc(sem["dpt_out"], 1)

                def df_out(u):
                    pe.wait_ge(sem["dpt_evac"], 12 * l + u + 1)
                    if u:
                        pe.wait_ge(sem["do_evac"], 12 * l + u)
                    t, h = dunits[u]
                    vs = [DV[:, 0, h * 64:h * 64 + 64]] if t == 0 else [DV[:, 1, h * 64:h * 64 + 64], DV[:, 2, h * 64:h * 64 + 64], VC[:, 1, h * 64:h * 64 + 64]]
                    for c, v in enumerate(vs):
                        mm = pe.matmul(PS[:, 7, 0:64], PTS[:, u % 2, c * 128:(c + 1) * 128], v, start=(c == 0), stop=(c == len(vs) - 1))
                    mm.then_inc(sem["do_out"], 1)

                for i in range(14):
                    if i < 12:
                        df_scores(i)
                    if i in FILL_DF:
                        fill()
                    if 1 <= i <= 12:
                        df_turn(i - 1)
                    if i >= 2:
                        df_out(i - 2)

                def scan_scores(kT, qT):
                    pe.matmul(PS[:, 2, 0:128], kT(0), qT(0, 1), start=True, stop=True)
                    pe.matmul(PS[:, 2, 128:384], kT(1), qT(1, 3), start=True, stop=True)
                    pe.matmul(PS[:, 3, 0:256], kT(2), qT(1, 3), start=True, stop=True).then_inc(sem["sT_out"], 1)

                def decay_row(kind, c):
                    h, d = c // 2, c % 2
                    if c >= 4:
                        pe.wait_ge(sem["e_ready"], 16 * l + 8 * kind + c - 3)
                    r = 32 * kind + 64 * d + h
                    pe.matmul(PS[:, 4 + c % 4, 0:T], ident[:, r:r + 1].broadcast_to([128, 128]), ROWS[:, 0, :], start=True, stop=True)\
                        .then_inc(sem["row_out"], 1)

                pe.wait_ge(sem["d_exp"], 12 * (l + 1))
                pe.wait_ge(sem["do_evac"], 12 * (l + 1))
                for c in range(8):
                    decay_row(0, c)
                    if c % 2 == 0:
                        h = c // 2
                        lo, ch = 64 * (h % 2), h // 2
                        if c:
                            pe.wait_ge(sem["pm_ready"], 16 * l + c)
                        scan_scores(lambda s_: QKT[lo:lo + 64, 2 + ch, s_ * 128:(s_ + 1) * 128],
                                    lambda a, b: QKT[lo:lo + 64, ch, a * 128:b * 128])

                def over_keys(dst, pairs, v):
                    for i, (d, ks, off) in enumerate(pairs):
                        mm = pe.matmul(dst, PM[:, 2 * h + d, off:off + 128], v(d, ks), start=(i == 0), stop=(i == len(pairs) - 1))
                    return mm

                pe.wait_ge(sem["pm_ready"], 16 * l + 8)
                for i, (t, d, b, bq) in enumerate(((0, 0, 2, None), (0, 1, 3, None), (1, 0, 4, 5), (1, 1, 6, 7), (2, 0, 2, 3), (2, 1, 4, 5))):
                    if i >= 4:
                        pe.wait_ge(sem["num_evac"], 9 * l + i - 2)
                    for h in range(4):
                        mm = over_keys(PS[:, b, 65 * h:65 * h + 65], [(d, ks, off) for ks, off in SEEN[d][t]], lambda _, ks: V1[:, ks, h, :])
                    if bq is not None:
                        for ch in range(2):
                            mm = pe.matmul(PS[:, bq, 130 * ch:130 * ch + 130], QKT[:, ch, t * 128:(t + 1) * 128], C0[:, ch, d, :], start=True, stop=True)
                    mm.then_inc(sem["num_out"], 1)
                pe.wait_ge(sem["num_evac"], 9 * l + 4)
                for c in range(2):
                    mm = pe.transpose(PS[:, 6, c * 128:(c + 1) * 128], QKT[:, 2 + c, 0:128], ident)
                mm.then_inc(sem["kt_out"], 1)
                pe.wait_ge(sem["kw_ready"], 2 * l + 1)
                pe.wait_ge(sem["num_evac"], 9 * l + 5)
                for d in range(2):
                    for h in range(4):
                        mm = pe.matmul(PS[0:64, 7 if d == 0 else 2, 65 * h:65 * h + 65], KW[:, d, h, :], V1[:, 0, h, :], start=True, stop=True)
                mm.then_inc(sem["st_out"], 1)

                pe.wait_ge(sem["st_evac"], 3 * l + 2)
                pe.wait_ge(sem["num_evac"], 9 * l + 6)
                for c in range(8):
                    decay_row(1, c)
                    if c % 4 == 0:
                        lo = 64 * (c // 4)
                        if c:
                            pe.wait_ge(sem["pm_ready"], 16 * l + 8 + c)
                        scan_scores(lambda s_: XS[lo:lo + 64, 2, s_ * 128:(s_ + 1) * 128],
                                    lambda a, b: XS[lo:lo + 64, 3, a * 128:b * 128])
                pe.wait_ge(sem["pm_ready"], 16 * l + 16)
                for t, b, bq in ((0, 2, None), (1, 3, (4, 5)), (2, 6, (7, 2))):
                    for h in range(4):
                        mm = over_keys(PS[:, b, 64 * h:64 * h + 64], [(d, ks, off) for d in range(2) for ks, off in SEEN[d][t]],
                                       lambda d, ks: XDT[:, d, ks, h, :])
                    if bq is not None:
                        for g in range(2):
                            if t == 2 and g == 1:
                                pe.wait_ge(sem["num_evac"], 9 * l + 7)
                            mm = pe.matmul(PS[:, bq[g], 0:256], XS[64 * g:64 * g + 64, 3, t * 128:(t + 1) * 128], H0[64 * g:64 * g + 64, :], start=True, stop=True)
                    mm.then_inc(sem["num_out"], 1)
                pe.wait_ge(sem["kw_ready"], 2 * l + 2)
                pe.wait_ge(sem["num_evac"], 9 * l + 8)
                for d in range(2):
                    for h in range(4):
                        c = 4 * d + h
                        mm = pe.matmul(PS[0:64, 3, 64 * c:64 * c + 64], KW[:, d, h, :], BTM[:, 64 * (h // 2):64 * (h // 2) + 64], start=True, stop=True)
                mm.then_inc(sem["st_out"], 1)

                while fills[0] < 8:
                    fill()

                pe.wait_ge(sem["br_ready"], l + 1)
                pe.wait_ge(sem["st_evac"], 3 * (l + 1))
                pe.wait_ge(sem["num_evac"], 9 * (l + 1))
                for g in range(6):
                    t, half = g // 2, g % 2
                    srcs = (MO, NAQK) if half == 0 else (DQK, SZ)
                    for c in range(4):
                        mm = pe.transpose(PS[:, 2 + g, c * 128:(c + 1) * 128], srcs[c // 2][:, t, (c % 2) * 128:(c % 2) * 128 + 128], ident)
                    mm.then_inc(sem["brt_out"], 1)
                pe.wait_ge(sem["brt_evac"], 6 * (l + 1))
                for nb in range(4):
                    w = tile(n0 + (21 if nb == 0 else 19 + 3 * nb), 1024)
                    for dc in range(8):
                        if nb:
                            fill()
                        j = 8 * nb + dc
                        if j >= 4:
                            pe.wait_ge(sem["bp_evac"], 32 * l + j - 3)
                        for k in range(2):
                            mm = pe.matmul(PS[:, 2 + j % 4, 0:T], w[:, k, dc * 128:(dc + 1) * 128], BRT[:, 2 * nb + k, :], start=(k == 0), stop=(k == 1))
                        mm.then_inc(sem["bp_out"], 1)
                pe.wait_ge(sem["mix_ready"], l + 1)
                for dc in range(8):
                    w = tile(n0 + 31 + dc // 4)
                    if dc >= 4:
                        pe.wait_ge(sem["x1_ready"], 8 * l + dc - 3)
                    for k in range(KC):
                        mm = pe.matmul(PS[:, 2 + dc % 4, 0:T], w[:, k, (dc % 4) * 128:(dc % 4) * 128 + 128], MIX[:, k, :], start=(k == 0), stop=(k == KC - 1))
                    mm.then_inc(sem["wo_out"], 1)

                sum_squares(1, 6)
                pe.wait_ge(sem["h_ready"], 2 * l + 2)
                for t in range(TT):
                    for k in range(KC):
                        mm = pe.matmul(PS[:, 7, 16 * t:16 * t + 16], hT[:, k, t * 128:(t + 1) * 128], wrt[:, k, :], start=(k == 0), stop=(k == KC - 1))
                mm.then_inc(sem["rt_out"], 1)
                pe.wait_ge(sem["x1_ready"], 8 * (l + 1))
                for g in range(6):
                    t, half = g // 2, g % 2
                    for c in range(4):
                        mm = pe.transpose(PS[:, g, c * 128:(c + 1) * 128], hT[:, 4 * half + c, t * 128:(t + 1) * 128], ident)
                    mm.then_inc(sem["h2t_out"], 1)
                pe.wait_ge(sem["aff_ready"], l + 1)
                for t in range(TT):
                    mm = pe.transpose(PS[0:NE, 6, t * 128:(t + 1) * 128], AFF[:, t, :], ident)
                mm.then_inc(sem["afT"], 1)
                pe.wait_ge(sem["pos_ready"], l + 1)
                for t in range(TT):
                    mm = pe.transpose(PS[:, 7, 16 * t:16 * t + 16], WK[0:NE, t * 128:(t + 1) * 128], ident[0:NE, 0:NE])
                mm.then_inc(sem["posT"], 1)

                pe.wait_ge(sem["sel_ready"], l + 1)
                pe.wait_ge(sem["h2t_evac"], 6 * (l + 1))
                for q in range(16):
                    dc, grp = q // 2, q % 2
                    if q >= 4:
                        pe.wait_ge(sem["xg_evac"], 16 * l + q - 3)
                    ts = (1, 2) if grp == 0 else (0,)
                    for i, t in enumerate(ts):
                        mm = pe.matmul(PS[:, q % 4, :], H2M[:, t, dc * 128:(dc + 1) * 128], SEL[:, t, :, :].rearrange("p a b -> p (a b)"),
                                       start=(i == 0), stop=(i == len(ts) - 1))
                    mm.then_inc(sem["xg_out"], 1)
                for i in range(3):
                    for j in range(4):
                        if i < 2:
                            eb, t = 2 * i + j // 2, 1 + j % 2
                        else:
                            eb, t = j, 0
                        mm = pe.transpose(PS[:, 4 + i, j * 128:(j + 1) * 128], SELG[:, t, 4 * eb:4 * eb + 4, :].rearrange("p a b -> p (a b)"), ident)
                    mm.then_inc(sem["sgt_out"], 1)
                pe.wait_ge(sem["xg_evac"], 16 * (l + 1))
                pe.wait_ge(sem["sgt_evac"], 3 * (l + 1))

                base = n0 + 33

                def pair_tiles(i):
                    return tile(base + i), tile(base + i + 1)

                def project(dst, w2, x):
                    for k in range(KC):
                        for hf in range(2):
                            mm = pe.matmul(dst[64 * hf:64 * hf + 64, :], x(k), w2[hf][:, k, :], start=(k == 0), stop=(k == KC - 1),
                                           tile_position=(0, 64 * hf))
                    return mm

                def expert_a(e):
                    g = l * NE + e
                    if e >= 2:
                        pe.wait_ge(sem["hh_ready"], g - 1)
                    project(PS[:, 2 * (e % 2), :], pair_tiles(0 if e == 0 else 6 * e - 2),
                            lambda k: XG[:, k, e, :, :].rearrange("p a b -> p (a b)")).then_inc(sem["a_out"], 1)

                def expert_u(e):
                    project(PS[:, 2 * (e % 2) + 1, :], pair_tiles(2 if e == 0 else 6 * e + 2),
                            lambda k: XG[:, k, e, :, :].rearrange("p a b -> p (a b)")).then_inc(sem["u_out"], 1)

                def expert_down(e):
                    g = l * NE + e
                    pe.wait_ge(sem["hh_ready"], g + 1)
                    if e:
                        pe.wait_ge(sem["ht_evac"], g)
                    for c in range(4):
                        mm = pe.transpose(PS[:, 4, c * 128:(c + 1) * 128], HH[:, e % 2, c * 128:(c + 1) * 128], ident)
                    mm.then_inc(sem["ht_out"], 1)
                    pe.wait_ge(sem["ht_evac"], g + 1)
                    if e >= 2:
                        pe.wait_ge(sem["yd_evac"], g - 1)
                    project(PS[:, 5 + e % 2, :], pair_tiles(6 * e + 6 if e < NE - 1 else 6 * e + 4),
                            lambda k: HTT[:, e % 2, k % 4, 64 * (k // 4):64 * (k // 4) + 64]).then_inc(sem["yd_out"], 1)

                expert_a(0)
                expert_u(0)
                for e in range(1, NE):
                    expert_a(e)
                    expert_down(e - 1)
                    expert_u(e)
                expert_down(NE - 1)

                pe.wait_ge(sem["yd_evac"], NE * (l + 1))
                for dc in range(8):
                    if dc >= 4:
                        pe.wait_ge(sem["cb_evac"], 8 * l + dc - 3)
                    for eb in range(4):
                        pe.matmul(PS[:, dc % 4, 0:128], YP[:, eb, dc * 128:(dc + 1) * 128], SGP[:, eb, :], start=(eb == 0), stop=(eb == 3))
                    for eb in range(4):
                        mm = pe.matmul(PS[:, dc % 4, 128:384], YS[:, eb, dc * 128:(dc + 1) * 128], SGT[:, eb, :], start=(eb == 0), stop=(eb == 3))
                    mm.then_inc(sem["cb_out"], 1)
            pe.wait_ge(sem["x_ready"], L)
            for g in range(6):
                t, h = g // 2, g % 2
                for c in range(4):
                    mm = pe.transpose(PS[:, g, c * 128:(c + 1) * 128], xT[:, 4 * h + c, t * 128:(t + 1) * 128], ident)
                mm.then_inc(sem["yt_out"], 1)

        @block.scalar
        def _(act):
            def copy(dst, src, scale=1.0):
                return act.activation(dst, src, ACT.Copy, scale=scale)

            act.dma_start(cst[:, :], dr["consts"]).then_inc(par_in[0], 16)
            act.dma_start(XIN[:, 0, :], dr["x_prompt"][0]).then_inc(par_in[0], 16)
            act.dma_start(XIN[:, 1:3, :], dr["x_sample"][0].rearrange("(t p) d -> p t d", p=128)).then_inc(par_in[0], 16)
            act.dma_start(small[:, 0:16], dr["cvec"]).then_inc(par_in[2], 16)
            act.wait_ge(par_in[2], 16)
            act.activation(small[:, 16:32], small[:, 0:16], ACT.Tanh, scale=0.5).then_inc(sem["tanh_out"], 1)
            for g in range(6):
                t, h = g // 2, g % 2
                act.wait_ge(sem["xT_out"], g + 1)
                ins = copy(xT[:, 4 * h:4 * h + 4, t * 128:(t + 1) * 128], PS[:, g, :].rearrange("p (a b) -> p a b", a=4))
                ins.then_inc(sem["xT_evac"], 1)
            act.wait_ge(sem["xT_evac"], 6)
            for l in range(L):
                nt0 = 1 + 3 * l

                def squares(which):
                    if l and which == 0:
                        act.wait_ge(sem["x_ready"], l)
                    if which:
                        act.wait_ge(sem["x1_ready"], 8 * (l + 1))
                    act.activation(hT[:, :, :], xT[:, :, :], ACT.Square).then_inc(sem["sq_ready"], 1)

                def root(which, bank):
                    act.wait_ge(sem["ss_ready"], 2 * l + which + 1)
                    act.activation(RSTD, PS[:, bank, 0:T], ACT.Sqrt, scale=1.0 / D, bias=K("eps")).then_inc(sem["rms_ready"], 1)

                squares(0)
                act.wait_ge(sem["mod_done"], l + 1)
                root(0, 3)

                j = [0]

                def proj(dsts):
                    j[0] += 1
                    act.wait_ge(sem["proj_out"], l * N_PROJ + j[0])
                    b = (j[0] - 1) % 4
                    for i, (dst, lo, hi, scale) in enumerate(dsts):
                        src = PS[:, b, lo:hi]
                        if len(dst.shape) == 3:
                            src = src.rearrange("p (a b) -> p a b", a=dst.shape[1])
                        ins = copy(dst, src, scale)
                    ins.then_inc(sem["proj_evac"], 1)

                for c in range(4):
                    proj([(QKT[:, c, :], 0, T, 1.0 if c < 2 else 0.125)])
                for t in range(TT):
                    proj([(NAQK[:, t, :], 0, 512, 1.0)])
                act.wait_ge(sem["gact_in"], l + 1)
                act.activation(GL, GA, ACT.Exp, scale=-1.0).then_inc(sem["gact_e"], 1)
                act.wait_ge(sem["gact_e"], l + 1)
                act.activation(GL, GL, ACT.Ln, bias=1.0)
                act.activation(AEXP, RP("a_log"), ACT.Exp).then_inc(sem["gact_out"], 1)
                for c in range(4):
                    proj([(XB[:, c, 2:130], 0, 128, 1.0), (XB[:, c, 134:390], 128, T, 1.0)])
                for t in range(TT):
                    proj([(V1[:, t, :, 0:64], 0, 256, 1.0), (MO[:, t, :], 256, 512, 1.0)])
                for t in range(TT):
                    proj([(NV[:, t, :], 0, 256, 1.0), (DQK[:, t, 0:256], 256, 512, 1.0)])
                act.wait_ge(sem["tmT"], l + 1)
                for i in range(3):
                    ins = copy(TM[:, i, :], PS[:, 4 + i, 0:T])
                ins.then_inc(sem["tm_evac"], 1)
                for t in range(TT):
                    proj([(DQK[:, t, 256:512], 0, 256, 1.0), (DV[:, t, :], 256, 512, 1.0)])
                for t in range(TT):
                    proj([(SZ[:, t, :], 0, 256, 1.0)])
                act.wait_ge(sem["tm_ready"], l + 1)
                act.activation(WPT, WPT, ACT.Exp)
                act.activation(EMT, EMT, ACT.Exp)
                act.activation(LAM[:, 0:2], LAM[:, 0:2], ACT.Exp).then_inc(sem["tm_exp"], 1)
                act.wait_ge(sem["conv_ready"], l + 1)
                for c in range(4):
                    ins = act.activation(XS[:, c, 0:128], CV[:, c, 2:130], ACT.Tanh, scale=0.5)
                    ins = act.activation(XS[:, c, 128:384], CV[:, c, 134:390], ACT.Tanh, scale=0.5)
                ins.then_inc(sem["silu_t"], 1)
                act.wait_ge(sem["xtr_out"], l + 1)
                copy(XTM[:, 0:2, :], PS[:, 4, :].rearrange("p (a b) -> p a b", a=2))
                copy(XTM[:, 2, :], PS[:, 5, 0:256])
                copy(BTM, PS[:, 5, 256:384]).then_inc(sem["xtr_evac"], 1)
                for i, b in enumerate((6, 7, 4)):
                    act.wait_ge(sem["ntr_out"], 4 * l + i + 1)
                    copy(NAT[:, :, i * 128:(i + 1) * 128], PS[:, b, :].rearrange("p (a b) -> p a b", a=4)).then_inc(sem["ntr_evac"], 1)
                act.wait_ge(sem["ntr_out"], 4 * l + 4)
                copy(KCT, PS[:, 5, :].rearrange("p (a b) -> p a b", a=4)).then_inc(sem["ntr_evac"], 1)

                nf = [0]

                def fill(dst):
                    i = nf[0]
                    nf[0] += 1
                    act.wait_ge(sem["fill_out"], 32 * l + i + 1)
                    act.activation(dst, PS[:, i % 2, 0:T], ACT.Tanh, scale=0.5).then_inc(sem["fill_evac"], 1)

                def na_exp(u):
                    act.wait_ge(sem["s_read"], 10 * l + u + 1)
                    if u < 2:
                        for c in range(2):
                            ins = act.activation(ED[:, u, c * 128:(c + 1) * 128], ED[:, 2 + u, c * 128:(c + 1) * 128], ACT.Exp,
                                                 bias=SMX[:, u, c:c + 1], accum_out=SSUM[:, u, c:c + 1])
                    else:
                        ins = act.activation(ED[:, u % 2, :], ED[:, 2 + u % 2, :], ACT.Exp, bias=SMX[:, u % 2, 0:1], accum_out=SSUM[:, u % 2, 0:1])
                    ins.then_inc(sem["p_exp"], 1)

                def na_turned(u):
                    act.wait_ge(sem["pt_out"], 10 * l + u + 1)
                    w = 256 if u < 2 else 384
                    copy(PTS[:, u % 2, 0:w], PS[:, 4 + u % 2, 0:w]).then_inc(sem["pt_evac"], 1)

                for i in range(11):
                    if i < 10:
                        if i >= 2:
                            act.wait_ge(sem["o_evac"], 10 * l + i - 1)
                        na_exp(i)
                    if i in FILL_NA:
                        fill(GATES[:, nf[0], :])
                    if i >= 1:
                        na_turned(i - 1)
                for t in range(TT):
                    act.wait_ge(sem["dtr_out"], 3 * l + t + 1)
                    copy(NAT[:, :, t * 128:(t + 1) * 128], PS[:, 2 + t, :].rearrange("p (a b) -> p a b", a=4)).then_inc(sem["dtr_evac"], 1)

                def df_exp(u):
                    act.wait_ge(sem["d_max"], 12 * l + u + 1)
                    w = 128 if u < 4 else 384
                    for mp in range(2):
                        ins = act.activation(ED[:, 2 * (u % 2) + mp, 0:w], PS[:, 2 + 2 * (u % 2) + mp, 0:w], ACT.Exp,
                                             scale=32 ** -0.5, bias=DMX[:, u % 2, mp:mp + 1], accum_out=DSUM[:, u % 2, mp:mp + 1])
                    ins.then_inc(sem["d_exp"], 1)

                def df_turned(u):
                    act.wait_ge(sem["dpt_out"], 12 * l + u + 1)
                    w = 128 if u < 4 else 384
                    copy(PTS[:, u % 2, 0:w], PS[:, 6, 0:w]).then_inc(sem["dpt_evac"], 1)

                for i in range(13):
                    if i < 12:
                        df_exp(i)
                    if i in FILL_DF:
                        fill(GATES[:, nf[0], :])
                    if i >= 1:
                        df_turned(i - 1)

                def combos(kind):
                    for c in range(8):
                        act.wait_ge(sem["e_ready"], 16 * l + 8 * kind + c + 1)
                        i = c % 2
                        act.activation(EDf[:, 512 * i:512 * i + 512], EDf[:, 512 * i:512 * i + 512], ACT.Exp).then_inc(sem["e_exp"], 1)

                combos(0)
                act.activation(W1[:, 0:768].rearrange("p (a b) -> p a b", a=TT), MO[:, :, :], ACT.Tanh, scale=0.5)
                act.activation(W1[:, 768:1536].rearrange("p (a b) -> p a b", a=TT), SZ[:, :, :], ACT.Tanh, scale=0.5).then_inc(sem["tanh_out"], 1)
                act.wait_ge(sem["st_out"], 2 * l + 1)
                for d in range(2):
                    copy(CN_OUT[0:64, d, :, :], PS[0:64, 7 if d == 0 else 2, 0:260].rearrange("p (a b) -> p a b", a=4)).then_inc(sem["st_evac"], 1)
                combos(1)
                act.wait_ge(sem["st_out"], 2 * l + 2)
                copy(SS_OUT[0:64, :, :], PS[0:64, 3, :].rearrange("p (a b) -> p a b", a=8)).then_inc(sem["st_evac"], 1)
                while nf[0] < 8:
                    fill(GATES[:, nf[0], :])
                for g in range(6):
                    t, half = g // 2, g % 2
                    act.wait_ge(sem["brt_out"], 6 * l + g + 1)
                    copy(BRT[:, 4 * half:4 * half + 4, t * 128:(t + 1) * 128], PS[:, 2 + g, :].rearrange("p (a b) -> p a b", a=4)).then_inc(sem["brt_evac"], 1)
                act.wait_ge(sem["tanh_in"], l + 1)
                for i in range(24):
                    if i >= 2:
                        act.wait_ge(sem["bp_evac"], 32 * l + 8 + i - 1)
                    fill(GT[:, i % 2, :])
                squares(1)
                root(1, 6)

                for t in range(TT):
                    act.wait_ge(sem["rt_max"], l + 1)
                    ins = act.activation(AFF[:, t, :], PS[:, 7, 16 * t:16 * t + 16], ACT.Exp, bias=RMX[:, t:t + 1], accum_out=RSUM[:, t:t + 1])
                ins.then_inc(sem["rt_exp"], 1)
                for g in range(6):
                    t, half = g // 2, g % 2
                    act.wait_ge(sem["h2t_out"], 6 * l + g + 1)
                    copy(H2M[:, t, 512 * half:512 * half + 512], PS[:, g, :]).then_inc(sem["h2t_evac"], 1)
                for q in range(0, 16):
                    dc, grp = q // 2, q % 2
                    act.wait_ge(sem["xg_out"], 16 * l + q + 1)
                    copy(XG[:, dc, :, grp, :], PS[:, q % 4, :].rearrange("p (a b) -> p a b", a=NE)).then_inc(sem["xg_evac"], 1)
                for i in range(3):
                    act.wait_ge(sem["sgt_out"], 3 * l + i + 1)
                    if i < 2:
                        ins = copy(SGT[:, 2 * i:2 * i + 2, :], PS[:, 4 + i, :].rearrange("p (a b) -> p a b", a=2))
                    else:
                        ins = copy(SGP, PS[:, 6, :].rearrange("p (a b) -> p a b", a=4))
                    ins.then_inc(sem["sgt_evac"], 1)

                def tanh_a(e):
                    g = l * NE + e
                    act.wait_ge(sem["a_out"], g + 1)
                    if e:
                        act.wait_ge(sem["hh_ready"], g)
                    act.activation(TH, PS[:, 2 * (e % 2), :], ACT.Tanh, scale=0.5).then_inc(sem["a_tanh"], 1)

                def down_side(e):
                    g = l * NE + e
                    act.wait_ge(sem["ht_out"], g + 1)
                    if e >= 2:
                        act.wait_ge(sem["yd_out"], g - 1)
                    copy(HTT[:, e % 2, :, :], PS[:, 4, :].rearrange("p (a b) -> p a b", a=4)).then_inc(sem["ht_evac"], 1)

                def take_y(e):
                    g = l * NE + e
                    act.wait_ge(sem["yd_out"], g + 1)
                    b, eb, o = 5 + e % 2, e // 4, 32 * (e % 4)
                    copy(YS[o:o + 32, eb, 0:512], PS[0:32, b, :])
                    copy(YP[o:o + 32, eb, 0:512], PS[32:64, b, :])
                    copy(YS[o:o + 32, eb, 512:1024], PS[64:96, b, :])
                    copy(YP[o:o + 32, eb, 512:1024], PS[96:128, b, :]).then_inc(sem["yd_evac"], 1)

                tanh_a(0)
                for e in range(1, NE):
                    tanh_a(e)
                    down_side(e - 1)
                    take_y(e - 1)
                down_side(NE - 1)
                take_y(NE - 1)
            for g in range(6):
                t, h = g // 2, g % 2
                act.wait_ge(sem["yt_out"], g + 1)
                copy(YOUT[:, t, 512 * h:512 * h + 512], PS[:, g, :]).then_inc(sem["yt_evac"], 1)

        @block.vector
        def _(dve):
            steps = [0]

            def step():
                steps[0] += 1
                return steps[0]

            TTo, TS, STT = dve.tensor_tensor, dve.tensor_scalar, dve.scalar_tensor_tensor

            dve.memset(c32[:, :, :], 0.0).then_inc(sem["pool_init"], 1)
            dve.wait_ge(sem["pool_init"], 1)
            dve.wait_ge(sem["tanh_out"], 1)
            dve.wait_ge(par_in[2], 16)
            TS(small[:, 32:48], small[:, 0:16], 0.5, None, ALU.mult).then_inc(dve_step, 1)
            dve.wait_ge(dve_step, step())
            STT(c32[:, :, 0:2], small[:, 16:32].rearrange("p (a b) -> p a b", a=8), 1.0, small[:, 32:48].rearrange("p (a b) -> p a b", a=8),
                ALU.add, ALU.mult).then_inc(sem["c_ready"], 1)
            dve.wait_ge(sem["c_ready"], 1)
            dve.wait_ge(sem["xT_evac"], 6)
            for l in range(L):
                lam_init = 0.8 - 0.6 * math.exp(-0.3 * l)
                if l:
                    dve.wait_ge(sem["x_ready"], l)
                for i in range(12):
                    dve.wait_ge(sem["ada_part"], 12 * l + i + 1)
                    if i >= 2:
                        dve.wait_ge(sem["ada_sel"], 12 * l + i - 1)
                    dve.tensor_copy(MP[:, i % 2, :], PS[:, i % 2, :]).then_inc(sem["ada_evac"], 1)
                dve.wait_ge(par_in[1], 80 * (l + 1))
                dve.wait_ge(sem["ada_sel"], 12 * (l + 1))
                TTo(mod[:, :, :], PS[:, 2, 0:96].rearrange("p (a b) -> p a b", a=48), over(CP("b_ada"), 2, 2), ALU.add).then_inc(dve_step, 1)
                dve.wait_ge(dve_step, step())
                for i, name in enumerate(("norm1", "norm2")):
                    STT(amp[:, i, :, :], mod[:, 24 * i + 8:24 * i + 16, :], 1.0, over(CP(name), 2, 2), ALU.add, ALU.mult)
                TS(mod[:, 16:24, :], mod[:, 16:24, :], 0.5, None, ALU.mult)
                TS(mod[:, 40:48, :], mod[:, 40:48, :], 0.5, None, ALU.mult).then_inc(sem["mod_done"], 1)
                dve.wait_ge(sem["mod_done"], l + 1)

                def modulated(which):
                    dve.wait_ge(sem["rms_ready"], 2 * l + which + 1)
                    dve.reciprocal(RSTD, RSTD).then_inc(dve_step, 1)
                    dve.wait_ge(dve_step, step())
                    TTo(hT[:, :, :], xT[:, :, :], over(RSTD, 1, KC), ALU.mult).then_inc(dve_step, 1)
                    dve.wait_ge(dve_step, step())
                    for c in range(KC):
                        for g, (a, b) in enumerate(((0, 128), (128, 384))):
                            ins = TS(hT[:, c, a:b], hT[:, c, a:b], amp[:, which, c, g:g + 1], mod[:, 24 * which + c, g:g + 1], ALU.mult, ALU.add)
                    ins.then_inc(sem["h_ready"], 1)
                    dve.wait_ge(sem["h_ready"], 2 * l + which + 1)

                modulated(0)
                dve.memset(TM[:, 0:2, :], 0.0)
                dve.memset(V1[:, :, :, 64:65], 1.0)
                for a in (0, 130, 132, 390):
                    ins = dve.memset(XB[:, :, a:a + 2], 0.0)
                ins.then_inc(dve_step, 1)
                dve.wait_ge(dve_step, step())

                dve.wait_ge(sem["gpre_out"], l + 1)
                g3 = PS[:, 7, 0:72].rearrange("p (a b) -> p a b", a=TT)
                TTo(G1, g3, over(rowp[:, 0:24], 1, TT), ALU.add).then_inc(dve_step, 1)
                dve.wait_ge(dve_step, step())
                STT(GA, G1, -1.0, G1, ALU.mult, ALU.max).then_inc(sem["gact_in"], 1)
                lam = RP("lambda").rearrange("p (a b c) -> p a b c", a=2, b=2)
                TTo(SS[:, 0:64].rearrange("p (a b) -> p a b", a=2), lam[:, :, 0, :], lam[:, :, 1, :], ALU.mult).then_inc(dve_step, 1)
                dve.wait_ge(dve_step, step())
                dve.tensor_reduce(LAM[:, 0:2], SS[:, 0:64].rearrange("p (a b) -> p a b", a=2), AX.X, ALU.add).then_inc(dve_step, 1)
                dve.wait_ge(dve_step, step())
                dve.wait_ge(sem["gact_out"], l + 1)
                gf = TM[:, 0, :].rearrange("p (t d k h) -> p t d k h", t=TT, d=2, k=2)
                gi = TM[:, 1, :].rearrange("p (t d k h) -> p t d k h", t=TT, d=2, k=2)
                STT(DTM, G1[:, :, 16:24], 0.0, GL[:, :, 16:24], ALU.max, ALU.add).then_inc(dve_step, 1)
                dve.wait_ge(dve_step, step())
                for d in range(2):
                    STT(gf[:, :, d, 0, 0:4], G1[:, :, 8 * d + 4:8 * d + 8], 0.0, GL[:, :, 8 * d + 4:8 * d + 8], ALU.min, ALU.subtract)
                    dve.tensor_copy(gi[:, :, d, 0, 0:4], G1[:, :, 8 * d:8 * d + 4])
                    ins = STT(gf[:, :, d, 1, 0:4], DTM[:, :, 4 * d:4 * d + 4], -1.0, over(AEXP[:, 4 * d:4 * d + 4], 1, TT), ALU.mult, ALU.mult)
                ins.then_inc(sem["gtm_ready"], 1)
                dve.wait_ge(sem["gtm_ready"], l + 1)
                dve.wait_ge(sem["proj_evac"], l * N_PROJ + 11)
                for c in range(4):
                    for jj in range(5):
                        wv = CP("conv_w")[:, 5 * c + jj:5 * c + jj + 1]
                        src = XB[:, c, jj:jj + 388]
                        if jj == 0:
                            ins = TS(CV[:, c, 2:390], src, wv, CP("conv_b")[:, c:c + 1], ALU.mult, ALU.add)
                        else:
                            ins = STT(CV[:, c, 2:390], src, wv, CV[:, c, 2:390], ALU.mult, ALU.add)
                        if jj < 4:
                            ins.then_inc(dve_step, 1)
                            dve.wait_ge(dve_step, step())
                ins.then_inc(sem["conv_ready"], 1)
                dve.wait_ge(sem["conv_ready"], l + 1)

                dve.wait_ge(sem["growT"], l + 1)
                segs = ((0, 128), (128, 384))
                for lo, rev in ((0, False), (64, True)):
                    for a, b in segs:
                        def run(v):
                            v = v[lo:lo + 64, a:b]
                            return v[:, ::-1] if rev else v
                        ins = dve.tensor_tensor_scan(run(ROWS[:, 2, :]), run(PS[:, 4, 0:T]), zeros[lo:lo + 64, :].broadcast_to([64, b - a]), 0.0, ALU.add, ALU.add)
                TS(NM0, CP("m0"), -1.0, None, ALU.mult)
                ins.then_inc(dve_step, 1)
                dve.wait_ge(dve_step, step())
                TTo(ROWS[:, 1, :], ROWS[:, 2, :], PS[:, 5, 0:T], ALU.subtract)
                dve.tensor_copy(ROWS[:, 0, :], ROWS[:, 2, :]).then_inc(dve_step, 1)
                dve.wait_ge(dve_step, step())
                for lo, rev in ((0, False), (64, True)):
                    for i, (a, b) in enumerate(segs):
                        def run(v):
                            v = v[lo:lo + 4, a:b]
                            return v[:, ::-1] if rev else v
                        ins = dve.tensor_tensor_scan(run(ROWS[:, 0, :]), run(ROWS[:, 1, :]), run(ROWS[:, 1, :]),
                                                     NM0[lo:lo + 4, :] if i else 0.0, ALU.min, ALU.min)
                ins.then_inc(sem["rows_ready"], 1)
                dve.wait_ge(sem["rows_ready"], l + 1)
                TTo(MOUT[0:4, 0:1], ROWS[0:4, 2, 127:128], ROWS[0:4, 0, 127:128], ALU.subtract)
                TTo(MOUT[64:68, 1:2], ROWS[64:68, 2, 0:1], ROWS[64:68, 0, 0:1], ALU.subtract).then_inc(sem["m_out"], 1)
                dve.wait_ge(sem["tm_evac"], l + 1)
                tmr, tmn, tmb = (TM[:, i, :].rearrange("p (t d k h) -> p t d k h", t=TT, d=2, k=2) for i in range(3))
                m0 = RP("m0").rearrange("p (d k h) -> p d k h", d=2, k=2)
                for k in range(2):
                    for d in range(2):
                        TTo(WPT[:, :, 8 * k + 4 * d:8 * k + 4 * d + 4], tmr[:, :, d, k, 0:4], over(m0[:, d, k, 0:4], 1, TT), ALU.add)
                for d in range(2):
                    ins = TTo(EMT[:, :, 4 * d:4 * d + 4], tmr[:, :, d, 0, 0:4], tmb[:, :, d, 0, 0:4], ALU.subtract)
                ins.then_inc(sem["tm_ready"], 1)

                dve.wait_ge(sem["silu_t"], l + 1)
                TS(CV[:, :, 2:390], CV[:, :, 2:390], 0.5, None, ALU.mult).then_inc(dve_step, 1)
                dve.wait_ge(dve_step, step())
                STT(XS[:, :, 0:128], XS[:, :, 0:128], 1.0, CV[:, :, 2:130], ALU.add, ALU.mult)
                STT(XS[:, :, 128:384], XS[:, :, 128:384], 1.0, CV[:, :, 134:390], ALU.add, ALU.mult).then_inc(sem["xs_ready"], 1)

                dve.wait_ge(sem["xs_ready"], l + 1)
                sq = W1.rearrange("p (a b) -> p a b", a=TT)
                dve.wait_ge(sem["proj_evac"], l * N_PROJ + 20)
                TTo(sq, NAQK[:, :, :], NAQK[:, :, :], ALU.mult).then_inc(dve_step, 1)
                dve.wait_ge(dve_step, step())
                dve.tensor_reduce(SS[:, 0:24], W1.rearrange("p (a b) -> p a b", b=64), AX.X, ALU.add).then_inc(dve_step, 1)
                dve.wait_ge(dve_step, step())
                TTo(sq, DQK[:, :, :], DQK[:, :, :], ALU.mult).then_inc(dve_step, 1)
                dve.wait_ge(dve_step, step())
                dve.tensor_reduce(SS[:, 24:72], W1.rearrange("p (a b) -> p a b", b=32), AX.X, ALU.add).then_inc(dve_step, 1)
                dve.wait_ge(dve_step, step())
                TS(SS[:, 0:24], SS[:, 0:24], 1.0 / 64, EPS, ALU.mult, ALU.add)
                TS(SS[:, 24:72], SS[:, 24:72], 1.0 / 32, EPS, ALU.mult, ALU.add).then_inc(sem["pool_in"], 1)
                dve.wait_ge(sem["pool_out"], 4 * l + 1)
                na = NAQK.rearrange("p t (g c) -> p (t g) c", c=64)
                TTo(na, na, over(RS[:, 0:24], 2, 64), ALU.mult).then_inc(dve_step, 1)
                dve.wait_ge(dve_step, step())
                for i, name in enumerate(("na_qn", "na_kn")):
                    ins = [TTo(NAQK[:, t, 256 * i:256 * i + 256].rearrange("p (g c) -> p g c", c=64), NAQK[:, t, 256 * i:256 * i + 256].rearrange("p (g c) -> p g c", c=64),
                               over(RP(name), 1, 4), ALU.mult) for t in range(TT)][-1]
                ins.then_inc(sem["nan_ready"], 1)
                df = DQK.rearrange("p t (g c) -> p (t g) c", c=32)
                TTo(df, df, over(RS[:, 24:72], 2, 32), ALU.mult).then_inc(dve_step, 1)
                dve.wait_ge(dve_step, step())
                for i, name in enumerate(("diff_qn", "diff_kn")):
                    for t in range(TT):
                        v = DQK[:, t, 256 * i:256 * i + 256].rearrange("p (g c) -> p g c", c=32)
                        ins = TTo(v, v, over(RP(name), 1, 8), ALU.mult)
                ins.then_inc(dve_step, 1)
                dve.wait_ge(dve_step, step())
                for t in range(2):
                    x4 = DQK[:, 1 + t, :].rearrange("p (g c) -> p g c", c=32)
                    cos = over(K("cos")[:, 32 * t:32 * t + 32], 1, 16)
                    TTo(W1[:, 512 * t:512 * t + 512].rearrange("p (g c) -> p g c", c=32), x4, cos, ALU.mult).then_inc(dve_step, 1)
                    dve.wait_ge(dve_step, step())
                    sin = K("sin")[:, 32 * t:32 * t + 32].rearrange("p (a b c) -> p a b c", a=2, b=2)
                    x5 = DQK[:, 1 + t, :].rearrange("p (g a b c) -> p g a b c", g=16, a=2, b=2)
                    w5 = W2[:, 512 * t:512 * t + 512].rearrange("p (g a b c) -> p g a b c", g=16, a=2, b=2)
                    for b in range(2):
                        ins = TTo(w5[:, :, :, b, :], x5[:, :, :, 1 - b, :], over(sin[:, :, b, :], 1, 16), ALU.mult)
                    ins.then_inc(dve_step, 1)
                    dve.wait_ge(dve_step, step())
                    ins = TTo(DQK[:, 1 + t, :], W1[:, 512 * t:512 * t + 512], W2[:, 512 * t:512 * t + 512], ALU.add)
                dve.wait_ge(sem["tm_exp"], l + 1)
                TTo(LAM[:, 2:3], LAM[:, 1:2], LAM[:, 0:1], ALU.subtract).then_inc(dve_step, 1)
                dve.wait_ge(dve_step, step())
                TS(LAM[:, 3:4], LAM[:, 2:3], -lam_init, None, ALU.add).then_inc(sem["dfn_ready"], 1)
                dve.wait_ge(sem["dfn_ready"], l + 1)

                dve.wait_ge(sem["bm_loaded"], 256 * (l + 1))
                win = over(K("win"), 1, 16)
                for t in range(2):
                    v = BM[:, t, :, :].rearrange("p h (r c) -> p (h r) c", c=64)
                    w_ = W1[:, 0:1024].rearrange("p (a b) -> p a b", a=16)
                    TTo(w_, v[:, :, ::-1], win, ALU.add).then_inc(dve_step, 1)
                    dve.wait_ge(dve_step, step())
                    dve.tensor_copy(v, w_).then_inc(dve_step, 1)
                    dve.wait_ge(dve_step, step())

                na_s = 64 ** -0.5

                def na_in(u):
                    dve.wait_ge(sem["s_out"], 10 * l + u + 1)
                    if u >= 2:
                        dve.wait_ge(sem["p_exp"], 10 * l + u - 1)
                    i = u % 2
                    if u < 2:
                        TS(ED[:, 2 + i, 0:256], PS[:, 2 + i, 0:256], na_s, None, ALU.mult).then_inc(dve_step, 1)
                        dve.wait_ge(dve_step, step())
                        dve.tensor_reduce(SMX[:, i, :], ED[:, 2 + i, 0:256].rearrange("p (a b) -> p a b", a=2), AX.X, ALU.max, negate=True)\
                            .then_inc(sem["s_read"], 1)
                    else:
                        t, h = (u - 2) // 4, (u - 2) % 4
                        TS(ED[:, 2 + i, 256:384], PS[:, 2 + i, 256:384], na_s, None, ALU.mult)
                        STT(ED[:, 2 + i, 0:256], PS[:, 2 + i, 0:256], na_s, BM[:, t, h, :], ALU.mult, ALU.add).then_inc(dve_step, 1)
                        dve.wait_ge(dve_step, step())
                        dve.tensor_reduce(SMX[:, i, 0:1], ED[:, 2 + i, :], AX.X, ALU.max, negate=True).then_inc(sem["s_read"], 1)

                def na_take(u):
                    dve.wait_ge(sem["o_out"], 10 * l + u + 1)
                    i = u % 2
                    dve.wait_ge(sem["p_exp"], 10 * l + u + 1)
                    dve.reciprocal(SREC[:, i, :] if u < 2 else SREC[:, i, 0:1], SSUM[:, i, :] if u < 2 else SSUM[:, i, 0:1]).then_inc(dve_step, 1)
                    dve.wait_ge(dve_step, step())
                    if u < 2:
                        for c in range(2):
                            h = 2 * c + i
                            ins = TS(NAQK[:, 0, h * 64:h * 64 + 64], PS[:, 6 + i, c * 64:c * 64 + 64], SREC[:, i, c:c + 1], None, ALU.mult)
                    else:
                        t, h = 1 + (u - 2) // 4, (u - 2) % 4
                        ins = TS(NAQK[:, t, h * 64:h * 64 + 64], PS[:, 6 + i, 0:64], SREC[:, i, 0:1], None, ALU.mult)
                    ins.then_inc(sem["o_evac"], 1)

                for i in range(12):
                    if i < 10:
                        na_in(i)
                    if i >= 2:
                        na_take(i - 2)

                def df_max(u):
                    dve.wait_ge(sem["ds_out"], 12 * l + u + 1)
                    if u >= 2:
                        dve.wait_ge(sem["dpt_out"], 12 * l + u - 1)
                    i, w = u % 2, (128 if u < 4 else 384)
                    dve.tensor_reduce(SMX[:, i, :], PS[:, 2 + 2 * i:4 + 2 * i, 0:w], AX.X, ALU.max, negate=True).then_inc(dve_step, 1)
                    dve.wait_ge(dve_step, step())
                    TS(DMX[:, i, :], SMX[:, i, :], 32 ** -0.5, None, ALU.mult).then_inc(sem["d_max"], 1)

                def df_mix(u):
                    dve.wait_ge(sem["d_exp"], 12 * l + u + 1)
                    i, w = u % 2, (128 if u < 4 else 384)
                    dve.reciprocal(DREC[:, i, :], DSUM[:, i, :]).then_inc(dve_step, 1)
                    dve.wait_ge(dve_step, step())
                    TS(ED[:, 2 * i, 0:w], ED[:, 2 * i, 0:w], DREC[:, i, 0:1], None, ALU.mult)
                    TTo(DREC[:, i, 1:2], DREC[:, i, 1:2], LAM[:, 3:4], ALU.mult).then_inc(dve_step, 1)
                    dve.wait_ge(dve_step, step())
                    STT(ED[:, 2 * i, 0:w], ED[:, 2 * i + 1, 0:w], DREC[:, i, 1:2], ED[:, 2 * i, 0:w], ALU.mult, ALU.add).then_inc(sem["d_ready"], 1)

                def df_take(u):
                    dve.wait_ge(sem["do_out"], 12 * l + u + 1)
                    t, h = u // 4, u % 4
                    dve.tensor_copy(DQK[:, t, h * 64:h * 64 + 64], PS[:, 7, 0:64]).then_inc(sem["do_evac"], 1)

                for i in range(14):
                    if i < 12:
                        df_max(i)
                    if 1 <= i <= 12:
                        df_mix(i - 1)
                    if i >= 2:
                        df_take(i - 2)

                def head_norm(src, n, c, scale, eps, power, lo):
                    w_ = W2[:, 0:n * c].rearrange("p (a b) -> p a b", a=n)
                    TTo(w_, src, src, ALU.mult).then_inc(dve_step, 1)
                    dve.wait_ge(dve_step, step())
                    dve.tensor_reduce(SS[:, 0:n], w_, AX.X, ALU.add).then_inc(dve_step, 1)
                    dve.wait_ge(dve_step, step())
                    TS(SS[:, 0:n], SS[:, 0:n], scale, eps, ALU.mult, ALU.add).then_inc(sem["pool_in"], 1)
                    dve.wait_ge(sem["pool_out"], power)

                dve.wait_ge(sem["do_evac"], 12 * (l + 1))
                dve.tensor_copy(W1[:, 0:768].rearrange("p (a b) -> p a b", a=TT), DQK[:, :, 0:256]).then_inc(dve_step, 1)
                dve.wait_ge(dve_step, step())
                o3 = W1[:, 0:768].rearrange("p (a b) -> p a b", b=64)
                head_norm(o3, 12, 64, 1.0 / 64, EPS, 4 * l + 2, 0)
                TTo(o3, o3, over(RS[:, 0:12], 2, 64), ALU.mult).then_inc(dve_step, 1)
                dve.wait_ge(dve_step, step())
                for t in range(TT):
                    ins = STT(DQK[:, t, 0:256].rearrange("p (a b) -> p a b", a=4), W1[:, 256 * t:256 * t + 256].rearrange("p (a b) -> p a b", a=4), 1.0 - lam_init,
                              over(RP("diff_norm"), 1, 4), ALU.mult, ALU.mult)
                ins.then_inc(dve_step, 1)
                dve.wait_ge(dve_step, step())

                def decays(kind):
                    def exponent(c):
                        h, d = c // 2, c % 2
                        k = 16 * l + 8 * kind + c
                        dve.wait_ge(sem["row_out"], k + 1)
                        if c >= 2:
                            dve.wait_ge(sem["pm_ready"], k - 1)
                        row = PS[:, 4 + c % 4, :]
                        e = EDf[:, 512 * (c % 2):512 * (c % 2) + 512]
                        bias = [tmn[:, t, d, kind, h:h + 1] for t in range(TT)]
                        M = K("mask")
                        STT(e[:, 0:128], row[:, 0:128], bias[0], M[:, 0:128] if d == 0 else M[:, 256:384], ALU.subtract, ALU.add)
                        if d == 0:
                            STT(e[:, 128:384], row[:, 128:384], bias[1], M[:, 0:256], ALU.subtract, ALU.add)
                            ins = STT(e[:, 384:512], row[:, 256:384], bias[2], M[:, 0:128], ALU.subtract, ALU.add)
                        else:
                            STT(e[:, 128:256], row[:, 128:256], bias[1], M[:, 256:384], ALU.subtract, ALU.add)
                            ins = STT(e[:, 256:512], row[:, 128:384], bias[2], M[:, 128:384], ALU.subtract, ALU.add)
                        ins.then_inc(sem["e_ready"], 1)

                    def scored(c):
                        h, d = c // 2, c % 2
                        k = 16 * l + 8 * kind + c
                        dve.wait_ge(sem["e_exp"], k + 1)
                        dve.wait_ge(sem["sT_out"], 6 * l + (h + 1 if kind == 0 else 5 + h // 2))
                        e = EDf[:, 512 * (c % 2):512 * (c % 2) + 512]
                        dve.tensor_copy(WS[:, 8 * kind + 4 * d + h:8 * kind + 4 * d + h + 1], e[:, 127:128] if d == 0 else e[:, 0:1])
                        if d == 0:
                            TTo(PM[:, c, 0:384], e[:, 0:384], PS[:, 2, 0:384], ALU.mult)
                            ins = TTo(PM[:, c, 384:512], e[:, 384:512], PS[:, 3, 128:256], ALU.mult)
                        else:
                            TTo(PM[:, c, 0:256], e[:, 0:256], PS[:, 2, 0:256], ALU.mult)
                            ins = TTo(PM[:, c, 256:512], e[:, 256:512], PS[:, 3, 0:256], ALU.mult)
                        ins.then_inc(sem["pm_ready"], 1)

                    exponent(0)
                    for c in range(1, 8):
                        exponent(c)
                        scored(c - 1)
                    scored(7)

                decays(0)
                for i, (t, d, b, bq) in enumerate(((0, 0, 2, None), (0, 1, 3, None), (1, 0, 4, 5), (1, 1, 6, 7), (2, 0, 2, 3), (2, 1, 4, 5))):
                    dve.wait_ge(sem["num_out"], 9 * l + i + 1)
                    dst = NUM[:, 2 * t + d, :, :]
                    src = PS[:, b, 0:260].rearrange("p (a b) -> p a b", a=4)
                    if bq is None:
                        ins = dve.tensor_copy(dst, src)
                    else:
                        qc = PS[:, bq, 0:260].rearrange("p (a b) -> p a b", a=4)
                        TTo(dst, qc, over(WPT[:, t, 4 * d:4 * d + 4], 2, 65), ALU.mult).then_inc(dve_step, 1)
                        dve.wait_ge(dve_step, step())
                        ins = TTo(dst, dst, src, ALU.add)
                    ins.then_inc(sem["num_evac"], 1)
                dve.wait_ge(sem["kt_out"], l + 1)
                for d in range(2):
                    ins = TTo(KW[:, d, :, :], PS[:, 6, 0:256].rearrange("p (a b) -> p a b", a=4), over(WS[:, 4 * d:4 * d + 4], 2, 64), ALU.mult)
                ins.then_inc(sem["kw_ready"], 1)
                dve.wait_ge(st_dma["nav"], 16 * (l + 1))
                dve.wait_ge(st_dma["dv"], 16 * (l + 1))
                for d in range(2):
                    for t in range(TT):
                        ins = TTo(XDT[:, d, t, :, :], XTM[:, t, :].rearrange("p (a b) -> p a b", a=4), over(DTM[:, t, 4 * d:4 * d + 4], 2, 64), ALU.mult)
                ins.then_inc(dve_step, 1)
                dve.wait_ge(dve_step, step())
                dve.wait_ge(sem["num_evac"], 9 * l + 6)
                den = NUM[:, :, :, 64:65].rearrange("p a b c -> p (a b c)")
                emt = EMT.rearrange("p a b -> p (a b)")
                STT(SS[:, 0:24], den, -1.0, den, ALU.mult, ALU.max).then_inc(dve_step, 1)
                dve.wait_ge(dve_step, step())
                TTo(SS[:, 0:24], SS[:, 0:24], emt, ALU.max).then_inc(dve_step, 1)
                dve.wait_ge(dve_step, step())
                dve.reciprocal(SS[:, 0:24], SS[:, 0:24]).then_inc(dve_step, 1)
                dve.wait_ge(dve_step, step())
                hn = W2.rearrange("p (a b) -> p a b", a=24)
                TTo(hn, NUM[:, :, :, 0:64].rearrange("p a b c -> p (a b) c"), over(SS[:, 0:24], 2, 64), ALU.mult).then_inc(dve_step, 1)
                dve.wait_ge(dve_step, step())
                hs = NUM.rearrange("p a b c -> p (a b c)")[:, 0:768].rearrange("p (a b) -> p a b", b=64)
                h2 = W2.rearrange("p (t d h c) -> p t d (h c)", t=TT, d=2, h=4)
                hs3 = NUM.rearrange("p a b c -> p (a b c)")[:, 0:768].rearrange("p (t c) -> p t c", t=TT)
                TTo(hs3, h2[:, :, 0, :], h2[:, :, 1, :], ALU.add).then_inc(dve_step, 1)
                dve.wait_ge(dve_step, step())
                head_norm(hs, 12, 64, 4.0 / 64, 4 * EPS, 4 * l + 3, 0)
                TTo(hs, hs, over(RS[:, 0:12], 2, 64), ALU.mult).then_inc(dve_step, 1)
                dve.wait_ge(dve_step, step())
                TTo(hs3, hs3, over(RP("mlstm_norm"), 1, TT), ALU.mult).then_inc(dve_step, 1)
                dve.wait_ge(dve_step, step())
                dve.wait_ge(sem["tanh_out"], 1 + (l + 1))
                STT(MO[:, :, :], W1[:, 0:768].rearrange("p (a b) -> p a b", a=TT), 1.0, hs3, ALU.add, ALU.mult).then_inc(dve_step, 1)
                dve.wait_ge(dve_step, step())

                decays(1)
                Y = NUM.rearrange("p a b c -> p (a b c)")[:, 0:768].rearrange("p (t c) -> p t c", t=TT)
                for t, b, bq in ((0, 2, None), (1, 3, (4, 5)), (2, 6, (7, 2))):
                    dve.wait_ge(sem["num_out"], 9 * l + 7 + t)
                    y4 = Y[:, t, :].rearrange("p (a b) -> p a b", a=4)
                    TTo(y4, XTM[:, t, :].rearrange("p (a b) -> p a b", a=4), over(RP("ssm_d"), 2, 64), ALU.mult).then_inc(dve_step, 1)
                    dve.wait_ge(dve_step, step())
                    if bq is not None:
                        for g in range(2):
                            qc = PS[:, bq[g], 0:256].rearrange("p (a b c) -> p a b c", a=2, b=2)
                            for d in range(2):
                                w_ = W2[:, 256 * g + 128 * d:256 * g + 128 * d + 128].rearrange("p (b c) -> p b c", b=2)
                                ins = TTo(w_, qc[:, d, :, :], over(WPT[:, t, 8 + 4 * d + 2 * g:8 + 4 * d + 2 * g + 2], 2, 64), ALU.mult)
                        ins.then_inc(dve_step, 1)
                        dve.wait_ge(dve_step, step())
                        for d in range(2):
                            w_ = W2[:, 0:512].rearrange("p (g d c) -> p g d c", g=2, d=2)[:, :, d, :]
                            y3 = Y[:, t, :].rearrange("p (g c) -> p g c", g=2)
                            TTo(y3, y3, w_, ALU.add).then_inc(dve_step, 1)
                            dve.wait_ge(dve_step, step())
                    TTo(Y[:, t, :], Y[:, t, :], PS[:, b, 0:256], ALU.add).then_inc(sem["num_evac"], 1)
                for d in range(2):
                    ins = TTo(KW[:, d, :, :], XDT[:, d, 0, :, :], over(WS[:, 8 + 4 * d:12 + 4 * d], 2, 64), ALU.mult)
                ins.then_inc(sem["kw_ready"], 1)
                dve.wait_ge(sem["num_evac"], 9 * (l + 1))
                STT(SZ[:, :, :], W1[:, 768:1536].rearrange("p (a b) -> p a b", a=TT), 1.0, SZ[:, :, :], ALU.add, ALU.mult).then_inc(dve_step, 1)
                dve.wait_ge(dve_step, step())
                TTo(Y, Y, SZ[:, :, :], ALU.mult).then_inc(dve_step, 1)
                dve.wait_ge(dve_step, step())
                head_norm(Y, 3, 256, 1.0 / 256, 4 * EPS, 4 * (l + 1), 0)
                TTo(Y, Y, over(RS[:, 0:3], 2, 256), ALU.mult).then_inc(dve_step, 1)
                dve.wait_ge(dve_step, step())
                TTo(SZ[:, :, :], Y, over(RP("ssm_norm"), 1, TT), ALU.mult).then_inc(sem["br_ready"], 1)

                dve.wait_ge(sem["brt_evac"], 6 * (l + 1))
                for name, k in (("nak", 1), ("nav", 1), ("dk", 1), ("dv", 1), ("C", 2), ("n", 2), ("ssm", 1)):
                    dve.wait_ge(st_dma[name], 16 * k * (l + 1))
                dve.memset(TMPB[:, 0, 0:1], 0.0).then_inc(sem["tanh_in"], 1)
                for j in range(32):
                    nb, dc = j // 8, j % 8
                    dve.wait_ge(sem["bp_out"], 32 * l + j + 1)
                    dve.wait_ge(sem["fill_evac"], 32 * l + j + 1)
                    gate = GATES[:, dc, :] if nb == 0 else GT[:, j % 2, :]
                    dst = MIX[:, dc, :] if nb == 0 else TMPB[:, j % 2, :]
                    ins = STT(dst, gate, 1.0, PS[:, 2 + j % 4, 0:T], ALU.add, ALU.mult)
                    ins.then_inc(sem["bp_evac"], 1)
                    dve.wait_ge(sem["bp_evac"], 32 * l + j + 1)
                    if nb:
                        ins = TTo(MIX[:, dc, :], MIX[:, dc, :], TMPB[:, j % 2, :], ALU.add)
                        if j < 31:
                            ins.then_inc(dve_step, 1)
                            dve.wait_ge(dve_step, step())
                        else:
                            ins.then_inc(sem["mix_ready"], 1)
                for dc in range(8):
                    dve.wait_ge(sem["wo_out"], 8 * l + dc + 1)
                    for g, (a, b) in enumerate(segs):
                        ins = STT(xT[:, dc, a:b], PS[:, 2 + dc % 4, a:b], mod[:, 16 + dc, g:g + 1], xT[:, dc, a:b], ALU.mult, ALU.add)
                    ins.then_inc(sem["x1_ready"], 1)
                dve.wait_ge(sem["x1_ready"], 8 * (l + 1))
                modulated(1)

                dve.wait_ge(sem["rt_out"], l + 1)
                dve.tensor_reduce(RMX, PS[:, 7, 0:48].rearrange("p (a b) -> p a b", a=TT), AX.X, ALU.max, negate=True).then_inc(sem["rt_max"], 1)
                dve.wait_ge(sem["rt_exp"], l + 1)
                dve.reciprocal(RSUM, RSUM).then_inc(dve_step, 1)
                dve.wait_ge(dve_step, step())
                TTo(AFF, AFF, over(RSUM, 2, NE), ALU.mult).then_inc(sem["aff_ready"], 1)
                dve.wait_ge(sem["afT"], l + 1)
                dve.tensor_copy(AFT[0:NE, :], PS[0:NE, 6, 0:T])
                dve.tensor_copy(WK[0:NE, :], PS[0:NE, 6, 0:T]).then_inc(dve_step, 1)
                dve.wait_ge(dve_step, step())
                for (a, b), rounds in zip(segs, (2, 4)):
                    for _ in range(rounds):
                        dve.max(TOP[0:NE, :], WK[0:NE, a:b]).then_inc(dve_step, 1)
                        dve.wait_ge(dve_step, step())
                        dve.match_replace(WK[0:NE, a:b], TOP[0:NE, :], WK[0:NE, a:b], -1.0).then_inc(dve_step, 1)
                        dve.wait_ge(dve_step, step())
                TS(MSK[0:NE, :], WK[0:NE, :], 0.0, None, ALU.is_lt).then_inc(dve_step, 1)
                dve.wait_ge(dve_step, step())
                for a, b in segs:
                    ins = dve.tensor_tensor_scan(AFT[0:NE, a:b], MSK[0:NE, a:b], zeros[0:NE, :].broadcast_to([NE, b - a]), 0.0, ALU.add, ALU.add)
                ins.then_inc(dve_step, 1)
                dve.wait_ge(dve_step, step())
                TTo(WK[0:NE, :], AFT[0:NE, :], MSK[0:NE, :], ALU.mult).then_inc(sem["pos_ready"], 1)
                dve.wait_ge(sem["posT"], l + 1)
                TS(POS, PS[:, 7, 0:48].rearrange("p (a b) -> p a b", a=TT), -1.0, None, ALU.add).then_inc(dve_step, 1)
                dve.wait_ge(dve_step, step())
                for t in range(TT):
                    TTo(SEL[:, t, :, :], over(K("iota"), 1, NE), over(POS[:, t, :], 2, 32), ALU.is_equal).then_inc(dve_step, 1)
                    dve.wait_ge(dve_step, step())
                    ins = TTo(SELG[:, t, :, :], SEL[:, t, :, :], over(AFF[:, t, :], 2, 32), ALU.mult)
                ins.then_inc(sem["sel_ready"], 1)

                for e in range(NE):
                    g = l * NE + e
                    dve.wait_ge(sem["a_tanh"], g + 1)
                    if e == 0:
                        dve.wait_ge(sem["sgt_evac"], 3 * (l + 1))
                    if e >= 2:
                        dve.wait_ge(sem["ht_out"], g - 1)
                    STT(SA, TH, 1.0, PS[:, 2 * (e % 2), :], ALU.add, ALU.mult).then_inc(dve_step, 1)
                    dve.wait_ge(dve_step, step())
                    dve.wait_ge(sem["u_out"], g + 1)
                    TTo(HH[:, e % 2, :], SA, PS[:, 2 * (e % 2) + 1, :], ALU.mult).then_inc(sem["hh_ready"], 1)
                for dc in range(8):
                    dve.wait_ge(sem["cb_out"], 8 * l + dc + 1)
                    for g, (a, b) in enumerate(segs):
                        ins = STT(xT[:, dc, a:b], PS[:, dc % 4, a:b], mod[:, 40 + dc, g:g + 1], xT[:, dc, a:b], ALU.mult, ALU.add)
                    ins.then_inc(sem["cb_evac"] if dc < 7 else sem["x_ready"], 1)


_WEIGHTS = ["w_ada", "w_in", "w_branch", "w_out", "w_router", "w_gate", "w_up", "w_down"]
_PLAIN = ["x_prompt", "x_sample", "cache_na_k", "cache_na_v", "cache_diff_k", "cache_diff_v"] + _WEIGHTS
_OUTS = [(1, 128, 1024), (1, 256, 1024), (1, 2, 128, 4, 64), (1, 2, 128, 4, 64), (1, 2, 128, 4, 64), (1, 2, 128, 4, 64),
         (1, 2, 2, 4, 64, 64), (1, 2, 2, 4, 64), (1, 2, 2, 4), (1, 2, 2, 4, 64, 64)]


def laid_out(i):
    a = {k: np.asarray(v) for k, v in i.items()}
    f = np.float32
    rows = {"gate_b": a["mlstm_gate_b"].reshape(L, 16), "dt_bias": a["ssm_dt_bias"].reshape(L, 8), "a_log": a["ssm_a_log"].reshape(L, 8),
            "ssm_d": a["ssm_d"], "na_qn": a["na_qnorm_w"], "na_kn": a["na_knorm_w"], "diff_qn": a["diff_qnorm_w"],
            "diff_kn": a["diff_knorm_w"], "diff_norm": a["diff_norm_w"], "mlstm_norm": a["mlstm_norm_w"], "ssm_norm": a["ssm_norm_w"],
            "lambda": a["diff_lambda"].reshape(L, 128)}
    m0 = np.zeros((L, 2, 2, 32), f)
    m0[:, :, 0, 0:4] = a["state_mlstm_m"][0]
    rows["m0"] = m0.reshape(L, 128)
    rowp = np.zeros((L, NROW), f)
    for n, v in rows.items():
        rowp[:, ROW[n][0]:ROW[n][0] + ROW[n][1]] = v
    cols = {"norm1": a["norm1_w"].reshape(L, 8, 128), "norm2": a["norm2_w"].reshape(L, 8, 128), "b_ada": a["b_ada"].reshape(L, 48, 128),
            "conv_w": a["ssm_conv_w"].reshape(L, 5, 4, 128).transpose(0, 2, 1, 3).reshape(L, 20, 128),
            "conv_b": a["ssm_conv_b"].reshape(L, 4, 128), "m0": m0.reshape(L, 1, 128)}
    colp = np.zeros((L, 128, NCOL), f)
    for n, v in cols.items():
        colp[:, :, COL[n][0]:COL[n][0] + COL[n][1]] = v.transpose(0, 2, 1)
    cn = np.concatenate([a["state_mlstm_C"][0], a["state_mlstm_n"][0][..., None]], -1)
    cn = cn.reshape(L, 2, 2, 2, 64, 65).transpose(0, 3, 4, 2, 1, 5)
    c0n = np.zeros((L, 2, 64, 2, 2, 2, 65), f)
    for h in range(2):
        c0n[:, h, :, :, :, h] = cn[:, h]
    c0n = c0n.reshape(L, 128, 520)
    h0t = a["state_ssm"][0].reshape(L, 2, 2, 2, 64, 64).transpose(0, 2, 5, 1, 3, 4).reshape(L, 128, 256)
    cvec = np.stack([a["c_ctx"].reshape(8, 128), a["c"][0].reshape(8, 128)], -1).transpose(1, 0, 2).reshape(128, 16)
    rpb_rev = a["na_rpb"][:, :, :, ::-1].reshape(L * 4 * 15 * 31)
    return {"rowp": rowp, "colp": colp, "c0n": c0n, "h0t": h0t, "cvec": cvec, "rpb_rev": rpb_rev, "consts": constants()}


def kernel(**inputs):
    import concourse.bacc as _bacc
    from concourse.bass_utils import run_bass_kernel_spmd as _run

    nc = _bacc.Bacc("TRN2", target_bir_lowering=False, num_devices=1)
    arrays, dr = {}, {}
    given = {n: inputs[n] for n in _PLAIN}
    given.update(laid_out(inputs))
    for name, v in given.items():
        v = np.ascontiguousarray(v)
        arrays[f"in_{name}"] = v
        dr[name] = nc.dram_tensor(f"in_{name}", v.shape, F32, kind="ExternalInput").ap()
    outs = [nc.dram_tensor(f"out_{i}", shape, F32, kind="ExternalOutput").ap() for i, shape in enumerate(_OUTS)]
    trunk_program(nc, dr, outs)
    r = _run(nc, [arrays], core_ids=[0])
    return tuple(r.results[0][f"out_{i}"] for i in range(len(_OUTS)))
```

```python
import math
from contextlib import ExitStack

import numpy as np

import concourse.bass as bass
from concourse import mybir

F32 = mybir.dt.float32
ALU = mybir.AluOpType
ACT = mybir.ActivationFunctionType
AX = mybir.AxisListType

D = 1024
KC = D // 128
L = 2
TT = 3
T = 128 * TT
NE = 16
IN_COLS = 7448
EPS = 1e-6
NEG = -1e30
RING = 4
SLOT = 4096

C_MQ, C_MV, C_MG, C_NQ, C_NV, C_DK, C_SZ, C_XBC, C_DT, C_GATE = 0, 512, 1024, 1040, 1552, 2064, 2576, 2832, 3344, 3352

ROW_WIDTHS = [("gate_b", 16), ("dt_bias", 8), ("a_log", 8), ("ssm_d", 4), ("na_qn", 64), ("na_kn", 64), ("diff_qn", 32),
              ("diff_kn", 32), ("diff_norm", 64), ("mlstm_norm", 256), ("ssm_norm", 256), ("lambda", 128), ("m0", 128)]
ROW, _at = {}, 0
for _n, _w in ROW_WIDTHS:
    ROW[_n] = (_at, _w)
    _at += _w
NROW = _at
COL_WIDTHS = [("norm1", 8), ("norm2", 8), ("b_ada", 48), ("conv_w", 20), ("conv_b", 4), ("m0", 1)]
COL, _at = {}, 0
for _n, _w in COL_WIDTHS:
    COL[_n] = (_at, _w)
    _at += _w
NCOL = _at
CST_WIDTHS = [("ident", 128), ("mask", 384), ("iota", 32), ("cos", 64), ("sin", 64), ("win", 64), ("adasel", 2),
              ("one", 1), ("eps", 1), ("mhalf", 1)]
CST, _at = {}, 0
for _n, _w in CST_WIDTHS:
    CST[_n] = (_at, _w)
    _at += _w
NCST = _at


SEEN = (((( 0, 0),), ((1, 128),), ((1, 256), (2, 384))), (((0, 0),), ((1, 128), (2, 256)), ((2, 384),)))


def constants():
    c = np.zeros((128, NCST), np.float32)

    def put(name, v):
        o, w = CST[name]
        c[:, o:o + w] = v

    p = np.arange(128)[:, None]
    q = np.arange(128)[None, :]
    put("ident", np.eye(128))
    fwd = np.where(q >= p, 0.0, NEG)
    bwd = np.where(q <= p, 0.0, NEG)
    put("mask", np.concatenate([fwd, np.zeros((128, 128)), bwd], 1))
    put("iota", np.arange(32)[None, :])
    nf = 8
    inv = 10000.0 ** (-np.arange(nf, dtype=np.float32) / np.float32(nf))
    cos, sin = np.zeros((128, 2, 2, 2, nf)), np.zeros((128, 2, 2, 2, nf))
    for tile in range(2):
        t = tile * 128 + np.arange(128)
        for half, pos in enumerate((t // 64, t % 64)):
            ang = (pos.astype(np.float32)[:, None] * inv).astype(np.float32)
            for x12 in range(2):
                cos[:, tile, half, x12] = np.cos(ang)
                sin[:, tile, half, x12] = np.sin(ang) * (-1.0 if x12 == 0 else 1.0)
    put("cos", cos.reshape(128, 64))
    put("sin", sin.reshape(128, 64))
    qc = np.arange(128) % 64
    lo = np.clip(qc - 8, 0, 48)[:, None]
    kc = np.arange(64)[None, :]
    put("win", np.where((kc >= lo) & (kc < lo + 16), 0.0, NEG))
    sel = np.zeros((128, 2))
    for g in range(4):
        for r in range(2):
            sel[32 * g + r, r] = 1.0
    put("adasel", sel)
    put("one", 1.0)
    put("eps", EPS)
    put("mhalf", -0.5)
    return c


N_PROJ = 23
PROJ_TILES = ((C_MQ, 512, 4), (C_NQ, 512, 7), (C_XBC, 512, 11), (C_MV, 512, 14), (C_NV, 512, 17), (C_DK, 512, 20), (C_SZ, 256, 23))
JOBS, JOB_TILES = [], []
for _i in range(4):
    JOBS += [("part", 2 * _i), ("gate", 4 * _i), ("sum", 2 * _i), ("gate", 4 * _i + 1),
             ("part", 2 * _i + 1), ("gate", 4 * _i + 2), ("sum", 2 * _i + 1), ("gate", 4 * _i + 3)]
    JOB_TILES += [("ada", 2 * _i, 8 * _i + 1), ("gate", _i, 8 * _i + 8), ("ada", 2 * _i + 1, 8 * _i + 5)]
for _i in range(4, 8):
    JOBS += [("gate", 4 * _i + _j) for _j in range(4)]
    JOB_TILES += [("gate", _i, 32 + 4 * (_i - 3))]
NJ = len(JOBS)
EARLY = 4
NT_LAYER = 7 + len(JOB_TILES) + 4 + 6 * NE + EARLY
SPILLED = 24
SEMS = ["ada_part", "ada_evac", "ada_sel", "mod_done", "proj_out", "proj_evac", "gpre_out", "xT_out", "xT_evac",
        "c_ready", "sq_ready", "ss_ready", "rms_ready", "h_ready", "small_used", "bm_loaded", "ctx_loaded",
        "gact_in", "gact_e", "gact_out", "gtm_ready", "growT", "rows_ready", "tmT", "tm_evac", "tm_ready", "tm_exp",
        "m_out", "pool_in", "pool_out", "conv_ready", "silu_t", "xs_ready", "xtr_out", "xtr_evac", "nan_ready", "ntr_out",
        "ntr_evac", "dfn_ready", "dtr_out", "dtr_evac", "s_out", "s_read", "p_exp", "p_ready", "pt_out", "pt_evac", "o_out", "o_evac",
        "ds_out", "d_max", "d_exp", "d_ready", "dpt_out", "dpt_evac", "do_out", "do_evac", "job_out", "job_evac", "hx_ready", "ada_taken", "mod_late",
        "row_out", "e_ready", "e_exp", "pm_ready", "sT_out", "num_out", "num_evac", "kt_out", "kw_ready", "st_out",
        "st_evac", "tokens_free", "tanh_out", "y_out", "y_evac", "brt_out", "brt_evac", "br_ready", "bp_out", "bp_evac",
        "mix_ready", "wo_out", "x1_ready", "rt_out", "rt_max", "rt_exp", "aff_ready", "afT", "pos_ready", "posT",
        "sel_ready", "h2t_out", "h2t_evac", "sgt_out", "sgt_evac", "xg_out", "xg_evac", "a_out", "u_out", "a_tanh", "hh_ready",
        "ht_out", "ht_evac", "yd_out", "yd_evac", "cb_out", "cb_evac", "x_ready", "yt_out", "yt_evac", "pool_init"]


def trunk_program(nc, dr, outs):
    (y_prompt, y_sample, new_na_k, new_na_v, new_diff_k, new_diff_v, new_C, new_n, new_m, new_ssm) = outs
    with ExitStack() as ctx:
        def sb(name, shape):
            return ctx.enter_context(nc.sbuf_tensor(name, shape, F32))

        sem = {n: ctx.enter_context(nc.semaphore(n)) for n in SEMS}
        landed = [ctx.enter_context(nc.semaphore(f"landed{i}")) for i in range(RING)]
        par_in = [ctx.enter_context(nc.semaphore(f"par_in{i}")) for i in range(3)]
        dve_step = ctx.enter_context(nc.semaphore("dve_step"))
        st_dma = {n: ctx.enter_context(nc.semaphore("st_" + n)) for n in ("nak", "nav", "dk", "dv", "C", "n", "m", "ssm", "y")}

        spilled = [ctx.enter_context(nc.semaphore(f"spilled{i}")) for i in range(8)]
        gate_in = [ctx.enter_context(nc.semaphore(f"gate_in{i}")) for i in range(4)]
        spill = nc.dram_tensor("gates_spill", (L, 8, 128, 3, T), F32, kind="Internal").ap()

        PS = ctx.enter_context(nc.psum_tensor("banks", [128, 8, 512], F32))
        ring = sb("ring", [128, RING, SLOT])
        wsm = sb("wsm", [128, KC, 24])
        wrt = sb("wrt", [128, KC, NE])
        xT = sb("xT", [128, KC, T])
        hT = sb("hT", [128, KC, T])
        cst = sb("cst", [128, NCST])
        rowp = sb("rowp", [128, NROW])
        colp = sb("colp", [128, NCOL])
        c32 = sb("c32", [128, KC, 32])
        mod = sb("mod", [128, 48, 2])
        amp = sb("amp", [128, 2, 8, 2])
        small = sb("small", [128, 536])
        WORK = 27500
        work = sb("work", [128, WORK])

        def K(name):
            o, w = CST[name]
            return cst[:, o:o + w]

        def RP(name):
            o, w = ROW[name]
            return rowp[:, o:o + w]

        def CP(name):
            o, w = COL[name]
            return colp[:, o:o + w]

        def region(base, end):
            at = [base]

            def take(shape):
                n = int(np.prod(shape))
                v = work[:, at[0]:at[0] + n]
                at[0] += n
                assert at[0] <= end, (at[0], end)
                if len(shape) == 1:
                    return v
                names = "abcd"[:len(shape)]
                spec = f"p ({' '.join(names)}) -> p {' '.join(names)}"
                return v.rearrange(spec, **{k: d for k, d in zip(names[1:], shape[1:])})
            take.at = at
            return take

        t = region(0, WORK)
        V1 = t([TT, 4, 65])
        MO = t([TT, 256])
        NAQK = t([TT, 512])
        base_nv = t.at[0]
        NV = t([TT, 256])
        DV = t([TT, 256])
        DQK = t([TT, 512])
        SZ = t([TT, 256])
        end_u = t.at[0]
        QKT = t([4, T])
        XS = t([4, T])
        base_ctx = t.at[0]
        KRAW = t([2, 256])
        KCT = t([4, 128])
        VC = t([2, 256])
        end_ctx = t.at[0] + 24
        t.at[0] = end_ctx
        base_cw = t.at[0]
        XB = t([4, 392])
        CV = t([4, 392])
        end_cw = t.at[0]
        base_pr = t.at[0]
        BM = t([2, 4, 256])
        PTS = t([2, 384])
        NAT = t([4, T])
        end_pr = t.at[0]
        ED = t([4, 384])
        EDf = ED.rearrange("p a b -> p (a b)")
        XTM = t([TT, 256])
        C0 = t([2, 2, 130])
        H0 = t([256])
        ROWS = t([3, T])
        TM = t([3, T])
        KW = ROWS[:, 1:3, :].rearrange("p a b -> p (a b)")[:, 0:512].rearrange("p (a b c) -> p a b c", a=2, b=4)
        BTM = ROWS[:, 1:3, :].rearrange("p a b -> p (a b)")[:, 512:640]
        base_gates = t.at[0]
        GATES = t([8, T])
        end_mix = t.at[0]
        r = region(base_nv, base_nv + 2 * 768)
        XDT = r([2, TT, 4, 64])
        r = region(base_ctx, end_ctx)
        NUM = r([2 * TT, 4, 65])
        r = region(base_cw, end_cw)
        W1 = r([1536])
        W2 = r([1536])
        WX = work[:, base_cw:base_cw + 2304]
        r = region(base_pr, end_pr)
        PM = r([8, 512])
        r = region(base_pr, end_pr)
        BRT = r([8, T])
        r = region(0, end_u)
        r.at[0] = 0
        MIX = r([8, T])
        TMPB = r([4, T])
        GT = [WX[:, 0:1152], WX[:, 1152:2304], r([1152]), r([1152])]
        GT = [v.rearrange("p (a b) -> p a b", a=3) for v in GT]
        RSTD = W2[:, 0:T]
        QF = QKT.rearrange("p a b -> p (a b)")
        CN_OUT = QF[:, 0:520].rearrange("p (a b c) -> p a b c", a=2, b=4)
        SS_OUT = QF[:, 520:1032].rearrange("p (a b) -> p a b", a=8)
        MPE = GATES[:, 0:3, :].rearrange("p a b -> p (a b)")[:, 0:1024].rearrange("p (a b) -> p a b", a=2)
        MPL = KRAW.rearrange("p a b -> p (a b)")

        m = region(0, WORK)
        XG = m([KC, NE, 2, 32])
        YS = m([4, D])
        YP = m([4, D])
        SGT = m([4, 256])
        SGP = m([4, 128])
        HH = m([2, 512])
        HTT = m([2, 4, 128])
        TH = m([512])
        SA = m([512])
        m2 = region(KC * NE * 64, KC * NE * 64 + 2 * 4 * D)
        H2M = m2([TT, D])
        SEL = m2([TT, NE, 32])
        SELG = m2([TT, NE, 32])
        POS = m2([TT, NE])
        AFF = m2([TT, NE])
        AFT = m2([T])
        WK = m2([T])
        MSK = m2([T])
        XIN = work[:, 0:TT * D].rearrange("p (a b) -> p a b", a=TT)
        YOUT = work[:, 0:TT * D].rearrange("p (a b) -> p a b", a=TT)

        sm = [0]

        def st(shape):
            n = int(np.prod(shape))
            v = small[:, sm[0]:sm[0] + n]
            sm[0] += n
            assert sm[0] <= 536, sm[0]
            if len(shape) == 1:
                return v
            names = "abcd"[:len(shape)]
            return v.rearrange(f"p ({' '.join(names)}) -> p {' '.join(names)}", **{k: d for k, d in zip(names[1:], shape[1:])})

        G1 = st([TT, 24])
        GA = st([TT, 24])
        GL = st([TT, 24])
        DTM = st([TT, 8])
        AEXP = st([8])
        WS = st([16])
        EMT = st([TT, 8])
        SS = st([TT * 24])
        RS = st([TT * 24])
        NM0 = st([1])
        MOUT = st([2])
        LAM = st([8])
        SMX = st([2, 2])
        SSUM = st([2, 2])
        SREC = st([2, 2])
        DMX = st([2, 2])
        DSUM = st([2, 2])
        DREC = st([2, 2])
        WPT = st([TT, 16])
        RMX = st([TT])
        RSUM = st([TT])
        TOP = st([8])

        ident = K("ident")
        zeros = K("iota")[:, 0:1]
        ones = K("one").broadcast_to([128, 128])

        def over(ap, axis, n):
            v = ap.unsqueeze(axis)
            shape = list(v.shape)
            shape[axis] = n
            return v.broadcast_to(shape)

        block = ctx.enter_context(nc.Block())

        @block.sync
        def _(sp):
            count = [0]

            def load(w, c0=0, width=512):
                n = count[0]
                count[0] += 1
                rows = w.shape[0] // 128
                dst = ring[:, n % RING, 0:rows * width].rearrange("p (k n) -> p k n", n=width)
                sp.dma_start(dst, w[:, c0:c0 + width].rearrange("(k p) n -> p k n", p=128)).then_inc(landed[n % RING], 16)

            def load_pair(w):
                for half in range(2):
                    load(w, 512 * half)

            for i in range(EARLY):
                load(dr["w_ada"][0], 512 * i)
            for l in range(L):
                e0 = NE * l
                for i, (c0, width, _) in enumerate(PROJ_TILES):
                    if i >= RING:
                        sp.wait_ge(sem["proj_out"], N_PROJ * l + PROJ_TILES[i - RING][2])
                    elif l == 0:
                        sp.wait_ge(sem["ada_part"], i + 1)
                    elif i < 2:
                        sp.wait_ge(sem["u_out"], e0)
                    else:
                        sp.wait_ge(sem["yd_out"], e0)
                    load(dr["w_in"][l], c0, width)
                for i, (kind, k, _) in enumerate(JOB_TILES):
                    if i < RING:
                        sp.wait_ge(sem["proj_out"], N_PROJ * l + PROJ_TILES[i + 7 - RING][2])
                    else:
                        sp.wait_ge(sem["job_out"], NJ * l + JOB_TILES[i - RING][2])
                    if kind == "ada":
                        load(dr["w_ada"][l], 512 * (EARLY + k))
                    else:
                        load(dr["w_in"][l], C_GATE + 512 * k)
                for i in range(2):
                    sp.wait_ge(sem["job_out"], NJ * l + JOB_TILES[i - RING][2])
                    load(dr["w_branch"][l, 2 * i:2 * i + 2].rearrange("b c d -> (b c) d"), 0, 1024)
                for i in range(2):
                    sp.wait_ge(sem["job_out"], NJ * l + JOB_TILES[i + 2 - RING][2])
                    load(dr["w_out"][l], 512 * i)
                if l < L - 1:
                    for i in range(EARLY):
                        if i < 2:
                            sp.wait_ge(sem["bp_out"], 8 * (l + 1))
                        else:
                            sp.wait_ge(sem["wo_out"], 8 * l + 4 * (i - 1))
                        load(dr["w_ada"][l + 1], 512 * i)
                    sp.wait_ge(sem["ada_part"], EARLY * (l + 1) + 2)
                    load_pair(dr["w_gate"][l, 0])
                    sp.wait_ge(sem["ada_part"], EARLY * (l + 2))
                    load_pair(dr["w_up"][l, 0])
                else:
                    sp.wait_ge(sem["bp_out"], 8 * (l + 1))
                    load_pair(dr["w_gate"][l, 0])
                    sp.wait_ge(sem["wo_out"], 8 * (l + 1))
                    load_pair(dr["w_up"][l, 0])
                sp.wait_ge(sem["a_out"], e0 + 1)
                load_pair(dr["w_gate"][l, 1])
                sp.wait_ge(sem["u_out"], e0 + 1)
                load_pair(dr["w_down"][l, 0])
                sp.wait_ge(sem["a_out"], e0 + 2)
                load_pair(dr["w_up"][l, 1])
                for e in range(2, NE):
                    sp.wait_ge(sem["yd_out"], e0 + e - 1)
                    load_pair(dr["w_gate"][l, e])
                    sp.wait_ge(sem["u_out"], e0 + e)
                    load_pair(dr["w_down"][l, e - 1])
                    sp.wait_ge(sem["a_out"], e0 + e + 1)
                    load_pair(dr["w_up"][l, e])
                sp.wait_ge(sem["yd_out"], e0 + NE - 1)
                load_pair(dr["w_down"][l, NE - 1])

        @block.gpsimd
        def _(pool):
            for l in range(L):
                if l:
                    pool.wait_ge(sem["rt_out"], l)
                    pool.wait_ge(sem["x1_ready"], 8 * l)
                pool.dma_start(rowp[:, :], dr["rowp"][l:l + 1, :].broadcast_to([128, NROW])).then_inc(par_in[1], 16)
                pool.dma_start(colp[:, :], dr["colp"][l]).then_inc(par_in[1], 16)
                pool.dma_start(wsm[:, :, 0:16], dr["w_in"][l, :, C_MG:C_MG + 16].rearrange("(k p) n -> p k n", p=128)).then_inc(par_in[1], 16)
                pool.dma_start(wsm[:, :, 16:24], dr["w_in"][l, :, C_DT:C_DT + 8].rearrange("(k p) n -> p k n", p=128)).then_inc(par_in[1], 16)
                pool.dma_start(wrt[:, :, :], dr["w_router"][l].rearrange("(k p) n -> p k n", p=128)).then_inc(par_in[1], 16)
                if l:
                    pool.wait_ge(sem["x_ready"], 8 * l)
                pool.dma_start(KRAW[:, 0, :], dr["cache_na_k"][0, l].rearrange("t h d -> t (h d)")).then_inc(sem["ctx_loaded"], 16)
                pool.dma_start(KRAW[:, 1, :], dr["cache_diff_k"][0, l].rearrange("t h d -> t (h d)")).then_inc(sem["ctx_loaded"], 16)
                pool.dma_start(VC[:, 0, :], dr["cache_na_v"][0, l].rearrange("t h d -> t (h d)")).then_inc(sem["ctx_loaded"], 16)
                pool.dma_start(VC[:, 1, :], dr["cache_diff_v"][0, l].rearrange("t h d -> t (h d)")).then_inc(sem["ctx_loaded"], 16)
                pool.dma_start(C0[:, :, :, :], dr["c0n"][l].rearrange("p (a b c) -> p a b c", a=2, b=2)).then_inc(sem["ctx_loaded"], 16)
                pool.dma_start(H0[:, :], dr["h0t"][l]).then_inc(sem["ctx_loaded"], 16)
                for h in range(4):
                    for qr in range(4):
                        off = l * 4 * 465 + h * 465 + (7 - qr) * 31 - 48
                        src = bass.AP(dr["rpb_rev"].tensor, off, [[1, 64], [31, 4], [1, 64]])
                        dst = BM[64 * (qr % 2):64 * (qr % 2) + 64, qr // 2, h, :].rearrange("p (a b) -> p a b", a=4)
                        pool.dma_start(dst, src).then_inc(sem["bm_loaded"], 16)

                def power(i, n):
                    pool.wait_ge(sem["pool_in"], 4 * l + i + 1)
                    pool.tensor_tensor(RS[:, 0:n], SS[:, 0:n], K("mhalf").broadcast_to([128, n]), ALU.pow).then_inc(sem["pool_out"], 1)

                power(0, 72)
                pool.wait_ge(sem["nan_ready"], l + 1)
                pool.dma_start(new_na_k[0, l].rearrange("t h d -> t (h d)"), NAQK[:, 0, 256:512]).then_inc(st_dma["nak"], 16)
                pool.wait_ge(sem["proj_evac"], l * N_PROJ + 23)
                pool.dma_start(new_na_v[0, l].rearrange("t h d -> t (h d)"), NV[:, 0, :]).then_inc(st_dma["nav"], 16)
                pool.dma_start(new_diff_v[0, l].rearrange("t h d -> t (h d)"), DV[:, 0, :]).then_inc(st_dma["dv"], 16)
                pool.wait_ge(sem["dfn_ready"], l + 1)
                pool.dma_start(new_diff_k[0, l].rearrange("t h d -> t (h d)"), DQK[:, 0, 256:512]).then_inc(st_dma["dk"], 16)
                pool.wait_ge(sem["m_out"], l + 1)
                pool.dma_start(new_m[0, l, 0].rearrange("(h a) -> h a", a=1), MOUT[0:4, 0:1]).then_inc(st_dma["m"], 16)
                pool.dma_start(new_m[0, l, 1].rearrange("(h a) -> h a", a=1), MOUT[64:68, 1:2]).then_inc(st_dma["m"], 16)
                power(1, 12)
                power(2, 12)
                pool.wait_ge(sem["st_evac"], 3 * l + 2)
                for d in range(2):
                    pool.dma_start(new_C[0, l, d].rearrange("h d e -> d h e"), CN_OUT[0:64, d, :, 0:64]).then_inc(st_dma["C"], 16)
                    pool.dma_start(new_n[0, l, d].rearrange("h (d a) -> d h a", a=1), CN_OUT[0:64, d, :, 64:65], allow_slow_non_contiguous=True).then_inc(st_dma["n"], 16)
                power(3, 3)
                pool.wait_ge(sem["st_evac"], 3 * l + 3)
                pool.dma_start(new_ssm[0, l].rearrange("d h p n -> p (d h) n"), SS_OUT[0:64, :, :]).then_inc(st_dma["ssm"], 16)
            for t in range(TT):
                pool.wait_ge(sem["yt_evac"], 2 * t + 2)
                dst = y_prompt[0] if t == 0 else y_sample[0, 128 * (t - 1):128 * t, :]
                pool.dma_start(dst, YOUT[:, t, :]).then_inc(st_dma["y"], 16)
            for n, k in (("nak", 1), ("nav", 1), ("dk", 1), ("dv", 1), ("C", 2), ("n", 2), ("m", 2), ("ssm", 1)):
                pool.wait_ge(st_dma[n], 16 * k * L)
            pool.wait_ge(st_dma["y"], 16 * TT)

        @block.tensor
        def _(pe):
            def tile(n, b=512):
                pe.wait_ge(landed[n % RING], 16 * (n // RING + 1))
                a = KC if b <= 512 else SLOT // b
                return ring[:, n % RING, 0:a * b].rearrange("p (a b) -> p a b", b=b)

            def ada_partial(bank, w):
                for k in range(KC):
                    g = k % 4
                    mm = pe.matmul(PS[32 * g:32 * g + 32, bank, :], c32[:, k, :], w[:, k, :], start=(k < 4), stop=(k >= 4),
                                   tile_position=(0, 32 * g))
                return mm

            def ada_sum(bank, partial):
                for j in range(4):
                    mm = pe.matmul(PS[:, bank, 2 * j:2 * j + 2], partial[:, j * 128:(j + 1) * 128], K("adasel"), start=True, stop=True)
                return mm

            def ada_early(layer, n):
                for i in range(0, EARLY, 2):
                    for j in range(i, i + 2):
                        w = tile(n + j)
                        if i:
                            pe.wait_ge(sem["ada_taken"], EARLY * layer + j - 1)
                        ada_partial(j % 2, w).then_inc(sem["ada_part"], 1)
                    for j in range(i, i + 2):
                        pe.wait_ge(sem["ada_evac"], EARLY * layer + j + 1)
                        ada_sum(j % 2, MPE[:, j % 2, :]).then_inc(sem["ada_sel"], 1)

            def sum_squares(layer, which, k):
                pe.wait_ge(sem["sq_ready"], 16 * layer + 8 * which + k + 1)
                mm = pe.matmul(PS[:, 6, 0:T], ones, hT[:, k, :], start=(k == 0), stop=(k == KC - 1))
                if k == KC - 1:
                    mm.then_inc(sem["ss_ready"], 1)

            pe.wait_ge(par_in[0], 16 * 3)
            for g in range(6):
                t, h = g // 2, g % 2
                for c in range(4):
                    mm = pe.transpose(PS[:, g, c * 128:(c + 1) * 128], XIN[:, t, (4 * h + c) * 128:(4 * h + c + 1) * 128], ident)
                mm.then_inc(sem["xT_out"], 1)
            for k in range(KC):
                sum_squares(0, 0, k)
            pe.wait_ge(sem["xT_evac"], 6)
            pe.wait_ge(sem["c_ready"], 1)
            ada_early(0, 0)
            for l in range(L):
                n0 = EARLY + NT_LAYER * l
                pe.wait_ge(par_in[1], 80 * (l + 1))
                for t in range(TT):
                    for k in range(KC):
                        if t == 0:
                            pe.wait_ge(sem["h_ready"], 16 * l + k + 1)
                        mm = pe.matmul(PS[:, 7, 24 * t:24 * t + 24], hT[:, k, t * 128:(t + 1) * 128], wsm[:, k, :],
                                       start=(k == 0), stop=(k == KC - 1))
                mm.then_inc(sem["gpre_out"], 1)

                po = [0]

                def out_bank():
                    j = po[0]
                    po[0] += 1
                    if j >= 4:
                        pe.wait_ge(sem["proj_evac"], l * N_PROJ + j - 3)
                    return j % 4

                def feature_major(n):
                    w = tile(n)
                    for c in range(4):
                        b = out_bank()
                        for k in range(KC):
                            mm = pe.matmul(PS[:, b, 0:T], w[:, k, c * 128:(c + 1) * 128], hT[:, k, :], start=(k == 0), stop=(k == KC - 1))
                        mm.then_inc(sem["proj_out"], 1)

                def token_major(n, width=512):
                    w = tile(n, width)
                    for t in range(TT):
                        b = out_bank()
                        for k in range(KC):
                            mm = pe.matmul(PS[:, b, 0:width], hT[:, k, t * 128:(t + 1) * 128], w[:, k, :], start=(k == 0), stop=(k == KC - 1))
                        mm.then_inc(sem["proj_out"], 1)

                def turn3(bank, src, width=128):
                    for t in range(TT):
                        mm = pe.transpose(PS[:, bank, t * 128:(t + 1) * 128], src(t), ident)
                    return mm

                n = n0
                feature_major(n)
                token_major(n + 1)
                feature_major(n + 2)
                token_major(n + 3)
                pe.wait_ge(sem["gtm_ready"], l + 1)
                turn3(4, lambda t: TM[:, 0, t * 128:(t + 1) * 128])
                turn3(5, lambda t: TM[:, 1, t * 128:(t + 1) * 128]).then_inc(sem["growT"], 1)
                token_major(n + 4)
                pe.wait_ge(sem["rows_ready"], l + 1)
                for i in range(3):
                    mm = turn3(4 + i, lambda t: ROWS[:, i, t * 128:(t + 1) * 128])
                mm.then_inc(sem["tmT"], 1)
                token_major(n + 5)
                token_major(n + 6, 256)

                pe.wait_ge(sem["ctx_loaded"], 96 * (l + 1))
                pe.wait_ge(sem["tm_evac"], l + 1)
                for c in range(4):
                    mm = pe.transpose(PS[:, 6, c * 128:(c + 1) * 128], KRAW[:, c // 2, (c % 2) * 128:(c % 2) * 128 + 128], ident)
                mm.then_inc(sem["ntr_out"], 1)

                jobs = [0]

                def job():
                    j = jobs[0]
                    jobs[0] += 1
                    kind, i = JOBS[j]
                    if j >= 2:
                        pe.wait_ge(sem["job_evac"], NJ * l + j - 1)
                    else:
                        pe.wait_ge(sem["proj_evac"], N_PROJ * (l + 1))
                    if kind == "sum":
                        mm = ada_sum(j % 2, MPL)
                    else:
                        at = [(a, b) for a, b, _ in JOB_TILES].index(("ada", i) if kind == "part" else ("gate", i // 4))
                        w = tile(n0 + 7 + at)
                        if kind == "part":
                            if i == 0:
                                pe.wait_ge(sem["ntr_evac"], 4 * l + 1)
                            mm = ada_partial(j % 2, w)
                        else:
                            for k in range(KC):
                                mm = pe.matmul(PS[:, j % 2, 0:T], w[:, k, (i % 4) * 128:(i % 4) * 128 + 128], hT[:, k, :], start=(k == 0), stop=(k == KC - 1))
                    mm.then_inc(sem["job_out"], 1)

                job()
                job()

                pe.wait_ge(sem["xs_ready"], l + 1)
                for t in range(TT):
                    for c in range(2):
                        o = 256 * (t % 2) + 128 * c
                        pe.transpose(PS[:, 4 + t // 2, o:o + 128], XS[:, c, t * 128:(t + 1) * 128], ident)
                pe.transpose(PS[:, 5, 256:384], XS[:, 2, 0:128], ident).then_inc(sem["xtr_out"], 1)

                for _ in range(6):
                    job()
                pe.wait_ge(sem["nan_ready"], l + 1)
                pe.wait_ge(sem["xtr_evac"], l + 1)
                for t, b in ((0, 7), (1, 4), (2, 5)):
                    for c in range(4):
                        mm = pe.transpose(PS[:, b, c * 128:(c + 1) * 128], NAQK[:, t, c * 128:(c + 1) * 128], ident)
                    mm.then_inc(sem["ntr_out"], 1)
                units = [("p", 0), ("p", 1)] + [(t, h) for t in (1, 2) for h in range(4)]

                def na_scores(u):
                    if u >= 2:
                        pe.wait_ge(sem["s_read"], 10 * l + u - 1)
                    else:
                        pe.wait_ge(sem["proj_evac"], (l + 1) * N_PROJ)
                        pe.wait_ge(sem["ntr_evac"], 4 * (l + 1))
                    t, h = units[u]
                    b = 2 + u % 2
                    if t == "p":
                        lo = 64 * h
                        for c in range(2):
                            mm = pe.matmul(PS[:, b, c * 128:(c + 1) * 128], NAT[lo:lo + 64, c, 0:128], NAT[lo:lo + 64, 2 + c, 0:128], start=True, stop=True)
                    else:
                        lo, c = 64 * (h % 2), h // 2
                        q = NAT[lo:lo + 64, c, t * 128:(t + 1) * 128]
                        pe.matmul(PS[:, b, 0:256], q, NAT[lo:lo + 64, 2 + c, 128:384], start=True, stop=True)
                        mm = pe.matmul(PS[:, b, 256:384], q, KCT[lo:lo + 64, c, :], start=True, stop=True)
                    mm.then_inc(sem["s_out"], 1)

                def na_turn(u):
                    pe.wait_ge(sem["p_exp"], 10 * l + u + 1)
                    if u >= 2:
                        pe.wait_ge(sem["pt_evac"], 10 * l + u - 1)
                    for c in range(2 if units[u][0] == "p" else 3):
                        mm = pe.transpose(PS[:, 4 + u % 2, c * 128:(c + 1) * 128], ED[:, u % 2, c * 128:(c + 1) * 128], ident)
                    mm.then_inc(sem["pt_out"], 1)

                def na_out(u):
                    pe.wait_ge(sem["pt_evac"], 10 * l + u + 1)
                    if u >= 2:
                        pe.wait_ge(sem["o_evac"], 10 * l + u - 1)
                    t, h = units[u]
                    b = 6 + u % 2
                    if t == "p":
                        for c in range(2):
                            hh = 2 * c + h
                            mm = pe.matmul(PS[:, b, c * 64:c * 64 + 64], PTS[:, u % 2, c * 128:(c + 1) * 128], NV[:, 0, hh * 64:hh * 64 + 64], start=True, stop=True)
                    else:
                        vs = [NV[:, 1, h * 64:h * 64 + 64], NV[:, 2, h * 64:h * 64 + 64], VC[:, 0, h * 64:h * 64 + 64]]
                        for c in range(3):
                            mm = pe.matmul(PS[:, b, 0:64], PTS[:, u % 2, c * 128:(c + 1) * 128], vs[c], start=(c == 0), stop=(c == 2))
                    mm.then_inc(sem["o_out"], 1)

                for i in range(12):
                    if i < 10:
                        na_scores(i)
                        job()
                    if 1 <= i <= 10:
                        na_turn(i - 1)
                    if i >= 2:
                        na_out(i - 2)

                pe.wait_ge(sem["dfn_ready"], l + 1)
                pe.wait_ge(sem["s_read"], 10 * (l + 1))
                for t in range(TT):
                    for c in range(4):
                        mm = pe.transpose(PS[:, 2 + t, c * 128:(c + 1) * 128], DQK[:, t, c * 128:(c + 1) * 128], ident)
                    mm.then_inc(sem["dtr_out"], 1)
                dunits = [(t, h) for t in range(TT) for h in range(4)]

                def df_scores(u):
                    t, h = dunits[u]
                    if u >= 2:
                        pe.wait_ge(sem["d_exp"], 12 * l + u - 1)
                    else:
                        pe.wait_ge(sem["dtr_evac"], 3 * (l + 1))
                    for mp in range(2):
                        b = 2 + 2 * (u % 2) + mp
                        lo, c = 32 * ((2 * h + mp) % 4), (2 * h + mp) // 4
                        q = NAT[lo:lo + 32, c, t * 128:(t + 1) * 128]
                        if t == 0:
                            mm = pe.matmul(PS[:, b, 0:128], q, NAT[lo:lo + 32, 2 + c, 0:128], start=True, stop=True, tile_position=(lo, 0))
                        else:
                            pe.matmul(PS[:, b, 0:256], q, NAT[lo:lo + 32, 2 + c, 128:384], start=True, stop=True, tile_position=(lo, 0))
                            mm = pe.matmul(PS[:, b, 256:384], q, KCT[lo:lo + 32, 2 + c, :], start=True, stop=True, tile_position=(lo, 0))
                    mm.then_inc(sem["ds_out"], 1)

                def df_turn(u):
                    pe.wait_ge(sem["d_ready"], 12 * l + u + 1)
                    if u:
                        pe.wait_ge(sem["dpt_evac"], 12 * l + u)
                    else:
                        pe.wait_ge(sem["o_evac"], 10 * (l + 1))
                    for c in range(1 if dunits[u][0] == 0 else 3):
                        mm = pe.transpose(PS[:, 6, c * 128:(c + 1) * 128], ED[:, 2 * (u % 2), c * 128:(c + 1) * 128], ident)
                    mm.then_inc(sem["dpt_out"], 1)

                def df_out(u):
                    pe.wait_ge(sem["dpt_evac"], 12 * l + u + 1)
                    if u:
                        pe.wait_ge(sem["do_evac"], 12 * l + u)
                    t, h = dunits[u]
                    vs = [DV[:, 0, h * 64:h * 64 + 64]] if t == 0 else [DV[:, 1, h * 64:h * 64 + 64], DV[:, 2, h * 64:h * 64 + 64], VC[:, 1, h * 64:h * 64 + 64]]
                    for c, v in enumerate(vs):
                        mm = pe.matmul(PS[:, 7, 0:64], PTS[:, u % 2, c * 128:(c + 1) * 128], v, start=(c == 0), stop=(c == len(vs) - 1))
                    mm.then_inc(sem["do_out"], 1)

                for i in range(14):
                    if i < 12:
                        df_scores(i)
                        job()
                    if 1 <= i <= 12:
                        df_turn(i - 1)
                    if i >= 2:
                        df_out(i - 2)

                def scan_scores(kT, qT):
                    pe.matmul(PS[:, 2, 0:128], kT(0), qT(0, 1), start=True, stop=True)
                    pe.matmul(PS[:, 2, 128:384], kT(1), qT(1, 3), start=True, stop=True)
                    pe.matmul(PS[:, 3, 0:256], kT(2), qT(1, 3), start=True, stop=True).then_inc(sem["sT_out"], 1)

                def decay_row(kind, c):
                    h, d = c // 2, c % 2
                    if c >= 4:
                        pe.wait_ge(sem["e_ready"], 16 * l + 8 * kind + c - 3)
                    r = 32 * kind + 64 * d + h
                    pe.matmul(PS[:, 4 + c % 4, 0:T], ident[:, r:r + 1].broadcast_to([128, 128]), ROWS[:, 0, :], start=True, stop=True)\
                        .then_inc(sem["row_out"], 1)

                pe.wait_ge(sem["d_exp"], 12 * (l + 1))
                pe.wait_ge(sem["do_evac"], 12 * (l + 1))
                for c in range(8):
                    decay_row(0, c)
                    if c % 2 == 0:
                        h = c // 2
                        lo, ch = 64 * (h % 2), h // 2
                        if c:
                            pe.wait_ge(sem["pm_ready"], 16 * l + c)
                        scan_scores(lambda s_: QKT[lo:lo + 64, 2 + ch, s_ * 128:(s_ + 1) * 128],
                                    lambda a, b: QKT[lo:lo + 64, ch, a * 128:b * 128])
                    job()

                def over_keys(dst, pairs, v):
                    for i, (d, ks, off) in enumerate(pairs):
                        mm = pe.matmul(dst, PM[:, 2 * h + d, off:off + 128], v(d, ks), start=(i == 0), stop=(i == len(pairs) - 1))
                    return mm

                pe.wait_ge(sem["pm_ready"], 16 * l + 8)
                for i, (t, d, b, bq) in enumerate(((0, 0, 2, None), (0, 1, 3, None), (1, 0, 4, 5), (1, 1, 6, 7), (2, 0, 2, 3), (2, 1, 4, 5))):
                    if i >= 4:
                        pe.wait_ge(sem["num_evac"], 9 * l + i - 2)
                    for h in range(4):
                        mm = over_keys(PS[:, b, 65 * h:65 * h + 65], [(d, ks, off) for ks, off in SEEN[d][t]], lambda _, ks: V1[:, ks, h, :])
                    if bq is not None:
                        for ch in range(2):
                            mm = pe.matmul(PS[:, bq, 130 * ch:130 * ch + 130], QKT[:, ch, t * 128:(t + 1) * 128], C0[:, ch, d, :], start=True, stop=True)
                    mm.then_inc(sem["num_out"], 1)
                pe.wait_ge(sem["num_evac"], 9 * l + 4)
                for c in range(2):
                    mm = pe.transpose(PS[:, 6, c * 128:(c + 1) * 128], QKT[:, 2 + c, 0:128], ident)
                mm.then_inc(sem["kt_out"], 1)
                job()
                pe.wait_ge(sem["kw_ready"], 2 * l + 1)
                pe.wait_ge(sem["num_evac"], 9 * l + 5)
                for d in range(2):
                    for h in range(4):
                        mm = pe.matmul(PS[0:64, 7 if d == 0 else 2, 65 * h:65 * h + 65], KW[:, d, h, :], V1[:, 0, h, :], start=True, stop=True)
                mm.then_inc(sem["st_out"], 1)

                job()
                pe.wait_ge(sem["st_evac"], 3 * l + 2)
                pe.wait_ge(sem["num_evac"], 9 * l + 6)
                for c in range(8):
                    decay_row(1, c)
                    if c % 4 == 0:
                        lo = 64 * (c // 4)
                        if c:
                            pe.wait_ge(sem["pm_ready"], 16 * l + 8 + c)
                        scan_scores(lambda s_: XS[lo:lo + 64, 2, s_ * 128:(s_ + 1) * 128],
                                    lambda a, b: XS[lo:lo + 64, 3, a * 128:b * 128])
                    if c >= 2:
                        job()
                pe.wait_ge(sem["pm_ready"], 16 * l + 16)
                for t, b, bq in ((0, 2, None), (1, 3, (4, 5)), (2, 6, (7, 2))):
                    for h in range(4):
                        mm = over_keys(PS[:, b, 64 * h:64 * h + 64], [(d, ks, off) for d in range(2) for ks, off in SEEN[d][t]],
                                       lambda d, ks: XDT[:, d, ks, h, :])
                    if bq is not None:
                        for g in range(2):
                            if t == 2 and g == 1:
                                pe.wait_ge(sem["num_evac"], 9 * l + 7)
                            mm = pe.matmul(PS[:, bq[g], 0:256], XS[64 * g:64 * g + 64, 3, t * 128:(t + 1) * 128], H0[64 * g:64 * g + 64, :], start=True, stop=True)
                    mm.then_inc(sem["num_out"], 1)
                pe.wait_ge(sem["kw_ready"], 2 * l + 2)
                pe.wait_ge(sem["num_evac"], 9 * l + 8)
                for d in range(2):
                    for h in range(4):
                        c = 4 * d + h
                        mm = pe.matmul(PS[0:64, 3, 64 * c:64 * c + 64], KW[:, d, h, :], BTM[:, 64 * (h // 2):64 * (h // 2) + 64], start=True, stop=True)
                mm.then_inc(sem["st_out"], 1)

                job()
                job()

                pe.wait_ge(sem["br_ready"], l + 1)
                pe.wait_ge(sem["st_evac"], 3 * (l + 1))
                pe.wait_ge(sem["num_evac"], 9 * (l + 1))
                for g in range(6):
                    t, half = g // 2, g % 2
                    srcs = (MO, NAQK) if half == 0 else (DQK, SZ)
                    for c in range(4):
                        mm = pe.transpose(PS[:, 2 + g, c * 128:(c + 1) * 128], srcs[c // 2][:, t, (c % 2) * 128:(c % 2) * 128 + 128], ident)
                    mm.then_inc(sem["brt_out"], 1)
                pe.wait_ge(sem["brt_evac"], 6 * (l + 1))
                pe.wait_ge(sem["job_evac"], NJ * (l + 1))
                for dc in range(8):
                    w = [tile(n0 + 23 + i, 1024) for i in range(2)] if dc == 0 else w
                    if dc >= 2:
                        pe.wait_ge(sem["bp_evac"], 8 * l + dc - 1)
                    for nb in range(4):
                        for k in range(2):
                            mm = pe.matmul(PS[:, 4 * (dc % 2) + nb, 0:T], w[nb // 2][:, 2 * (nb % 2) + k, dc * 128:(dc + 1) * 128],
                                           BRT[:, 2 * nb + k, :], start=(k == 0), stop=(k == 1))
                    mm.then_inc(sem["bp_out"], 1)
                pe.wait_ge(sem["mix_ready"], 8 * (l + 1))
                for dc in range(8):
                    w = tile(n0 + 25 + dc // 4)
                    if dc >= 4:
                        pe.wait_ge(sem["x1_ready"], 8 * l + dc - 3)
                    for k in range(KC):
                        mm = pe.matmul(PS[:, 2 + dc % 4, 0:T], w[:, k, (dc % 4) * 128:(dc % 4) * 128 + 128], MIX[:, k, :], start=(k == 0), stop=(k == KC - 1))
                    mm.then_inc(sem["wo_out"], 1)
                    if dc >= 2:
                        sum_squares(l, 1, dc - 2)
                sum_squares(l, 1, KC - 2)
                sum_squares(l, 1, KC - 1)

                for t in range(TT):
                    for k in range(KC):
                        if t == 0:
                            pe.wait_ge(sem["h_ready"], 16 * l + 8 + k + 1)
                        mm = pe.matmul(PS[:, 7, 16 * t:16 * t + 16], hT[:, k, t * 128:(t + 1) * 128], wrt[:, k, :], start=(k == 0), stop=(k == KC - 1))
                mm.then_inc(sem["rt_out"], 1)
                pe.wait_ge(sem["x1_ready"], 8 * (l + 1))
                for g in range(6):
                    t, half = g // 2, g % 2
                    for c in range(4):
                        mm = pe.transpose(PS[:, g, c * 128:(c + 1) * 128], hT[:, 4 * half + c, t * 128:(t + 1) * 128], ident)
                    mm.then_inc(sem["h2t_out"], 1)
                pe.wait_ge(sem["aff_ready"], l + 1)
                for t in range(TT):
                    mm = pe.transpose(PS[0:NE, 6, t * 128:(t + 1) * 128], AFF[:, t, :], ident)
                mm.then_inc(sem["afT"], 1)
                if l < L - 1:
                    pe.wait_ge(sem["h2t_evac"], 6 * (l + 1))
                    ada_early(l + 1, n0 + 27)
                pe.wait_ge(sem["pos_ready"], l + 1)
                for t in range(TT):
                    mm = pe.transpose(PS[:, 7, 16 * t:16 * t + 16], WK[0:NE, t * 128:(t + 1) * 128], ident[0:NE, 0:NE])
                mm.then_inc(sem["posT"], 1)

                pe.wait_ge(sem["sel_ready"], l + 1)
                pe.wait_ge(sem["h2t_evac"], 6 * (l + 1))
                if l < L - 1:
                    pe.wait_ge(sem["ada_taken"], EARLY * (l + 2))
                for q in range(16):
                    dc, grp = q // 2, q % 2
                    if q >= 4:
                        pe.wait_ge(sem["xg_evac"], 16 * l + q - 3)
                    ts = (1, 2) if grp == 0 else (0,)
                    for i, t in enumerate(ts):
                        mm = pe.matmul(PS[:, q % 4, :], H2M[:, t, dc * 128:(dc + 1) * 128], SEL[:, t, :, :].rearrange("p a b -> p (a b)"),
                                       start=(i == 0), stop=(i == len(ts) - 1))
                    mm.then_inc(sem["xg_out"], 1)
                for i in range(3):
                    for j in range(4):
                        if i < 2:
                            eb, t = 2 * i + j // 2, 1 + j % 2
                        else:
                            eb, t = j, 0
                        mm = pe.transpose(PS[:, 4 + i, j * 128:(j + 1) * 128], SELG[:, t, 4 * eb:4 * eb + 4, :].rearrange("p a b -> p (a b)"), ident)
                    mm.then_inc(sem["sgt_out"], 1)
                pe.wait_ge(sem["xg_evac"], 16 * (l + 1))
                pe.wait_ge(sem["sgt_evac"], 3 * (l + 1))

                base = n0 + 27 + (EARLY if l < L - 1 else 0)

                def pair_tiles(i):
                    return tile(base + i), tile(base + i + 1)

                def project(dst, w2, x):
                    for k in range(KC):
                        for hf in range(2):
                            mm = pe.matmul(dst[64 * hf:64 * hf + 64, :], x(k), w2[hf][:, k, :], start=(k == 0), stop=(k == KC - 1),
                                           tile_position=(0, 64 * hf))
                    return mm

                def expert_a(e):
                    g = l * NE + e
                    if e >= 2:
                        pe.wait_ge(sem["hh_ready"], g - 1)
                    project(PS[:, 2 * (e % 2), :], pair_tiles(0 if e == 0 else 6 * e - 2),
                            lambda k: XG[:, k, e, :, :].rearrange("p a b -> p (a b)")).then_inc(sem["a_out"], 1)

                def expert_u(e):
                    project(PS[:, 2 * (e % 2) + 1, :], pair_tiles(2 if e == 0 else 6 * e + 2),
                            lambda k: XG[:, k, e, :, :].rearrange("p a b -> p (a b)")).then_inc(sem["u_out"], 1)

                def expert_down(e):
                    g = l * NE + e
                    pe.wait_ge(sem["hh_ready"], g + 1)
                    if e:
                        pe.wait_ge(sem["ht_evac"], g)
                    for c in range(4):
                        mm = pe.transpose(PS[:, 4, c * 128:(c + 1) * 128], HH[:, e % 2, c * 128:(c + 1) * 128], ident)
                    mm.then_inc(sem["ht_out"], 1)
                    pe.wait_ge(sem["ht_evac"], g + 1)
                    if e >= 2:
                        pe.wait_ge(sem["yd_evac"], g - 1)
                    project(PS[:, 5 + e % 2, :], pair_tiles(6 * e + 6 if e < NE - 1 else 6 * e + 4),
                            lambda k: HTT[:, e % 2, k % 4, 64 * (k // 4):64 * (k // 4) + 64]).then_inc(sem["yd_out"], 1)

                expert_a(0)
                expert_u(0)
                for e in range(1, NE):
                    expert_a(e)
                    expert_down(e - 1)
                    expert_u(e)
                expert_down(NE - 1)

                pe.wait_ge(sem["yd_evac"], NE * (l + 1))
                for dc in range(8):
                    if dc >= 4:
                        pe.wait_ge(sem["x_ready"], 8 * l + dc - 3)
                    for eb in range(4):
                        pe.matmul(PS[:, dc % 4, 0:128], YP[:, eb, dc * 128:(dc + 1) * 128], SGP[:, eb, :], start=(eb == 0), stop=(eb == 3))
                    for eb in range(4):
                        mm = pe.matmul(PS[:, dc % 4, 128:384], YS[:, eb, dc * 128:(dc + 1) * 128], SGT[:, eb, :], start=(eb == 0), stop=(eb == 3))
                    mm.then_inc(sem["cb_out"], 1)
                    if dc >= 2 and l < L - 1:
                        sum_squares(l + 1, 0, dc - 2)
                if l < L - 1:
                    sum_squares(l + 1, 0, KC - 2)
                    sum_squares(l + 1, 0, KC - 1)
            pe.wait_ge(sem["x_ready"], 8 * L)
            for g in range(6):
                t, h = g // 2, g % 2
                for c in range(4):
                    mm = pe.transpose(PS[:, g, c * 128:(c + 1) * 128], xT[:, 4 * h + c, t * 128:(t + 1) * 128], ident)
                mm.then_inc(sem["yt_out"], 1)

        @block.scalar
        def _(act):
            def copy(dst, src, scale=1.0):
                return act.activation(dst, src, ACT.Copy, scale=scale)

            act.dma_start(small[:, 0:16], dr["cvec"]).then_inc(par_in[2], 16)
            act.dma_start(cst[:, :], dr["consts"]).then_inc(par_in[0], 16)
            act.dma_start(XIN[:, 0, :], dr["x_prompt"][0]).then_inc(par_in[0], 16)
            act.dma_start(XIN[:, 1:3, :], dr["x_sample"][0].rearrange("(t p) d -> p t d", p=128)).then_inc(par_in[0], 16)
            act.wait_ge(par_in[2], 16)
            act.activation(small[:, 16:32], small[:, 0:16], ACT.Tanh, scale=0.5).then_inc(sem["tanh_out"], 1)
            for g in range(6):
                t, h = g // 2, g % 2
                act.wait_ge(sem["xT_out"], g + 1)
                ins = copy(xT[:, 4 * h:4 * h + 4, t * 128:(t + 1) * 128], PS[:, g, :].rearrange("p (a b) -> p a b", a=4))
                ins.then_inc(sem["xT_evac"], 1)
            act.wait_ge(sem["xT_evac"], 6)

            def squares(k):
                act.activation(hT[:, k, :], xT[:, k, :], ACT.Square).then_inc(sem["sq_ready"], 1)

            def root(layer, which):
                act.wait_ge(sem["ss_ready"], 2 * layer + which + 1)
                act.activation(RSTD, PS[:, 6, 0:T], ACT.Sqrt, scale=1.0 / D, bias=K("eps")).then_inc(sem["rms_ready"], 1)

            def modulate(layer, which):
                for k in range(KC):
                    act.wait_ge(sem["hx_ready"], 16 * layer + 8 * which + k + 1)
                    for g, (a, b) in enumerate(((0, 128), (128, 384))):
                        ins = act.activation(hT[:, k, a:b], hT[:, k, a:b], ACT.Identity, scale=amp[:, which, k, g:g + 1],
                                             bias=mod[:, 24 * which + k, g:g + 1])
                    ins.then_inc(sem["h_ready"], 1)

            def ada_early(layer):
                for i in range(0, EARLY, 2):
                    for j in range(i, i + 2):
                        act.wait_ge(sem["ada_part"], EARLY * layer + j + 1)
                        copy(MPE[:, j % 2, :], PS[:, j % 2, :]).then_inc(sem["ada_evac"], 1)
                    for j in range(i, i + 2):
                        act.wait_ge(sem["ada_sel"], EARLY * layer + j + 1)
                        copy(mod[:, 4 * j:4 * j + 4, :], PS[:, j % 2, 0:8].rearrange("p (a b) -> p a b", a=4)).then_inc(sem["ada_taken"], 1)

            for k in range(KC):
                squares(k)
            root(0, 0)
            ada_early(0)
            for l in range(L):
                modulate(l, 0)

                j = [0]

                def proj(dsts):
                    j[0] += 1
                    act.wait_ge(sem["proj_out"], l * N_PROJ + j[0])
                    b = (j[0] - 1) % 4
                    for i, (dst, lo, hi, scale) in enumerate(dsts):
                        src = PS[:, b, lo:hi]
                        if len(dst.shape) == 3:
                            src = src.rearrange("p (a b) -> p a b", a=dst.shape[1])
                        ins = copy(dst, src, scale)
                    ins.then_inc(sem["proj_evac"], 1)

                for c in range(4):
                    proj([(QKT[:, c, :], 0, T, 1.0 if c < 2 else 0.125)])
                for t in range(TT):
                    proj([(NAQK[:, t, :], 0, 512, 1.0)])
                act.wait_ge(sem["gact_in"], l + 1)
                act.activation(GL, GA, ACT.Exp, scale=-1.0).then_inc(sem["gact_e"], 1)
                act.wait_ge(sem["gact_e"], l + 1)
                act.activation(GL, GL, ACT.Ln, bias=1.0)
                act.activation(AEXP, RP("a_log"), ACT.Exp).then_inc(sem["gact_out"], 1)
                for c in range(4):
                    proj([(XB[:, c, 2:130], 0, 128, 1.0), (XB[:, c, 134:390], 128, T, 1.0)])
                for t in range(TT):
                    proj([(V1[:, t, :, 0:64], 0, 256, 1.0), (MO[:, t, :], 256, 512, 1.0)])
                for t in range(TT):
                    proj([(NV[:, t, :], 0, 256, 1.0), (DQK[:, t, 0:256], 256, 512, 1.0)])
                act.wait_ge(sem["tmT"], l + 1)
                for i in range(3):
                    ins = copy(TM[:, i, :], PS[:, 4 + i, 0:T])
                ins.then_inc(sem["tm_evac"], 1)
                for t in range(TT):
                    proj([(DQK[:, t, 256:512], 0, 256, 1.0), (DV[:, t, :], 256, 512, 1.0)])
                for t in range(TT):
                    proj([(SZ[:, t, :], 0, 256, 1.0)])
                act.wait_ge(sem["tm_ready"], l + 1)
                act.activation(WPT, WPT, ACT.Exp)
                act.activation(EMT, EMT, ACT.Exp)
                act.activation(LAM[:, 0:2], LAM[:, 0:2], ACT.Exp).then_inc(sem["tm_exp"], 1)
                act.wait_ge(sem["ntr_out"], 4 * l + 1)
                copy(KCT, PS[:, 6, :].rearrange("p (a b) -> p a b", a=4)).then_inc(sem["ntr_evac"], 1)
                act.wait_ge(sem["conv_ready"], l + 1)
                for c in range(4):
                    ins = act.activation(XS[:, c, 0:128], CV[:, c, 2:130], ACT.Tanh, scale=0.5)
                    ins = act.activation(XS[:, c, 128:384], CV[:, c, 134:390], ACT.Tanh, scale=0.5)
                ins.then_inc(sem["silu_t"], 1)
                act.wait_ge(sem["xtr_out"], l + 1)
                copy(XTM[:, 0:2, :], PS[:, 4, :].rearrange("p (a b) -> p a b", a=2))
                copy(XTM[:, 2, :], PS[:, 5, 0:256])
                copy(BTM, PS[:, 5, 256:384]).then_inc(sem["xtr_evac"], 1)

                jobs = [0]

                def take_job():
                    j = jobs[0]
                    jobs[0] += 1
                    kind, i = JOBS[j]
                    act.wait_ge(sem["job_out"], NJ * l + j + 1)
                    if kind == "part":
                        ins = copy(MPL, PS[:, j % 2, :])
                    elif kind == "sum":
                        ins = copy(mod[:, 4 * (EARLY + i):4 * (EARLY + i) + 4, :], PS[:, j % 2, 0:8].rearrange("p (a b) -> p a b", a=4))
                    else:
                        if 8 <= i:
                            act.wait_ge(spilled[i % 8], 16 * (SPILLED // 8 * l + i // 8))
                        ins = act.activation(GATES[:, i % 8, :], PS[:, j % 2, 0:T], ACT.Tanh, scale=0.5)
                    ins.then_inc(sem["job_evac"], 1)
                    if j and JOBS[j - 1][0] == "gate" and JOBS[j - 1][1] < SPILLED:
                        g = JOBS[j - 1][1]
                        act.wait_ge(sem["job_evac"], NJ * l + j)
                        act.dma_start(spill[l, g % 8, :, g // 8, :], GATES[:, g % 8, :]).then_inc(spilled[g % 8], 16)

                for _ in range(8):
                    take_job()
                for i, b in enumerate((7, 4, 5)):
                    act.wait_ge(sem["ntr_out"], 4 * l + i + 2)
                    copy(NAT[:, :, i * 128:(i + 1) * 128], PS[:, b, :].rearrange("p (a b) -> p a b", a=4)).then_inc(sem["ntr_evac"], 1)

                def na_exp(u):
                    act.wait_ge(sem["s_read"], 10 * l + u + 1)
                    if u < 2:
                        for c in range(2):
                            ins = act.activation(ED[:, u, c * 128:(c + 1) * 128], ED[:, 2 + u, c * 128:(c + 1) * 128], ACT.Exp,
                                                 bias=SMX[:, u, c:c + 1], accum_out=SSUM[:, u, c:c + 1])
                    else:
                        ins = act.activation(ED[:, u % 2, :], ED[:, 2 + u % 2, :], ACT.Exp, bias=SMX[:, u % 2, 0:1], accum_out=SSUM[:, u % 2, 0:1])
                    ins.then_inc(sem["p_exp"], 1)

                def na_turned(u):
                    act.wait_ge(sem["pt_out"], 10 * l + u + 1)
                    w = 256 if u < 2 else 384
                    copy(PTS[:, u % 2, 0:w], PS[:, 4 + u % 2, 0:w]).then_inc(sem["pt_evac"], 1)

                for i in range(11):
                    if i < 10:
                        if i >= 2:
                            act.wait_ge(sem["o_evac"], 10 * l + i - 1)
                        na_exp(i)
                        take_job()
                    if i >= 1:
                        na_turned(i - 1)
                for t in range(TT):
                    act.wait_ge(sem["dtr_out"], 3 * l + t + 1)
                    copy(NAT[:, :, t * 128:(t + 1) * 128], PS[:, 2 + t, :].rearrange("p (a b) -> p a b", a=4)).then_inc(sem["dtr_evac"], 1)

                def df_exp(u):
                    act.wait_ge(sem["d_max"], 12 * l + u + 1)
                    w = 128 if u < 4 else 384
                    for mp in range(2):
                        ins = act.activation(ED[:, 2 * (u % 2) + mp, 0:w], PS[:, 2 + 2 * (u % 2) + mp, 0:w], ACT.Exp,
                                             scale=32 ** -0.5, bias=DMX[:, u % 2, mp:mp + 1], accum_out=DSUM[:, u % 2, mp:mp + 1])
                    ins.then_inc(sem["d_exp"], 1)

                def df_turned(u):
                    act.wait_ge(sem["dpt_out"], 12 * l + u + 1)
                    w = 128 if u < 4 else 384
                    copy(PTS[:, u % 2, 0:w], PS[:, 6, 0:w]).then_inc(sem["dpt_evac"], 1)

                for i in range(13):
                    if i < 12:
                        df_exp(i)
                        take_job()
                    if i >= 1:
                        df_turned(i - 1)

                def combos(kind):
                    for c in range(8):
                        act.wait_ge(sem["e_ready"], 16 * l + 8 * kind + c + 1)
                        i = c % 2
                        act.activation(EDf[:, 512 * i:512 * i + 512], EDf[:, 512 * i:512 * i + 512], ACT.Exp).then_inc(sem["e_exp"], 1)
                        if kind == 0 or c >= 2:
                            take_job()

                combos(0)
                act.activation(W1[:, 0:768].rearrange("p (a b) -> p a b", a=TT), MO[:, :, :], ACT.Tanh, scale=0.5)
                act.activation(W1[:, 768:1536].rearrange("p (a b) -> p a b", a=TT), SZ[:, :, :], ACT.Tanh, scale=0.5).then_inc(sem["tanh_out"], 1)
                take_job()
                act.wait_ge(sem["st_out"], 2 * l + 1)
                for d in range(2):
                    copy(CN_OUT[0:64, d, :, :], PS[0:64, 7 if d == 0 else 2, 0:260].rearrange("p (a b) -> p a b", a=4)).then_inc(sem["st_evac"], 1)
                take_job()
                combos(1)
                act.wait_ge(sem["st_out"], 2 * l + 2)
                copy(SS_OUT[0:64, :, :], PS[0:64, 3, :].rearrange("p (a b) -> p a b", a=8)).then_inc(sem["st_evac"], 1)
                take_job()
                take_job()
                for g in range(6):
                    t, half = g // 2, g % 2
                    act.wait_ge(sem["brt_out"], 6 * l + g + 1)
                    copy(BRT[:, 4 * half:4 * half + 4, t * 128:(t + 1) * 128], PS[:, 2 + g, :].rearrange("p (a b) -> p a b", a=4)).then_inc(sem["brt_evac"], 1)
                for slot in spilled:
                    act.wait_ge(slot, 16 * (SPILLED // 8) * (l + 1))
                for dc in range(8):
                    if dc == 0:
                        act.wait_ge(sem["br_ready"], l + 1)
                    if dc == 2:
                        act.wait_ge(sem["tokens_free"], l + 1)
                    if dc >= 4:
                        act.wait_ge(sem["mix_ready"], 8 * l + dc - 3)
                    act.dma_start(GT[dc % 4], spill[l, dc]).then_inc(gate_in[dc % 4], 16)
                for k in range(KC):
                    act.wait_ge(sem["x1_ready"], 8 * l + k + 1)
                    squares(k)
                root(l, 1)
                modulate(l, 1)

                for t in range(TT):
                    act.wait_ge(sem["rt_max"], l + 1)
                    ins = act.activation(AFF[:, t, :], PS[:, 7, 16 * t:16 * t + 16], ACT.Exp, bias=RMX[:, t:t + 1], accum_out=RSUM[:, t:t + 1])
                ins.then_inc(sem["rt_exp"], 1)
                for g in range(6):
                    t, half = g // 2, g % 2
                    act.wait_ge(sem["h2t_out"], 6 * l + g + 1)
                    copy(H2M[:, t, 512 * half:512 * half + 512], PS[:, g, :]).then_inc(sem["h2t_evac"], 1)
                if l < L - 1:
                    ada_early(l + 1)
                for q in range(0, 16):
                    dc, grp = q // 2, q % 2
                    act.wait_ge(sem["xg_out"], 16 * l + q + 1)
                    copy(XG[:, dc, :, grp, :], PS[:, q % 4, :].rearrange("p (a b) -> p a b", a=NE)).then_inc(sem["xg_evac"], 1)
                for i in range(3):
                    act.wait_ge(sem["sgt_out"], 3 * l + i + 1)
                    if i < 2:
                        ins = copy(SGT[:, 2 * i:2 * i + 2, :], PS[:, 4 + i, :].rearrange("p (a b) -> p a b", a=2))
                    else:
                        ins = copy(SGP, PS[:, 6, :].rearrange("p (a b) -> p a b", a=4))
                    ins.then_inc(sem["sgt_evac"], 1)

                def tanh_a(e):
                    g = l * NE + e
                    act.wait_ge(sem["a_out"], g + 1)
                    if e:
                        act.wait_ge(sem["hh_ready"], g)
                    act.activation(TH, PS[:, 2 * (e % 2), :], ACT.Tanh, scale=0.5).then_inc(sem["a_tanh"], 1)

                def down_side(e):
                    g = l * NE + e
                    act.wait_ge(sem["ht_out"], g + 1)
                    if e >= 2:
                        act.wait_ge(sem["yd_out"], g - 1)
                    copy(HTT[:, e % 2, :, :], PS[:, 4, :].rearrange("p (a b) -> p a b", a=4)).then_inc(sem["ht_evac"], 1)

                def take_y(e):
                    g = l * NE + e
                    act.wait_ge(sem["yd_out"], g + 1)
                    b, eb, o = 5 + e % 2, e // 4, 32 * (e % 4)
                    copy(YS[o:o + 32, eb, 0:512], PS[0:32, b, :])
                    copy(YP[o:o + 32, eb, 0:512], PS[32:64, b, :])
                    copy(YS[o:o + 32, eb, 512:1024], PS[64:96, b, :])
                    copy(YP[o:o + 32, eb, 512:1024], PS[96:128, b, :]).then_inc(sem["yd_evac"], 1)

                tanh_a(0)
                for e in range(1, NE):
                    tanh_a(e)
                    down_side(e - 1)
                    take_y(e - 1)
                down_side(NE - 1)
                take_y(NE - 1)
                if l < L - 1:
                    for k in range(KC):
                        act.wait_ge(sem["x_ready"], 8 * l + k + 1)
                        squares(k)
                    root(l + 1, 0)
            for g in range(6):
                t, h = g // 2, g % 2
                act.wait_ge(sem["yt_out"], g + 1)
                copy(YOUT[:, t, 512 * h:512 * h + 512], PS[:, g, :]).then_inc(sem["yt_evac"], 1)

        @block.vector
        def _(dve):
            steps = [0]

            def step():
                steps[0] += 1
                return steps[0]

            TTo, TS, STT = dve.tensor_tensor, dve.tensor_scalar, dve.scalar_tensor_tensor

            dve.memset(c32[:, :, :], 0.0).then_inc(sem["pool_init"], 1)
            dve.wait_ge(sem["pool_init"], 1)
            dve.wait_ge(sem["tanh_out"], 1)
            dve.wait_ge(par_in[2], 16)
            TS(small[:, 32:48], small[:, 0:16], 0.5, None, ALU.mult).then_inc(dve_step, 1)
            dve.wait_ge(dve_step, step())
            STT(c32[:, :, 0:2], small[:, 16:32].rearrange("p (a b) -> p a b", a=8), 1.0, small[:, 32:48].rearrange("p (a b) -> p a b", a=8),
                ALU.add, ALU.mult).then_inc(sem["c_ready"], 1)
            dve.wait_ge(sem["c_ready"], 1)
            dve.wait_ge(sem["xT_evac"], 6)
            for l in range(L):
                lam_init = 0.8 - 0.6 * math.exp(-0.3 * l)
                dve.wait_ge(par_in[1], 80 * (l + 1))
                dve.wait_ge(sem["ada_taken"], EARLY * (l + 1))
                TTo(mod[:, 0:16, :], mod[:, 0:16, :], over(CP("b_ada")[:, 0:16], 2, 2), ALU.add).then_inc(dve_step, 1)
                dve.wait_ge(dve_step, step())
                STT(amp[:, 0, :, :], mod[:, 8:16, :], 1.0, over(CP("norm1"), 2, 2), ALU.add, ALU.mult).then_inc(dve_step, 1)
                dve.wait_ge(dve_step, step())

                def modulated(which):
                    dve.wait_ge(sem["rms_ready"], 2 * l + which + 1)
                    dve.reciprocal(RSTD, RSTD).then_inc(dve_step, 1)
                    dve.wait_ge(dve_step, step())
                    for k in range(KC):
                        TTo(hT[:, k, :], xT[:, k, :], RSTD, ALU.mult).then_inc(sem["hx_ready"], 1)
                    dve.wait_ge(sem["hx_ready"], 16 * l + 8 * (which + 1))

                modulated(0)
                dve.memset(TM[:, 0:2, :], 0.0)
                dve.memset(V1[:, :, :, 64:65], 1.0)
                for a in (0, 130, 132, 390):
                    ins = dve.memset(XB[:, :, a:a + 2], 0.0)
                ins.then_inc(dve_step, 1)
                dve.wait_ge(dve_step, step())

                dve.wait_ge(sem["gpre_out"], l + 1)
                g3 = PS[:, 7, 0:72].rearrange("p (a b) -> p a b", a=TT)
                TTo(G1, g3, over(rowp[:, 0:24], 1, TT), ALU.add).then_inc(dve_step, 1)
                dve.wait_ge(dve_step, step())
                STT(GA, G1, -1.0, G1, ALU.mult, ALU.max).then_inc(sem["gact_in"], 1)
                lam = RP("lambda").rearrange("p (a b c) -> p a b c", a=2, b=2)
                TTo(SS[:, 0:64].rearrange("p (a b) -> p a b", a=2), lam[:, :, 0, :], lam[:, :, 1, :], ALU.mult).then_inc(dve_step, 1)
                dve.wait_ge(dve_step, step())
                dve.tensor_reduce(LAM[:, 0:2], SS[:, 0:64].rearrange("p (a b) -> p a b", a=2), AX.X, ALU.add).then_inc(dve_step, 1)
                dve.wait_ge(dve_step, step())
                dve.wait_ge(sem["gact_out"], l + 1)
                gf = TM[:, 0, :].rearrange("p (t d k h) -> p t d k h", t=TT, d=2, k=2)
                gi = TM[:, 1, :].rearrange("p (t d k h) -> p t d k h", t=TT, d=2, k=2)
                STT(DTM, G1[:, :, 16:24], 0.0, GL[:, :, 16:24], ALU.max, ALU.add).then_inc(dve_step, 1)
                dve.wait_ge(dve_step, step())
                for d in range(2):
                    STT(gf[:, :, d, 0, 0:4], G1[:, :, 8 * d + 4:8 * d + 8], 0.0, GL[:, :, 8 * d + 4:8 * d + 8], ALU.min, ALU.subtract)
                    dve.tensor_copy(gi[:, :, d, 0, 0:4], G1[:, :, 8 * d:8 * d + 4])
                    ins = STT(gf[:, :, d, 1, 0:4], DTM[:, :, 4 * d:4 * d + 4], -1.0, over(AEXP[:, 4 * d:4 * d + 4], 1, TT), ALU.mult, ALU.mult)
                ins.then_inc(sem["gtm_ready"], 1)
                dve.wait_ge(sem["gtm_ready"], l + 1)
                dve.wait_ge(sem["proj_evac"], l * N_PROJ + 11)
                for c in range(4):
                    for jj in range(5):
                        wv = CP("conv_w")[:, 5 * c + jj:5 * c + jj + 1]
                        src = XB[:, c, jj:jj + 388]
                        if jj == 0:
                            ins = TS(CV[:, c, 2:390], src, wv, CP("conv_b")[:, c:c + 1], ALU.mult, ALU.add)
                        else:
                            ins = STT(CV[:, c, 2:390], src, wv, CV[:, c, 2:390], ALU.mult, ALU.add)
                        if jj < 4:
                            ins.then_inc(dve_step, 1)
                            dve.wait_ge(dve_step, step())
                ins.then_inc(sem["conv_ready"], 1)
                dve.wait_ge(sem["conv_ready"], l + 1)

                dve.wait_ge(sem["growT"], l + 1)
                segs = ((0, 128), (128, 384))
                for lo, rev in ((0, False), (64, True)):
                    for a, b in segs:
                        def run(v):
                            v = v[lo:lo + 64, a:b]
                            return v[:, ::-1] if rev else v
                        ins = dve.tensor_tensor_scan(run(ROWS[:, 2, :]), run(PS[:, 4, 0:T]), zeros[lo:lo + 64, :].broadcast_to([64, b - a]), 0.0, ALU.add, ALU.add)
                TS(NM0, CP("m0"), -1.0, None, ALU.mult)
                ins.then_inc(dve_step, 1)
                dve.wait_ge(dve_step, step())
                TTo(ROWS[:, 1, :], ROWS[:, 2, :], PS[:, 5, 0:T], ALU.subtract)
                dve.tensor_copy(ROWS[:, 0, :], ROWS[:, 2, :]).then_inc(dve_step, 1)
                dve.wait_ge(dve_step, step())
                for lo, rev in ((0, False), (64, True)):
                    for i, (a, b) in enumerate(segs):
                        def run(v):
                            v = v[lo:lo + 4, a:b]
                            return v[:, ::-1] if rev else v
                        ins = dve.tensor_tensor_scan(run(ROWS[:, 0, :]), run(ROWS[:, 1, :]), run(ROWS[:, 1, :]),
                                                     NM0[lo:lo + 4, :] if i else 0.0, ALU.min, ALU.min)
                ins.then_inc(sem["rows_ready"], 1)
                dve.wait_ge(sem["rows_ready"], l + 1)
                TTo(MOUT[0:4, 0:1], ROWS[0:4, 2, 127:128], ROWS[0:4, 0, 127:128], ALU.subtract)
                TTo(MOUT[64:68, 1:2], ROWS[64:68, 2, 0:1], ROWS[64:68, 0, 0:1], ALU.subtract).then_inc(sem["m_out"], 1)
                dve.wait_ge(sem["tm_evac"], l + 1)
                tmr, tmn, tmb = (TM[:, i, :].rearrange("p (t d k h) -> p t d k h", t=TT, d=2, k=2) for i in range(3))
                m0 = RP("m0").rearrange("p (d k h) -> p d k h", d=2, k=2)
                for k in range(2):
                    for d in range(2):
                        TTo(WPT[:, :, 8 * k + 4 * d:8 * k + 4 * d + 4], tmr[:, :, d, k, 0:4], over(m0[:, d, k, 0:4], 1, TT), ALU.add)
                for d in range(2):
                    ins = TTo(EMT[:, :, 4 * d:4 * d + 4], tmr[:, :, d, 0, 0:4], tmb[:, :, d, 0, 0:4], ALU.subtract)
                ins.then_inc(sem["tm_ready"], 1)

                dve.wait_ge(sem["silu_t"], l + 1)
                TS(CV[:, :, 2:390], CV[:, :, 2:390], 0.5, None, ALU.mult).then_inc(dve_step, 1)
                dve.wait_ge(dve_step, step())
                STT(XS[:, :, 0:128], XS[:, :, 0:128], 1.0, CV[:, :, 2:130], ALU.add, ALU.mult)
                STT(XS[:, :, 128:384], XS[:, :, 128:384], 1.0, CV[:, :, 134:390], ALU.add, ALU.mult).then_inc(sem["xs_ready"], 1)

                dve.wait_ge(sem["xs_ready"], l + 1)
                sq = W1.rearrange("p (a b) -> p a b", a=TT)
                dve.wait_ge(sem["proj_evac"], l * N_PROJ + 20)
                TTo(sq, NAQK[:, :, :], NAQK[:, :, :], ALU.mult).then_inc(dve_step, 1)
                dve.wait_ge(dve_step, step())
                dve.tensor_reduce(SS[:, 0:24], W1.rearrange("p (a b) -> p a b", b=64), AX.X, ALU.add).then_inc(dve_step, 1)
                dve.wait_ge(dve_step, step())
                TTo(sq, DQK[:, :, :], DQK[:, :, :], ALU.mult).then_inc(dve_step, 1)
                dve.wait_ge(dve_step, step())
                dve.tensor_reduce(SS[:, 24:72], W1.rearrange("p (a b) -> p a b", b=32), AX.X, ALU.add).then_inc(dve_step, 1)
                dve.wait_ge(dve_step, step())
                TS(SS[:, 0:24], SS[:, 0:24], 1.0 / 64, EPS, ALU.mult, ALU.add)
                TS(SS[:, 24:72], SS[:, 24:72], 1.0 / 32, EPS, ALU.mult, ALU.add).then_inc(sem["pool_in"], 1)
                dve.wait_ge(sem["pool_out"], 4 * l + 1)
                na = NAQK.rearrange("p t (g c) -> p (t g) c", c=64)
                TTo(na, na, over(RS[:, 0:24], 2, 64), ALU.mult).then_inc(dve_step, 1)
                dve.wait_ge(dve_step, step())
                for i, name in enumerate(("na_qn", "na_kn")):
                    ins = [TTo(NAQK[:, t, 256 * i:256 * i + 256].rearrange("p (g c) -> p g c", c=64), NAQK[:, t, 256 * i:256 * i + 256].rearrange("p (g c) -> p g c", c=64),
                               over(RP(name), 1, 4), ALU.mult) for t in range(TT)][-1]
                ins.then_inc(sem["nan_ready"], 1)
                df = DQK.rearrange("p t (g c) -> p (t g) c", c=32)
                TTo(df, df, over(RS[:, 24:72], 2, 32), ALU.mult).then_inc(dve_step, 1)
                dve.wait_ge(dve_step, step())
                for i, name in enumerate(("diff_qn", "diff_kn")):
                    for t in range(TT):
                        v = DQK[:, t, 256 * i:256 * i + 256].rearrange("p (g c) -> p g c", c=32)
                        ins = TTo(v, v, over(RP(name), 1, 8), ALU.mult)
                ins.then_inc(dve_step, 1)
                dve.wait_ge(dve_step, step())
                for t in range(2):
                    x4 = DQK[:, 1 + t, :].rearrange("p (g c) -> p g c", c=32)
                    cos = over(K("cos")[:, 32 * t:32 * t + 32], 1, 16)
                    TTo(W1[:, 512 * t:512 * t + 512].rearrange("p (g c) -> p g c", c=32), x4, cos, ALU.mult).then_inc(dve_step, 1)
                    dve.wait_ge(dve_step, step())
                    sin = K("sin")[:, 32 * t:32 * t + 32].rearrange("p (a b c) -> p a b c", a=2, b=2)
                    x5 = DQK[:, 1 + t, :].rearrange("p (g a b c) -> p g a b c", g=16, a=2, b=2)
                    w5 = W2[:, 512 * t:512 * t + 512].rearrange("p (g a b c) -> p g a b c", g=16, a=2, b=2)
                    for b in range(2):
                        ins = TTo(w5[:, :, :, b, :], x5[:, :, :, 1 - b, :], over(sin[:, :, b, :], 1, 16), ALU.mult)
                    ins.then_inc(dve_step, 1)
                    dve.wait_ge(dve_step, step())
                    ins = TTo(DQK[:, 1 + t, :], W1[:, 512 * t:512 * t + 512], W2[:, 512 * t:512 * t + 512], ALU.add)
                dve.wait_ge(sem["tm_exp"], l + 1)
                TTo(LAM[:, 2:3], LAM[:, 1:2], LAM[:, 0:1], ALU.subtract).then_inc(dve_step, 1)
                dve.wait_ge(dve_step, step())
                TS(LAM[:, 3:4], LAM[:, 2:3], -lam_init, None, ALU.add).then_inc(sem["dfn_ready"], 1)
                dve.wait_ge(sem["dfn_ready"], l + 1)

                dve.wait_ge(sem["bm_loaded"], 256 * (l + 1))
                win = over(K("win"), 1, 16)
                for t in range(2):
                    v = BM[:, t, :, :].rearrange("p h (r c) -> p (h r) c", c=64)
                    w_ = W1[:, 0:1024].rearrange("p (a b) -> p a b", a=16)
                    TTo(w_, v[:, :, ::-1], win, ALU.add).then_inc(dve_step, 1)
                    dve.wait_ge(dve_step, step())
                    dve.tensor_copy(v, w_).then_inc(dve_step, 1)
                    dve.wait_ge(dve_step, step())

                na_s = 64 ** -0.5

                def na_in(u):
                    dve.wait_ge(sem["s_out"], 10 * l + u + 1)
                    if u >= 2:
                        dve.wait_ge(sem["p_exp"], 10 * l + u - 1)
                    i = u % 2
                    if u < 2:
                        TS(ED[:, 2 + i, 0:256], PS[:, 2 + i, 0:256], na_s, None, ALU.mult).then_inc(dve_step, 1)
                        dve.wait_ge(dve_step, step())
                        dve.tensor_reduce(SMX[:, i, :], ED[:, 2 + i, 0:256].rearrange("p (a b) -> p a b", a=2), AX.X, ALU.max, negate=True)\
                            .then_inc(sem["s_read"], 1)
                    else:
                        t, h = (u - 2) // 4, (u - 2) % 4
                        TS(ED[:, 2 + i, 256:384], PS[:, 2 + i, 256:384], na_s, None, ALU.mult)
                        STT(ED[:, 2 + i, 0:256], PS[:, 2 + i, 0:256], na_s, BM[:, t, h, :], ALU.mult, ALU.add).then_inc(dve_step, 1)
                        dve.wait_ge(dve_step, step())
                        dve.tensor_reduce(SMX[:, i, 0:1], ED[:, 2 + i, :], AX.X, ALU.max, negate=True).then_inc(sem["s_read"], 1)

                def na_take(u):
                    dve.wait_ge(sem["o_out"], 10 * l + u + 1)
                    i = u % 2
                    dve.wait_ge(sem["p_exp"], 10 * l + u + 1)
                    dve.reciprocal(SREC[:, i, :] if u < 2 else SREC[:, i, 0:1], SSUM[:, i, :] if u < 2 else SSUM[:, i, 0:1]).then_inc(dve_step, 1)
                    dve.wait_ge(dve_step, step())
                    if u < 2:
                        for c in range(2):
                            h = 2 * c + i
                            ins = TS(NAQK[:, 0, h * 64:h * 64 + 64], PS[:, 6 + i, c * 64:c * 64 + 64], SREC[:, i, c:c + 1], None, ALU.mult)
                    else:
                        t, h = 1 + (u - 2) // 4, (u - 2) % 4
                        ins = TS(NAQK[:, t, h * 64:h * 64 + 64], PS[:, 6 + i, 0:64], SREC[:, i, 0:1], None, ALU.mult)
                    ins.then_inc(sem["o_evac"], 1)

                for i in range(12):
                    if i < 10:
                        na_in(i)
                    if i >= 2:
                        na_take(i - 2)

                def df_max(u):
                    dve.wait_ge(sem["ds_out"], 12 * l + u + 1)
                    if u >= 2:
                        dve.wait_ge(sem["dpt_out"], 12 * l + u - 1)
                    i, w = u % 2, (128 if u < 4 else 384)
                    dve.tensor_reduce(SMX[:, i, :], PS[:, 2 + 2 * i:4 + 2 * i, 0:w], AX.X, ALU.max, negate=True).then_inc(dve_step, 1)
                    dve.wait_ge(dve_step, step())
                    TS(DMX[:, i, :], SMX[:, i, :], 32 ** -0.5, None, ALU.mult).then_inc(sem["d_max"], 1)

                def df_mix(u):
                    dve.wait_ge(sem["d_exp"], 12 * l + u + 1)
                    i, w = u % 2, (128 if u < 4 else 384)
                    dve.reciprocal(DREC[:, i, :], DSUM[:, i, :]).then_inc(dve_step, 1)
                    dve.wait_ge(dve_step, step())
                    TS(ED[:, 2 * i, 0:w], ED[:, 2 * i, 0:w], DREC[:, i, 0:1], None, ALU.mult)
                    TTo(DREC[:, i, 1:2], DREC[:, i, 1:2], LAM[:, 3:4], ALU.mult).then_inc(dve_step, 1)
                    dve.wait_ge(dve_step, step())
                    STT(ED[:, 2 * i, 0:w], ED[:, 2 * i + 1, 0:w], DREC[:, i, 1:2], ED[:, 2 * i, 0:w], ALU.mult, ALU.add).then_inc(sem["d_ready"], 1)

                def df_take(u):
                    dve.wait_ge(sem["do_out"], 12 * l + u + 1)
                    t, h = u // 4, u % 4
                    dve.tensor_copy(DQK[:, t, h * 64:h * 64 + 64], PS[:, 7, 0:64]).then_inc(sem["do_evac"], 1)

                for i in range(14):
                    if i < 12:
                        df_max(i)
                    if 1 <= i <= 12:
                        df_mix(i - 1)
                    if i >= 2:
                        df_take(i - 2)

                def head_norm(src, n, c, scale, eps, power, lo):
                    w_ = W2[:, 0:n * c].rearrange("p (a b) -> p a b", a=n)
                    TTo(w_, src, src, ALU.mult).then_inc(dve_step, 1)
                    dve.wait_ge(dve_step, step())
                    dve.tensor_reduce(SS[:, 0:n], w_, AX.X, ALU.add).then_inc(dve_step, 1)
                    dve.wait_ge(dve_step, step())
                    TS(SS[:, 0:n], SS[:, 0:n], scale, eps, ALU.mult, ALU.add).then_inc(sem["pool_in"], 1)
                    dve.wait_ge(sem["pool_out"], power)

                dve.wait_ge(sem["do_evac"], 12 * (l + 1))
                dve.tensor_copy(W1[:, 0:768].rearrange("p (a b) -> p a b", a=TT), DQK[:, :, 0:256]).then_inc(dve_step, 1)
                dve.wait_ge(dve_step, step())
                o3 = W1[:, 0:768].rearrange("p (a b) -> p a b", b=64)
                head_norm(o3, 12, 64, 1.0 / 64, EPS, 4 * l + 2, 0)
                TTo(o3, o3, over(RS[:, 0:12], 2, 64), ALU.mult).then_inc(dve_step, 1)
                dve.wait_ge(dve_step, step())
                for t in range(TT):
                    ins = STT(DQK[:, t, 0:256].rearrange("p (a b) -> p a b", a=4), W1[:, 256 * t:256 * t + 256].rearrange("p (a b) -> p a b", a=4), 1.0 - lam_init,
                              over(RP("diff_norm"), 1, 4), ALU.mult, ALU.mult)
                ins.then_inc(dve_step, 1)
                dve.wait_ge(dve_step, step())

                def decays(kind):
                    def exponent(c):
                        h, d = c // 2, c % 2
                        k = 16 * l + 8 * kind + c
                        dve.wait_ge(sem["row_out"], k + 1)
                        if c >= 2:
                            dve.wait_ge(sem["pm_ready"], k - 1)
                        row = PS[:, 4 + c % 4, :]
                        e = EDf[:, 512 * (c % 2):512 * (c % 2) + 512]
                        bias = [tmn[:, t, d, kind, h:h + 1] for t in range(TT)]
                        M = K("mask")
                        STT(e[:, 0:128], row[:, 0:128], bias[0], M[:, 0:128] if d == 0 else M[:, 256:384], ALU.subtract, ALU.add)
                        if d == 0:
                            STT(e[:, 128:384], row[:, 128:384], bias[1], M[:, 0:256], ALU.subtract, ALU.add)
                            ins = STT(e[:, 384:512], row[:, 256:384], bias[2], M[:, 0:128], ALU.subtract, ALU.add)
                        else:
                            STT(e[:, 128:256], row[:, 128:256], bias[1], M[:, 256:384], ALU.subtract, ALU.add)
                            ins = STT(e[:, 256:512], row[:, 128:384], bias[2], M[:, 128:384], ALU.subtract, ALU.add)
                        ins.then_inc(sem["e_ready"], 1)

                    def scored(c):
                        h, d = c // 2, c % 2
                        k = 16 * l + 8 * kind + c
                        dve.wait_ge(sem["e_exp"], k + 1)
                        dve.wait_ge(sem["sT_out"], 6 * l + (h + 1 if kind == 0 else 5 + h // 2))
                        e = EDf[:, 512 * (c % 2):512 * (c % 2) + 512]
                        dve.tensor_copy(WS[:, 8 * kind + 4 * d + h:8 * kind + 4 * d + h + 1], e[:, 127:128] if d == 0 else e[:, 0:1])
                        if d == 0:
                            TTo(PM[:, c, 0:384], e[:, 0:384], PS[:, 2, 0:384], ALU.mult)
                            ins = TTo(PM[:, c, 384:512], e[:, 384:512], PS[:, 3, 128:256], ALU.mult)
                        else:
                            TTo(PM[:, c, 0:256], e[:, 0:256], PS[:, 2, 0:256], ALU.mult)
                            ins = TTo(PM[:, c, 256:512], e[:, 256:512], PS[:, 3, 0:256], ALU.mult)
                        ins.then_inc(sem["pm_ready"], 1)

                    exponent(0)
                    for c in range(1, 8):
                        exponent(c)
                        scored(c - 1)
                    scored(7)

                decays(0)
                dve.wait_ge(sem["job_evac"], NJ * l + JOBS.index(("sum", 7)) + 1)
                TTo(mod[:, 16:48, :], mod[:, 16:48, :], over(CP("b_ada")[:, 16:48], 2, 2), ALU.add).then_inc(dve_step, 1)
                dve.wait_ge(dve_step, step())
                STT(amp[:, 1, :, :], mod[:, 32:40, :], 1.0, over(CP("norm2"), 2, 2), ALU.add, ALU.mult)
                TS(mod[:, 16:24, :], mod[:, 16:24, :], 0.5, None, ALU.mult)
                TS(mod[:, 40:48, :], mod[:, 40:48, :], 0.5, None, ALU.mult).then_inc(dve_step, 1)
                dve.wait_ge(dve_step, step())
                for i, (t, d, b, bq) in enumerate(((0, 0, 2, None), (0, 1, 3, None), (1, 0, 4, 5), (1, 1, 6, 7), (2, 0, 2, 3), (2, 1, 4, 5))):
                    dve.wait_ge(sem["num_out"], 9 * l + i + 1)
                    dst = NUM[:, 2 * t + d, :, :]
                    src = PS[:, b, 0:260].rearrange("p (a b) -> p a b", a=4)
                    if bq is None:
                        ins = dve.tensor_copy(dst, src)
                    else:
                        qc = PS[:, bq, 0:260].rearrange("p (a b) -> p a b", a=4)
                        TTo(dst, qc, over(WPT[:, t, 4 * d:4 * d + 4], 2, 65), ALU.mult).then_inc(dve_step, 1)
                        dve.wait_ge(dve_step, step())
                        ins = TTo(dst, dst, src, ALU.add)
                    ins.then_inc(sem["num_evac"], 1)
                dve.wait_ge(sem["kt_out"], l + 1)
                for d in range(2):
                    ins = TTo(KW[:, d, :, :], PS[:, 6, 0:256].rearrange("p (a b) -> p a b", a=4), over(WS[:, 4 * d:4 * d + 4], 2, 64), ALU.mult)
                ins.then_inc(sem["kw_ready"], 1)
                dve.wait_ge(st_dma["nav"], 16 * (l + 1))
                dve.wait_ge(st_dma["dv"], 16 * (l + 1))
                for d in range(2):
                    for t in range(TT):
                        ins = TTo(XDT[:, d, t, :, :], XTM[:, t, :].rearrange("p (a b) -> p a b", a=4), over(DTM[:, t, 4 * d:4 * d + 4], 2, 64), ALU.mult)
                ins.then_inc(dve_step, 1)
                dve.wait_ge(dve_step, step())
                dve.wait_ge(sem["num_evac"], 9 * l + 6)
                den = NUM[:, :, :, 64:65].rearrange("p a b c -> p (a b c)")
                emt = EMT.rearrange("p a b -> p (a b)")
                STT(SS[:, 0:24], den, -1.0, den, ALU.mult, ALU.max).then_inc(dve_step, 1)
                dve.wait_ge(dve_step, step())
                TTo(SS[:, 0:24], SS[:, 0:24], emt, ALU.max).then_inc(dve_step, 1)
                dve.wait_ge(dve_step, step())
                dve.reciprocal(SS[:, 0:24], SS[:, 0:24]).then_inc(dve_step, 1)
                dve.wait_ge(dve_step, step())
                hn = W2.rearrange("p (a b) -> p a b", a=24)
                TTo(hn, NUM[:, :, :, 0:64].rearrange("p a b c -> p (a b) c"), over(SS[:, 0:24], 2, 64), ALU.mult).then_inc(dve_step, 1)
                dve.wait_ge(dve_step, step())
                hs = NUM.rearrange("p a b c -> p (a b c)")[:, 0:768].rearrange("p (a b) -> p a b", b=64)
                h2 = W2.rearrange("p (t d h c) -> p t d (h c)", t=TT, d=2, h=4)
                hs3 = NUM.rearrange("p a b c -> p (a b c)")[:, 0:768].rearrange("p (t c) -> p t c", t=TT)
                TTo(hs3, h2[:, :, 0, :], h2[:, :, 1, :], ALU.add).then_inc(dve_step, 1)
                dve.wait_ge(dve_step, step())
                head_norm(hs, 12, 64, 4.0 / 64, 4 * EPS, 4 * l + 3, 0)
                TTo(hs, hs, over(RS[:, 0:12], 2, 64), ALU.mult).then_inc(dve_step, 1)
                dve.wait_ge(dve_step, step())
                TTo(hs3, hs3, over(RP("mlstm_norm"), 1, TT), ALU.mult).then_inc(dve_step, 1)
                dve.wait_ge(dve_step, step())
                dve.wait_ge(sem["tanh_out"], 1 + (l + 1))
                STT(MO[:, :, :], W1[:, 0:768].rearrange("p (a b) -> p a b", a=TT), 1.0, hs3, ALU.add, ALU.mult).then_inc(dve_step, 1)
                dve.wait_ge(dve_step, step())

                decays(1)
                Y = NUM.rearrange("p a b c -> p (a b c)")[:, 0:768].rearrange("p (t c) -> p t c", t=TT)
                for t, b, bq in ((0, 2, None), (1, 3, (4, 5)), (2, 6, (7, 2))):
                    dve.wait_ge(sem["num_out"], 9 * l + 7 + t)
                    y4 = Y[:, t, :].rearrange("p (a b) -> p a b", a=4)
                    TTo(y4, XTM[:, t, :].rearrange("p (a b) -> p a b", a=4), over(RP("ssm_d"), 2, 64), ALU.mult).then_inc(dve_step, 1)
                    dve.wait_ge(dve_step, step())
                    if bq is not None:
                        for g in range(2):
                            qc = PS[:, bq[g], 0:256].rearrange("p (a b c) -> p a b c", a=2, b=2)
                            for d in range(2):
                                w_ = W2[:, 256 * g + 128 * d:256 * g + 128 * d + 128].rearrange("p (b c) -> p b c", b=2)
                                ins = TTo(w_, qc[:, d, :, :], over(WPT[:, t, 8 + 4 * d + 2 * g:8 + 4 * d + 2 * g + 2], 2, 64), ALU.mult)
                        ins.then_inc(dve_step, 1)
                        dve.wait_ge(dve_step, step())
                        for d in range(2):
                            w_ = W2[:, 0:512].rearrange("p (g d c) -> p g d c", g=2, d=2)[:, :, d, :]
                            y3 = Y[:, t, :].rearrange("p (g c) -> p g c", g=2)
                            TTo(y3, y3, w_, ALU.add).then_inc(dve_step, 1)
                            dve.wait_ge(dve_step, step())
                    TTo(Y[:, t, :], Y[:, t, :], PS[:, b, 0:256], ALU.add).then_inc(sem["num_evac"], 1)
                for d in range(2):
                    ins = TTo(KW[:, d, :, :], XDT[:, d, 0, :, :], over(WS[:, 8 + 4 * d:12 + 4 * d], 2, 64), ALU.mult)
                ins.then_inc(sem["kw_ready"], 1)
                dve.wait_ge(sem["num_evac"], 9 * (l + 1))
                STT(SZ[:, :, :], W1[:, 768:1536].rearrange("p (a b) -> p a b", a=TT), 1.0, SZ[:, :, :], ALU.add, ALU.mult).then_inc(dve_step, 1)
                dve.wait_ge(dve_step, step())
                TTo(Y, Y, SZ[:, :, :], ALU.mult).then_inc(dve_step, 1)
                dve.wait_ge(dve_step, step())
                head_norm(Y, 3, 256, 1.0 / 256, 4 * EPS, 4 * (l + 1), 0)
                TTo(Y, Y, over(RS[:, 0:3], 2, 256), ALU.mult).then_inc(dve_step, 1)
                dve.wait_ge(dve_step, step())
                TTo(SZ[:, :, :], Y, over(RP("ssm_norm"), 1, TT), ALU.mult).then_inc(sem["br_ready"], 1)

                dve.wait_ge(sem["brt_evac"], 6 * (l + 1))
                for name, k in (("nak", 1), ("nav", 1), ("dk", 1), ("dv", 1), ("C", 2), ("n", 2), ("ssm", 1)):
                    dve.wait_ge(st_dma[name], 16 * k * (l + 1))
                dve.memset(TMPB[:, 0, 0:1], 0.0).then_inc(sem["tokens_free"], 1)
                dve.wait_ge(sem["tokens_free"], l + 1)
                for dc in range(8):
                    dve.wait_ge(sem["bp_out"], 8 * l + dc + 1)
                    dve.wait_ge(gate_in[dc % 4], 16 * (2 * l + dc // 4 + 1))
                    b = 4 * (dc % 2)
                    STT(TMPB[:, 0:3, :], GT[dc % 4], 1.0, PS[:, b:b + 3, 0:T], ALU.add, ALU.mult)
                    STT(TMPB[:, 3, :], GATES[:, dc, :], 1.0, PS[:, b + 3, 0:T], ALU.add, ALU.mult).then_inc(sem["bp_evac"], 1)
                    dve.wait_ge(sem["bp_evac"], 8 * l + dc + 1)
                    TTo(TMPB[:, 0:2, :], TMPB[:, 0:2, :], TMPB[:, 2:4, :], ALU.add).then_inc(dve_step, 1)
                    dve.wait_ge(dve_step, step())
                    TTo(MIX[:, dc, :], TMPB[:, 0, :], TMPB[:, 1, :], ALU.add).then_inc(sem["mix_ready"], 1)
                    dve.wait_ge(sem["mix_ready"], 8 * l + dc + 1)
                for dc in range(8):
                    dve.wait_ge(sem["wo_out"], 8 * l + dc + 1)
                    for g, (a, b) in enumerate(segs):
                        ins = STT(xT[:, dc, a:b], PS[:, 2 + dc % 4, a:b], mod[:, 16 + dc, g:g + 1], xT[:, dc, a:b], ALU.mult, ALU.add)
                    ins.then_inc(sem["x1_ready"], 1)
                dve.wait_ge(sem["x1_ready"], 8 * (l + 1))
                modulated(1)

                dve.wait_ge(sem["rt_out"], l + 1)
                dve.tensor_reduce(RMX, PS[:, 7, 0:48].rearrange("p (a b) -> p a b", a=TT), AX.X, ALU.max, negate=True).then_inc(sem["rt_max"], 1)
                dve.wait_ge(sem["rt_exp"], l + 1)
                dve.reciprocal(RSUM, RSUM).then_inc(dve_step, 1)
                dve.wait_ge(dve_step, step())
                TTo(AFF, AFF, over(RSUM, 2, NE), ALU.mult).then_inc(sem["aff_ready"], 1)
                dve.wait_ge(sem["afT"], l + 1)
                dve.tensor_copy(AFT[0:NE, :], PS[0:NE, 6, 0:T])
                dve.tensor_copy(WK[0:NE, :], PS[0:NE, 6, 0:T]).then_inc(dve_step, 1)
                dve.wait_ge(dve_step, step())
                for (a, b), rounds in zip(segs, (2, 4)):
                    for _ in range(rounds):
                        dve.max(TOP[0:NE, :], WK[0:NE, a:b]).then_inc(dve_step, 1)
                        dve.wait_ge(dve_step, step())
                        dve.match_replace(WK[0:NE, a:b], TOP[0:NE, :], WK[0:NE, a:b], -1.0).then_inc(dve_step, 1)
                        dve.wait_ge(dve_step, step())
                TS(MSK[0:NE, :], WK[0:NE, :], 0.0, None, ALU.is_lt).then_inc(dve_step, 1)
                dve.wait_ge(dve_step, step())
                for a, b in segs:
                    ins = dve.tensor_tensor_scan(AFT[0:NE, a:b], MSK[0:NE, a:b], zeros[0:NE, :].broadcast_to([NE, b - a]), 0.0, ALU.add, ALU.add)
                ins.then_inc(dve_step, 1)
                dve.wait_ge(dve_step, step())
                TTo(WK[0:NE, :], AFT[0:NE, :], MSK[0:NE, :], ALU.mult).then_inc(sem["pos_ready"], 1)
                dve.wait_ge(sem["posT"], l + 1)
                TS(POS, PS[:, 7, 0:48].rearrange("p (a b) -> p a b", a=TT), -1.0, None, ALU.add).then_inc(dve_step, 1)
                dve.wait_ge(dve_step, step())
                for t in range(TT):
                    TTo(SEL[:, t, :, :], over(K("iota"), 1, NE), over(POS[:, t, :], 2, 32), ALU.is_equal).then_inc(dve_step, 1)
                    dve.wait_ge(dve_step, step())
                    ins = TTo(SELG[:, t, :, :], SEL[:, t, :, :], over(AFF[:, t, :], 2, 32), ALU.mult)
                ins.then_inc(sem["sel_ready"], 1)

                for e in range(NE):
                    g = l * NE + e
                    dve.wait_ge(sem["a_tanh"], g + 1)
                    if e == 0:
                        dve.wait_ge(sem["sgt_evac"], 3 * (l + 1))
                    if e >= 2:
                        dve.wait_ge(sem["ht_out"], g - 1)
                    STT(SA, TH, 1.0, PS[:, 2 * (e % 2), :], ALU.add, ALU.mult).then_inc(dve_step, 1)
                    dve.wait_ge(dve_step, step())
                    dve.wait_ge(sem["u_out"], g + 1)
                    TTo(HH[:, e % 2, :], SA, PS[:, 2 * (e % 2) + 1, :], ALU.mult).then_inc(sem["hh_ready"], 1)
                for dc in range(8):
                    dve.wait_ge(sem["cb_out"], 8 * l + dc + 1)
                    for g, (a, b) in enumerate(segs):
                        ins = STT(xT[:, dc, a:b], PS[:, dc % 4, a:b], mod[:, 40 + dc, g:g + 1], xT[:, dc, a:b], ALU.mult, ALU.add)
                    ins.then_inc(sem["x_ready"], 1)


_WEIGHTS = ["w_ada", "w_in", "w_branch", "w_out", "w_router", "w_gate", "w_up", "w_down"]
_PLAIN = ["x_prompt", "x_sample", "cache_na_k", "cache_na_v", "cache_diff_k", "cache_diff_v"] + _WEIGHTS
_OUTS = [(1, 128, 1024), (1, 256, 1024), (1, 2, 128, 4, 64), (1, 2, 128, 4, 64), (1, 2, 128, 4, 64), (1, 2, 128, 4, 64),
         (1, 2, 2, 4, 64, 64), (1, 2, 2, 4, 64), (1, 2, 2, 4), (1, 2, 2, 4, 64, 64)]


def laid_out(i):
    a = {k: np.asarray(v) for k, v in i.items()}
    f = np.float32
    rows = {"gate_b": a["mlstm_gate_b"].reshape(L, 16), "dt_bias": a["ssm_dt_bias"].reshape(L, 8), "a_log": a["ssm_a_log"].reshape(L, 8),
            "ssm_d": a["ssm_d"], "na_qn": a["na_qnorm_w"], "na_kn": a["na_knorm_w"], "diff_qn": a["diff_qnorm_w"],
            "diff_kn": a["diff_knorm_w"], "diff_norm": a["diff_norm_w"], "mlstm_norm": a["mlstm_norm_w"], "ssm_norm": a["ssm_norm_w"],
            "lambda": a["diff_lambda"].reshape(L, 128)}
    m0 = np.zeros((L, 2, 2, 32), f)
    m0[:, :, 0, 0:4] = a["state_mlstm_m"][0]
    rows["m0"] = m0.reshape(L, 128)
    rowp = np.zeros((L, NROW), f)
    for n, v in rows.items():
        rowp[:, ROW[n][0]:ROW[n][0] + ROW[n][1]] = v
    cols = {"norm1": a["norm1_w"].reshape(L, 8, 128), "norm2": a["norm2_w"].reshape(L, 8, 128), "b_ada": a["b_ada"].reshape(L, 48, 128),
            "conv_w": a["ssm_conv_w"].reshape(L, 5, 4, 128).transpose(0, 2, 1, 3).reshape(L, 20, 128),
            "conv_b": a["ssm_conv_b"].reshape(L, 4, 128), "m0": m0.reshape(L, 1, 128)}
    colp = np.zeros((L, 128, NCOL), f)
    for n, v in cols.items():
        colp[:, :, COL[n][0]:COL[n][0] + COL[n][1]] = v.transpose(0, 2, 1)
    cn = np.concatenate([a["state_mlstm_C"][0], a["state_mlstm_n"][0][..., None]], -1)
    cn = cn.reshape(L, 2, 2, 2, 64, 65).transpose(0, 3, 4, 2, 1, 5)
    c0n = np.zeros((L, 2, 64, 2, 2, 2, 65), f)
    for h in range(2):
        c0n[:, h, :, :, :, h] = cn[:, h]
    c0n = c0n.reshape(L, 128, 520)
    h0t = a["state_ssm"][0].reshape(L, 2, 2, 2, 64, 64).transpose(0, 2, 5, 1, 3, 4).reshape(L, 128, 256)
    cvec = np.stack([a["c_ctx"].reshape(8, 128), a["c"][0].reshape(8, 128)], -1).transpose(1, 0, 2).reshape(128, 16)
    rpb_rev = a["na_rpb"][:, :, :, ::-1].reshape(L * 4 * 15 * 31)
    return {"rowp": rowp, "colp": colp, "c0n": c0n, "h0t": h0t, "cvec": cvec, "rpb_rev": rpb_rev, "consts": constants()}


def kernel(**inputs):
    import concourse.bacc as _bacc
    from concourse.bass_utils import run_bass_kernel_spmd as _run

    nc = _bacc.Bacc("TRN2", target_bir_lowering=False, num_devices=1)
    arrays, dr = {}, {}
    given = {n: inputs[n] for n in _PLAIN}
    given.update(laid_out(inputs))
    for name, v in given.items():
        v = np.ascontiguousarray(v)
        arrays[f"in_{name}"] = v
        dr[name] = nc.dram_tensor(f"in_{name}", v.shape, F32, kind="ExternalInput").ap()
    outs = [nc.dram_tensor(f"out_{i}", shape, F32, kind="ExternalOutput").ap() for i, shape in enumerate(_OUTS)]
    trunk_program(nc, dr, outs)
    r = _run(nc, [arrays], core_ids=[0])
    return tuple(r.results[0][f"out_{i}"] for i in range(len(_OUTS)))
```

```python
import math
from contextlib import ExitStack

import numpy as np

import concourse.bass as bass
from concourse import mybir

F32 = mybir.dt.float32
F32R = mybir.dt.float32r
ALU = mybir.AluOpType
ACT = mybir.ActivationFunctionType
AX = mybir.AxisListType

D = 1024
KC = D // 128
L = 2
TT = 3
T = 128 * TT
NE = 16
IN_COLS = 7448
EPS = 1e-6
NEG = -1e30
RING = 4
SLOT = 4096

C_MQ, C_MV, C_MG, C_NQ, C_NV, C_DK, C_SZ, C_XBC, C_DT, C_GATE = 0, 512, 1024, 1040, 1552, 2064, 2576, 2832, 3344, 3352

ROW_WIDTHS = [("gate_b", 16), ("dt_bias", 8), ("a_log", 8), ("ssm_d", 4), ("na_qn", 64), ("na_kn", 64), ("diff_qn", 32),
              ("diff_kn", 32), ("diff_norm", 64), ("mlstm_norm", 256), ("ssm_norm", 256), ("lambda", 128), ("m0", 128)]
ROW, _at = {}, 0
for _n, _w in ROW_WIDTHS:
    ROW[_n] = (_at, _w)
    _at += _w
NROW = _at
COL_WIDTHS = [("norm1", 8), ("norm2", 8), ("b_ada", 48), ("conv_w", 20), ("conv_b", 4), ("m0", 1)]
COL, _at = {}, 0
for _n, _w in COL_WIDTHS:
    COL[_n] = (_at, _w)
    _at += _w
NCOL = _at
CST_WIDTHS = [("ident", 128), ("mask", 384), ("iota", 32), ("cos", 64), ("sin", 64), ("win", 64), ("adasel", 2),
              ("one", 1), ("eps", 1), ("mhalf", 1)]
CST, _at = {}, 0
for _n, _w in CST_WIDTHS:
    CST[_n] = (_at, _w)
    _at += _w
NCST = _at


SEEN = ((((0, 0),), ((1, 128),), ((1, 256), (2, 384))), (((0, 0),), ((1, 128), (2, 256)), ((2, 384),)))


def constants():
    c = np.zeros((128, NCST), np.float32)

    def put(name, v):
        o, w = CST[name]
        c[:, o:o + w] = v

    p = np.arange(128)[:, None]
    q = np.arange(128)[None, :]
    put("ident", np.eye(128))
    fwd = np.where(q >= p, 0.0, NEG)
    bwd = np.where(q <= p, 0.0, NEG)
    put("mask", np.concatenate([fwd, np.zeros((128, 128)), bwd], 1))
    put("iota", np.arange(32)[None, :])
    nf = 8
    inv = 10000.0 ** (-np.arange(nf, dtype=np.float32) / np.float32(nf))
    cos, sin = np.zeros((128, 2, 2, 2, nf)), np.zeros((128, 2, 2, 2, nf))
    for tile in range(2):
        t = tile * 128 + np.arange(128)
        for half, pos in enumerate((t // 64, t % 64)):
            ang = (pos.astype(np.float32)[:, None] * inv).astype(np.float32)
            for x12 in range(2):
                cos[:, tile, half, x12] = np.cos(ang)
                sin[:, tile, half, x12] = np.sin(ang) * (-1.0 if x12 == 0 else 1.0)
    put("cos", cos.reshape(128, 64))
    put("sin", sin.reshape(128, 64))
    qc = np.arange(128) % 64
    lo = np.clip(qc - 8, 0, 48)[:, None]
    kc = np.arange(64)[None, :]
    put("win", np.where((kc >= lo) & (kc < lo + 16), 0.0, NEG))
    sel = np.zeros((128, 2))
    for g in range(4):
        for r in range(2):
            sel[32 * g + r, r] = 1.0
    put("adasel", sel)
    put("one", 1.0)
    put("eps", EPS)
    put("mhalf", -0.5)
    return c


N_PROJ = 23
PROJ_TILES = ((C_MQ, 512, 4), (C_NQ, 512, 7), (C_XBC, 512, 11), (C_MV, 512, 14), (C_NV, 512, 17), (C_DK, 512, 20), (C_SZ, 256, 23))
JOBS, JOB_TILES = [], []
for _i in range(8):
    JOBS += [("part", _i), ("gate", 4 * _i), ("gate", 4 * _i + 1), ("sum", _i), ("gate", 4 * _i + 2), ("gate", 4 * _i + 3)]
    JOB_TILES += [("ada", _i, 6 * _i + 1), ("gate", _i, 6 * _i + 6)]
NJ = len(JOBS)
EARLY = 4
N_MIX = 7 + len(JOB_TILES) + 4
EXPERT_SLOTS = (3, 1, 2, 0)
LANDING, _count = {}, [0] * RING


def _place(key, slot):
    _count[slot] += 1
    LANDING[key] = (slot, 16 * _count[slot])


for _i in range(EARLY):
    _place(("first", 0, _i), _i)
for _l in range(L):
    for _i in range(N_MIX + (EARLY if _l < L - 1 else 0)):
        _place(("mix", _l, _i), _i % 3)
    for _i in range(6 * NE):
        _place(("expert", _l, _i), EXPERT_SLOTS[_i % 4])

Q_GATE, Q_BRANCH, Q_OUT, NQ = 26, 58, 66, 74
FEATURE_MAJOR = (True, False, True, False, False, False, False)


def quarter_end(l, q):
    if q < Q_GATE:
        i, c = q // 4, q % 4
        before = PROJ_TILES[i - 1][2] if i else 0
        if FEATURE_MAJOR[i]:
            return "proj_out", N_PROJ * l + before + c + 1
        if c == (1 if i == 6 else 3):
            return "proj_out", N_PROJ * l + before + 3
        return "part_out", 13 * l + 3 * sum(not f for f in FEATURE_MAJOR[:i]) + c + 1
    if q < Q_BRANCH:
        return "job_out", NJ * l + JOBS.index(("gate", q - Q_GATE)) + 1
    if q < Q_OUT:
        return "bp_out", 8 * l + q - Q_BRANCH + 1
    return "wo_out", 8 * l + q - Q_OUT + 1


def splits_ahead():
    ahead, q = [], Q_GATE + 4
    for j in range(NJ):
        for _ in range(2):
            if q < Q_BRANCH:
                m = [t[:2] for t in JOB_TILES].index(("gate", (q - Q_GATE) // 4))
                free = j + 1 >= JOB_TILES[m - 3][2]
            else:
                free = q < Q_BRANCH + 4
            if free and JOBS.index(("gate", q - Q_GATE - 4)) <= j:
                q += 1
        ahead.append(q)
    return ahead


AHEAD = splits_ahead()
COMBINED = {_e: (2 * (_e - 5), 2 * (_e - 5) + 1) for _e in range(5, 13)}
COMBINED.update({13: (16, 17, 18), 14: (19, 20, 21), 15: (22, 23)})
SPILLED = 24
SEMS = ["ada_part", "ada_evac", "ada_sel", "proj_out", "proj_evac", "gpre_out", "xT_out", "xT_evac", "c_ready",
        "sq_ready", "ss_ready", "rms_ready", "h_ready", "bm_loaded", "ctx_loaded", "gact_in", "gact_e", "gact_out",
        "gtm_ready", "growT", "rows_ready", "tmT", "tm_evac", "tm_ready", "tm_exp", "m_out", "pool_in", "pool_out",
        "conv_ready", "silu_t", "xs_ready", "xtr_out", "xtr_evac", "nan_ready", "ntr_out", "ntr_evac", "dfn_ready",
        "dtr_out", "dtr_evac", "s_out", "s_read", "p_exp", "pt_out", "pt_evac", "o_out", "o_evac", "ds_out", "d_max",
        "d_exp", "d_ready", "dpt_out", "dpt_evac", "do_out", "do_evac", "job_out", "job_evac", "hx_ready",
        "ada_taken", "row_out", "e_ready", "e_exp", "pm_ready", "sT_out", "num_out", "num_evac", "kt_out",
        "kw_ready", "st_out", "st_evac", "tokens_free", "tanh_out", "brt_out", "brt_evac", "br_ready", "bp_out",
        "bp_evac", "mix_ready", "wo_out", "x1_ready", "rt_out", "rt_max", "rt_exp", "aff_ready", "afT", "pos_ready",
        "posT", "sel_ready", "selg_ready", "h2t_out", "h2t_evac", "h2t_lo", "sgt_out", "sgt_evac", "hi_ready",
        "lo_ready", "part_out", "x_stored", "x_back", "hl_ready", "hl_odd", "wsm_hi", "wsm_lo", "gpre_raw",
        "gpre_sb", "rt_raw", "rt_sb", "mixl_ready", "brt_lo", "xh_ready", "xf_out", "xf_evac", "xg_out", "xg_evac",
        "a_out", "u_out", "a_tanh", "hh_ready", "ht_out", "ht_evac", "yd_out", "yd_evac", "cb_out", "early_out",
        "early_taken", "x_ready", "yt_out", "yt_evac"]


def trunk_program(nc, dr, outs):
    (y_prompt, y_sample, new_na_k, new_na_v, new_diff_k, new_diff_v, new_C, new_n, new_m, new_ssm) = outs
    with ExitStack() as ctx:
        def sb(name, shape):
            return ctx.enter_context(nc.sbuf_tensor(name, shape, F32))

        sem = {n: ctx.enter_context(nc.semaphore(n)) for n in SEMS}
        landed = [ctx.enter_context(nc.semaphore(f"landed{i}")) for i in range(RING)]
        par_in = [ctx.enter_context(nc.semaphore(f"par_in{i}")) for i in range(3)]
        dve_step = ctx.enter_context(nc.semaphore("dve_step"))
        st_dma = {n: ctx.enter_context(nc.semaphore("st_" + n)) for n in ("nak", "nav", "dk", "dv", "C", "n", "m", "ssm", "y")}

        spilled = [ctx.enter_context(nc.semaphore(f"spilled{i}")) for i in range(8)]
        gate_in = [ctx.enter_context(nc.semaphore(f"gate_in{i}")) for i in range(4)]
        x_store = nc.dram_tensor("x_store", (L, 128, KC * T), F32, kind="Internal").ap()
        spill = nc.dram_tensor("gates_spill", (L, 8, 128, 3, T), F32, kind="Internal").ap()

        PS = ctx.enter_context(nc.psum_tensor("banks", [128, 8, 512], F32))
        as_fp32r = {}

        def sb_split(name, shape):
            with nc.sbuf_tensor(name + "_fp32r", shape, F32R) as twin:
                pass
            v = sb(name, shape)
            as_fp32r[name] = twin
            return v

        def rounded(v):
            return bass.AP(as_fp32r[v.tensor.name], v.offset, v.ap)

        ring = sb_split("ring", [128, RING, SLOT])
        wsm = sb_split("wsm", [128, KC, 24])
        wrt = sb("wrt", [128, KC, NE])
        xT = sb_split("xT", [128, KC, T])
        hT = sb_split("hT", [128, KC, T])
        cst = sb("cst", [128, NCST])
        rowp = sb("rowp", [128, NROW])
        colp = sb("colp", [128, NCOL])
        c32 = sb("c32", [128, KC, 32])
        mod = sb("mod", [128, 48, 2])
        amp = sb("amp", [128, 2, 8, 2])
        small = sb("small", [128, 536])
        WORK = 27500
        work = sb_split("work", [128, WORK])

        def K(name):
            o, w = CST[name]
            return cst[:, o:o + w]

        def RP(name):
            o, w = ROW[name]
            return rowp[:, o:o + w]

        def CP(name):
            o, w = COL[name]
            return colp[:, o:o + w]

        def region(base, end):
            at = [base]

            def take(shape):
                n = int(np.prod(shape))
                v = work[:, at[0]:at[0] + n]
                at[0] += n
                assert at[0] <= end, (at[0], end)
                if len(shape) == 1:
                    return v
                names = "abcd"[:len(shape)]
                spec = f"p ({' '.join(names)}) -> p {' '.join(names)}"
                return v.rearrange(spec, **{k: d for k, d in zip(names[1:], shape[1:])})
            take.at = at
            return take

        t = region(0, WORK)
        V1 = t([TT, 4, 65])
        MO = t([TT, 256])
        NAQK = t([TT, 512])
        base_nv = t.at[0]
        NV = t([TT, 256])
        DV = t([TT, 256])
        DQK = t([TT, 512])
        SZ = t([TT, 256])
        end_u = t.at[0]
        base_qk = t.at[0]
        QKT = t([4, T])
        XS = t([4, T])
        base_ctx = t.at[0]
        KRAW = t([2, 256])
        KCT = t([4, 128])
        VC = t([2, 256])
        end_ctx = t.at[0] + 24
        t.at[0] = end_ctx
        base_cw = t.at[0]
        XB = t([4, 392])
        CV = t([4, 392])
        end_cw = t.at[0]
        base_pr = t.at[0]
        BM = t([2, 4, 256])
        PTS = t([2, 384])
        NAT = t([4, T])
        end_pr = t.at[0]
        ED = t([4, 384])
        EDf = ED.rearrange("p a b -> p (a b)")
        XTM = t([TT, 256])
        C0 = t([2, 2, 130])
        H0 = t([256])
        ROWS = t([3, T])
        TM = t([3, T])
        KW = ROWS[:, 1:3, :].rearrange("p a b -> p (a b)")[:, 0:512].rearrange("p (a b c) -> p a b c", a=2, b=4)
        BTM = ROWS[:, 1:3, :].rearrange("p a b -> p (a b)")[:, 512:640]
        base_gates = t.at[0]
        GATES = t([8, T])
        end_mix = t.at[0]
        r = region(base_nv, base_nv + 2 * 768)
        XDT = r([2, TT, 4, 64])
        r = region(base_ctx, end_ctx)
        NUM = r([2 * TT, 4, 65])
        r = region(base_cw, end_cw)
        W1 = r([1536])
        W2 = r([1536])
        WX = work[:, base_cw:base_cw + 2304]
        r = region(base_pr, end_pr)
        PM = r([8, 512])
        r = region(base_pr, end_pr)
        BRT = r([8, T])
        r = region(end_pr, end_pr + 8 * T + 8)
        BRTL = r([8, T])
        r = region(0, end_u)
        r.at[0] = 0
        MIX = r([8, T])
        TMPB = r([4, T])
        GT = [WX[:, 0:1152], WX[:, 1152:2304], r([1152]), r([1152])]
        GT = [v.rearrange("p (a b) -> p a b", a=3) for v in GT]
        RSTD = W2[:, 0:T]
        QF = QKT.rearrange("p a b -> p (a b)")
        CN_OUT = QF[:, 0:520].rearrange("p (a b c) -> p a b c", a=2, b=4)
        SS_OUT = QF[:, 520:1032].rearrange("p (a b) -> p a b", a=8)
        MPE = GATES[:, 0:3, :].rearrange("p a b -> p (a b)")[:, 0:1024].rearrange("p (a b) -> p a b", a=2)
        WSMH = GATES[:, 0:1, :].rearrange("p a b -> p (a b)")[:, 0:192].rearrange("p (a b) -> p a b", a=KC)
        GRAW = GATES[:, 1, :]
        RRAW = GATES[:, 4, :]
        XF = GATES[:, 5:8, :].rearrange("p a b -> p (a b)")[:, 0:1024].rearrange("p (a b) -> p a b", a=2)
        HH_IN = xT
        MIXH = work[:, base_qk:base_qk + KC * T].rearrange("p (a b) -> p a b", a=KC)

        def MPL(i):
            return KRAW if i < 2 else NAQK[:, 1:3, 256:512]

        m = region(0, WORK)
        XG = m([KC, NE, 2, 32])
        YS = m([4, D])
        YP = m([4, D])
        SGT = m([4, 256])
        SGP = m([4, 128])
        HH = m([2, 512])
        HTT = m([2, 4, 128])
        TH = m([512])
        SA = m([512])
        H2MH = work[:, m.at[0]:m.at[0] + TT * D].rearrange("p (a b) -> p a b", a=TT)
        assert m.at[0] + TT * D <= base_gates
        m2 = region(KC * NE * 64, KC * NE * 64 + 2 * 4 * D)
        H2M = m2([TT, D])
        SEL = m2([TT, NE, 32])
        SELG = m2([TT, NE, 32])
        POS = m2([TT, NE])
        AFF = m2([TT, NE])
        AFT = m2([T])
        WK = m2([T])
        MSK = m2([T])
        XIN = work[:, 0:TT * D].rearrange("p (a b) -> p a b", a=TT)
        YOUT = work[:, 0:TT * D].rearrange("p (a b) -> p a b", a=TT)

        sm = [0]

        def st(shape):
            n = int(np.prod(shape))
            v = small[:, sm[0]:sm[0] + n]
            sm[0] += n
            assert sm[0] <= 536, sm[0]
            if len(shape) == 1:
                return v
            names = "abcd"[:len(shape)]
            return v.rearrange(f"p ({' '.join(names)}) -> p {' '.join(names)}", **{k: d for k, d in zip(names[1:], shape[1:])})

        G1 = st([TT, 24])
        GA = st([TT, 24])
        GL = st([TT, 24])
        DTM = st([TT, 8])
        AEXP = st([8])
        WS = st([16])
        EMT = st([TT, 8])
        SS = st([TT * 24])
        RS = st([TT * 24])
        NM0 = st([1])
        MOUT = st([2])
        LAM = st([8])
        SMX = st([2, 2])
        SSUM = st([2, 2])
        SREC = st([2, 2])
        DMX = st([2, 2])
        DSUM = st([2, 2])
        DREC = st([2, 2])
        WPT = st([TT, 16])
        RMX = st([TT])
        RSUM = st([TT])
        TOP = st([8])

        ident = K("ident")
        zeros = K("iota")[:, 0:1]
        ones = K("one").broadcast_to([128, 128])

        def over(ap, axis, n):
            v = ap.unsqueeze(axis)
            shape = list(v.shape)
            shape[axis] = n
            return v.broadcast_to(shape)

        block = ctx.enter_context(nc.Block())

        def quarter(q):
            def tile_of(i, width):
                return ring[:, i % 3, 0:SLOT if width != 256 else SLOT // 2].rearrange("p (k n) -> p k n", n=width)

            hi = ring[:, 3, 1024 * (q % 4):1024 * (q % 4) + 1024]
            if q < Q_GATE:
                i, c = q // 4, q % 4
                w = tile_of(i, PROJ_TILES[i][1])
                if FEATURE_MAJOR[i]:
                    return [(w[:, :, c * 128:(c + 1) * 128], hi.rearrange("p (k n) -> p k n", n=128))]
                n = KC // 2 if i == 6 else KC // 4
                return [(w[:, n * c:n * c + n, :], hi.rearrange("p (k n) -> p k n", k=n))]
            if Q_BRANCH <= q < Q_OUT:
                dc = q - Q_BRANCH
                return [(tile_of(23 + i, 1024)[:, :, dc * 128:(dc + 1) * 128],
                         hi[:, 512 * i:512 * i + 512].rearrange("p (k n) -> p k n", n=128)) for i in range(2)]
            if q < Q_BRANCH:
                i, c = (q - Q_GATE) // 4, (q - Q_GATE) % 4
                at = 7 + [t_[:2] for t_ in JOB_TILES].index(("gate", i))
            else:
                at, c = 25 + (q - Q_OUT) // 4, (q - Q_OUT) % 4
            return [(tile_of(at, 512)[:, :, c * 128:(c + 1) * 128], hi.rearrange("p (k n) -> p k n", n=128))]

        def tiles_begun(q):
            if q < Q_GATE:
                return [q // 4] if q % 4 == 0 else []
            if q == Q_BRANCH:
                return [23, 24]
            if Q_BRANCH < q < Q_OUT or (q - Q_GATE) % 4:
                return []
            if q < Q_BRANCH:
                return [7 + [t_[:2] for t_ in JOB_TILES].index(("gate", (q - Q_GATE) // 4))]
            return [25 + (q - Q_OUT) // 4]

        @block.sync
        def _(sp):
            def load(key, w, c0=0, width=512):
                slot = LANDING[key][0]
                rows = w.shape[0] // 128
                dst = ring[:, slot, 0:rows * width].rearrange("p (k n) -> p k n", n=width)
                sp.dma_start(dst, w[:, c0:c0 + width].rearrange("(k p) n -> p k n", p=128)).then_inc(landed[slot], 16)

            def load_pair(l, m, w):
                for half in range(2):
                    load(("expert", l, m + half), w, 512 * half)

            def load_parameters(l):
                sp.dma_start(rowp[:, :], dr["rowp"][l:l + 1, :].broadcast_to([128, NROW])).then_inc(par_in[1], 16)
                sp.dma_start(colp[:, :], dr["colp"][l]).then_inc(par_in[1], 16)
                sp.dma_start(wsm[:, :, 0:16], dr["w_in"][l, :, C_MG:C_MG + 16].rearrange("(k p) n -> p k n", p=128)).then_inc(par_in[1], 16)
                sp.dma_start(wsm[:, :, 16:24], dr["w_in"][l, :, C_DT:C_DT + 8].rearrange("(k p) n -> p k n", p=128)).then_inc(par_in[1], 16)
                sp.dma_start(wrt[:, :, :], dr["w_router"][l].rearrange("(k p) n -> p k n", p=128)).then_inc(par_in[1], 16)

            sp.wait_ge(par_in[2], 16)
            load(("first", 0, 0), dr["w_ada"][0], 0)
            load_parameters(0)
            load(("first", 0, 1), dr["w_ada"][0], 512)
            for i in range(2, EARLY):
                load(("first", 0, i), dr["w_ada"][0], 512 * i)
            sp.wait_ge(sem["xT_evac"], 6)
            sp.dma_start(x_store[0], xT[:, :, :].rearrange("p a b -> p (a b)")).then_inc(sem["x_stored"], 16)
            for l in range(L):
                e0 = NE * l
                for i in range(3):
                    if l == 0:
                        sp.wait_ge(sem["ada_part"], i + 1)
                    elif i == 0:
                        sp.wait_ge(sem["yd_out"], e0)
                    load(("mix", l, i), dr["w_in"][l], PROJ_TILES[i][0])
                if l:
                    sp.wait_ge(sem["x_ready"], 8 * l)
                    sp.dma_start(x_store[l], xT[:, :, :].rearrange("p a b -> p (a b)")).then_inc(sem["x_stored"], 16)
                sp.dma_start(KRAW[:, 0, :], dr["cache_na_k"][0, l].rearrange("t h d -> t (h d)")).then_inc(sem["ctx_loaded"], 16)
                sp.dma_start(KRAW[:, 1, :], dr["cache_diff_k"][0, l].rearrange("t h d -> t (h d)")).then_inc(sem["ctx_loaded"], 16)
                sp.dma_start(VC[:, 0, :], dr["cache_na_v"][0, l].rearrange("t h d -> t (h d)")).then_inc(sem["ctx_loaded"], 16)
                sp.dma_start(VC[:, 1, :], dr["cache_diff_v"][0, l].rearrange("t h d -> t (h d)")).then_inc(sem["ctx_loaded"], 16)
                sp.dma_start(C0[:, :, :, :], dr["c0n"][l].rearrange("p (a b c) -> p a b c", a=2, b=2)).then_inc(sem["ctx_loaded"], 16)
                sp.dma_start(H0[:, :], dr["h0t"][l]).then_inc(sem["ctx_loaded"], 16)
                for h in range(4):
                    for qr in range(4):
                        off = l * 4 * 465 + h * 465 + (7 - qr) * 31 - 48
                        src = bass.AP(dr["rpb_rev"].tensor, off, [[1, 64], [31, 4], [1, 64]])
                        dst = BM[64 * (qr % 2):64 * (qr % 2) + 64, qr // 2, h, :].rearrange("p (a b) -> p a b", a=4)
                        sp.dma_start(dst, src).then_inc(sem["bm_loaded"], 16)
                for i in range(3, 7):
                    sp.wait_ge(sem["proj_out"], N_PROJ * l + PROJ_TILES[i - 3][2])
                    load(("mix", l, i), dr["w_in"][l], PROJ_TILES[i][0], PROJ_TILES[i][1])
                for i, (kind, k, _) in enumerate(JOB_TILES):
                    if i < 3:
                        sp.wait_ge(sem["proj_out"], N_PROJ * l + PROJ_TILES[i + 4][2])
                    else:
                        sp.wait_ge(sem["job_out"], NJ * l + JOB_TILES[i - 3][2])
                    if kind == "ada":
                        load(("mix", l, 7 + i), dr["w_ada"][l], 512 * (EARLY + k))
                    else:
                        load(("mix", l, 7 + i), dr["w_in"][l], C_GATE + 512 * k)
                for i in range(2):
                    sp.wait_ge(sem["job_out"], NJ * l + JOB_TILES[i - 3][2])
                    load(("mix", l, 23 + i), dr["w_branch"][l, 2 * i:2 * i + 2].rearrange("b c d -> (b c) d"), 0, 1024)
                sp.wait_ge(sem["job_out"], NJ * (l + 1))
                sp.dma_start(xT[:, :, :].rearrange("p a b -> p (a b)"), x_store[l]).then_inc(sem["x_back"], 16)
                load(("mix", l, 25), dr["w_out"][l], 0)
                sp.wait_ge(sem["bp_out"], 8 * (l + 1))
                load(("mix", l, 26), dr["w_out"][l], 512)
                if l < L - 1:
                    load(("mix", l, 27), dr["w_ada"][l + 1], 0)
                    sp.wait_ge(sem["wo_out"], 8 * l + 4)
                    load(("mix", l, 28), dr["w_ada"][l + 1], 512)
                    sp.wait_ge(sem["wo_out"], 8 * (l + 1))
                    load(("mix", l, 29), dr["w_ada"][l + 1], 1024)
                    load(("expert", l, 0), dr["w_gate"][l, 0], 0)
                    sp.wait_ge(sem["rt_raw"], l + 1)
                    load_parameters(l + 1)
                    sp.wait_ge(sem["ada_part"], EARLY * (l + 1) + 1)
                    load(("mix", l, 30), dr["w_ada"][l + 1], 1536)
                    sp.wait_ge(sem["ada_part"], EARLY * (l + 1) + 2)
                    load(("expert", l, 1), dr["w_gate"][l, 0], 512)
                    sp.wait_ge(sem["ada_part"], EARLY * (l + 1) + 3)
                    load(("expert", l, 2), dr["w_up"][l, 0], 0)
                    sp.wait_ge(sem["ada_part"], EARLY * (l + 2))
                    load(("expert", l, 3), dr["w_up"][l, 0], 512)
                else:
                    sp.wait_ge(sem["wo_out"], 8 * (l + 1))
                    load_pair(l, 0, dr["w_gate"][l, 0])
                    load_pair(l, 2, dr["w_up"][l, 0])
                for e in range(1, NE):
                    if e == 1:
                        sp.wait_ge(sem["a_out"], e0 + 1)
                    else:
                        sp.wait_ge(sem["yd_out"], e0 + e - 1)
                    load_pair(l, 6 * e - 2, dr["w_gate"][l, e])
                    sp.wait_ge(sem["u_out"], e0 + e)
                    load_pair(l, 6 * e, dr["w_down"][l, e - 1])
                    sp.wait_ge(sem["a_out"], e0 + e + 1)
                    load_pair(l, 6 * e + 2, dr["w_up"][l, e])
                sp.wait_ge(sem["yd_out"], e0 + NE - 1)
                load_pair(l, 6 * NE - 2, dr["w_down"][l, NE - 1])
            for g in range(6):
                h, t = g // 3, g % 3
                dst = y_prompt[0] if t == 0 else y_sample[0, 128 * (t - 1):128 * t, :]
                sp.wait_ge(sem["yt_evac"], g + 1)
                sp.dma_start(dst[:, 512 * h:512 * h + 512], YOUT[:, t, 512 * h:512 * h + 512]).then_inc(st_dma["y"], 16)
            sp.wait_ge(st_dma["y"], 16 * 6)

        @block.gpsimd
        def _(pool):
            for l in range(L):
                def low_parts(until):
                    while low[0] < until:
                        q = low[0]
                        low[0] += 1
                        pool.wait_ge(sem["hi_ready"], NQ * l + q + 1)
                        for w, hi in quarter(q):
                            ins = pool.tensor_tensor(rounded(w), w, rounded(hi), ALU.subtract)
                        ins.then_inc(sem["lo_ready"], 1)

                low = [0]
                if l:
                    low_parts(1)
                for k in range(0, KC, 2):
                    pool.wait_ge(sem["xh_ready"], 8 * l + k + 1)
                    pool.tensor_tensor(rounded(hT[:, k, :]), hT[:, k, :], rounded(HH_IN[:, k, :]), ALU.subtract).then_inc(sem["hl_ready"], 1)
                low_parts(Q_GATE + 4)

                def power(i, n):
                    pool.wait_ge(sem["pool_in"], 4 * l + i + 1)
                    pool.tensor_tensor(RS[:, 0:n], SS[:, 0:n], K("mhalf").broadcast_to([128, n]), ALU.pow).then_inc(sem["pool_out"], 1)

                power(0, 72)
                pool.wait_ge(sem["nan_ready"], l + 1)
                pool.dma_start(new_na_k[0, l].rearrange("t h d -> t (h d)"), NAQK[:, 0, 256:512]).then_inc(st_dma["nak"], 16)
                pool.wait_ge(sem["proj_evac"], l * N_PROJ + 23)
                pool.dma_start(new_na_v[0, l].rearrange("t h d -> t (h d)"), NV[:, 0, :]).then_inc(st_dma["nav"], 16)
                pool.dma_start(new_diff_v[0, l].rearrange("t h d -> t (h d)"), DV[:, 0, :]).then_inc(st_dma["dv"], 16)
                pool.wait_ge(sem["dfn_ready"], l + 1)
                pool.dma_start(new_diff_k[0, l].rearrange("t h d -> t (h d)"), DQK[:, 0, 256:512]).then_inc(st_dma["dk"], 16)
                pool.wait_ge(sem["m_out"], l + 1)
                pool.dma_start(new_m[0, l, 0].rearrange("(h a) -> h a", a=1), MOUT[0:4, 0:1]).then_inc(st_dma["m"], 16)
                pool.dma_start(new_m[0, l, 1].rearrange("(h a) -> h a", a=1), MOUT[64:68, 1:2]).then_inc(st_dma["m"], 16)
                low_parts(AHEAD[29])
                power(1, 12)
                low_parts(AHEAD[39])
                power(2, 12)
                pool.wait_ge(sem["st_evac"], 3 * l + 2)
                for d in range(2):
                    pool.dma_start(new_C[0, l, d].rearrange("h d e -> d h e"), CN_OUT[0:64, d, :, 0:64]).then_inc(st_dma["C"], 16)
                    pool.dma_start(new_n[0, l, d].rearrange("h (d a) -> d h a", a=1), CN_OUT[0:64, d, :, 64:65], allow_slow_non_contiguous=True).then_inc(st_dma["n"], 16)
                low_parts(Q_BRANCH)
                power(3, 3)
                pool.wait_ge(sem["st_evac"], 3 * l + 3)
                pool.dma_start(new_ssm[0, l].rearrange("d h p n -> p (d h) n"), SS_OUT[0:64, :, :]).then_inc(st_dma["ssm"], 16)
                low_parts(Q_BRANCH + 4)
                for dc in range(8):
                    low_parts(Q_BRANCH + 5 + dc)
                    pool.wait_ge(sem["mix_ready"], 8 * l + dc + 1)
                    pool.tensor_tensor(rounded(MIX[:, dc, :]), MIX[:, dc, :], rounded(MIXH[:, dc, :]), ALU.subtract).then_inc(sem["mixl_ready"], 1)
                low_parts(NQ)
                for g in range(6):
                    t, half = g // 2, g % 2
                    pool.wait_ge(sem["h2t_evac"], 6 * l + g + 1)
                    h2 = H2M[:, t, 512 * half:512 * half + 512]
                    pool.tensor_tensor(rounded(h2), h2, rounded(H2MH[:, t, 512 * half:512 * half + 512]), ALU.subtract)\
                        .then_inc(sem["h2t_lo"], 1)
            for n, k in (("nak", 1), ("nav", 1), ("dk", 1), ("dv", 1), ("C", 2), ("n", 2), ("m", 2), ("ssm", 1)):
                pool.wait_ge(st_dma[n], 16 * k * L)

        @block.tensor
        def _(pe):
            def tile(key):
                slot, v = LANDING[key]
                pe.wait_ge(landed[slot], v)
                return ring[:, slot, :].rearrange("p (a b) -> p a b", b=512)

            def three_passes(dst, w, x, first, last):
                for i, (a, b) in enumerate(((0, 0), (0, 1), (1, 0))):
                    a_, b_ = rounded(w[a]), rounded(x[b])
                    mm = pe.matmul(dst, a_, b_, start=(first and i == 0), stop=(last and i == 2))
                return mm

            def ada_partial(bank, w):
                for k in range(KC):
                    g = k % 4
                    mm = pe.matmul(PS[32 * g:32 * g + 32, bank, :], c32[:, k, :], w[:, k, :], start=(k < 4), stop=(k >= 4),
                                   tile_position=(0, 32 * g))
                return mm

            def ada_sum(bank, partial):
                for j in range(4):
                    mm = pe.matmul(PS[:, bank, 2 * j:2 * j + 2], partial[:, j // 2, 128 * (j % 2):128 * (j % 2) + 128], K("adasel"), start=True, stop=True)
                return mm

            def ada_early(layer, i, keys):
                for j in range(i, i + 2):
                    w = tile(keys[j - i])
                    if i:
                        pe.wait_ge(sem["ada_taken"], EARLY * layer + j - 1)
                    ada_partial(j % 2, w).then_inc(sem["ada_part"], 1)
                for j in range(i, i + 2):
                    pe.wait_ge(sem["ada_evac"], EARLY * layer + j + 1)
                    ada_sum(j % 2, MPE[:, j % 2, :].rearrange("p (a b) -> p a b", a=2)).then_inc(sem["ada_sel"], 1)

            def sum_squares(layer, which, k):
                pe.wait_ge(sem["sq_ready"], 16 * layer + 8 * which + k + 1)
                mm = pe.matmul(PS[:, 6, 0:T], ones, hT[:, k, :], start=(k == 0), stop=(k == KC - 1))
                if k == KC - 1:
                    mm.then_inc(sem["ss_ready"], 1)

            pe.wait_ge(par_in[0], 16 * 3)
            for g in range(6):
                t, h = g // 2, g % 2
                for c in range(4):
                    mm = pe.transpose(PS[:, g, c * 128:(c + 1) * 128], XIN[:, t, (4 * h + c) * 128:(4 * h + c + 1) * 128], ident)
                mm.then_inc(sem["xT_out"], 1)
            for k in range(KC):
                sum_squares(0, 0, k)
            pe.wait_ge(sem["xT_evac"], 6)
            pe.wait_ge(sem["c_ready"], 1)
            for i in (0, 2):
                ada_early(0, i, [("first", 0, i), ("first", 0, i + 1)])
            for l in range(L):
                def h_in(k, a=0, b=T):
                    return HH_IN[:, k, a:b], hT[:, k, a:b]

                pe.wait_ge(sem["wsm_lo"], l + 1)
                for k in range(KC):
                    pe.wait_ge(sem["hl_odd" if k % 2 else "hl_ready"], 4 * l + k // 2 + 1)
                    mm = three_passes(PS[0:24, 7, 0:T], (WSMH[:, k, :], wsm[:, k, :]), h_in(k), k == 0, k == KC - 1)
                mm.then_inc(sem["gpre_raw"], 1)

                banks, po, quarters = (0, 1, 2, 3, 7), [0], [0]

                def out_bank():
                    j = po[0]
                    po[0] += 1
                    if j >= 5:
                        pe.wait_ge(sem["proj_evac"], l * N_PROJ + j - 4)
                    if j == 4:
                        pe.wait_ge(sem["gact_in"], l + 1)
                    return banks[j % 5]

                def next_quarter():
                    q = quarters[0]
                    quarters[0] += 1
                    pe.wait_ge(sem["lo_ready"], NQ * l + q + 1)
                    return [(hi, w) for w, hi in quarter(q)]

                def feature_major():
                    for c in range(4):
                        b = out_bank()
                        hi, lo_ = next_quarter()[0]
                        for k in range(KC):
                            mm = three_passes(PS[:, b, 0:T], (hi[:, k, :], lo_[:, k, :]), h_in(k), k == 0, k == KC - 1)
                        mm.then_inc(sem["proj_out"], 1)

                def token_major(width=512, parts=4):
                    b = [out_bank() for _ in range(TT)]
                    n = KC // parts
                    for c in range(parts):
                        hi, lo_ = next_quarter()[0]
                        for i in range(n):
                            k = n * c + i
                            for t in range(TT):
                                mm = three_passes(PS[:, b[t], 0:width], h_in(k, t * 128, (t + 1) * 128), (hi[:, i, :], lo_[:, i, :]),
                                                  k == 0, k == KC - 1)
                                if k == KC - 1:
                                    mm.then_inc(sem["proj_out"], 1)
                        if c < parts - 1:
                            mm.then_inc(sem["part_out"], 1)

                def turn3(bank, src, width=128):
                    for t in range(TT):
                        mm = pe.transpose(PS[:, bank, t * 128:(t + 1) * 128], src(t), ident)
                    return mm

                feature_major()
                pe.wait_ge(sem["gpre_sb"], l + 1)
                for t in range(TT):
                    mm = pe.transpose(PS[:, 7, 24 * t:24 * t + 24], GRAW[0:24, t * 128:(t + 1) * 128], ident[0:24, 0:24])
                mm.then_inc(sem["gpre_out"], 1)
                token_major()
                feature_major()
                token_major()
                pe.wait_ge(sem["gtm_ready"], l + 1)
                turn3(4, lambda t: TM[:, 0, t * 128:(t + 1) * 128])
                turn3(5, lambda t: TM[:, 1, t * 128:(t + 1) * 128]).then_inc(sem["growT"], 1)
                token_major()
                pe.wait_ge(sem["rows_ready"], l + 1)
                for i in range(3):
                    mm = turn3(4 + i, lambda t: ROWS[:, i, t * 128:(t + 1) * 128])
                mm.then_inc(sem["tmT"], 1)
                token_major()
                token_major(256, 2)

                pe.wait_ge(sem["ctx_loaded"], 96 * (l + 1))
                pe.wait_ge(sem["tm_evac"], l + 1)
                for c in range(4):
                    mm = pe.transpose(PS[:, 6, c * 128:(c + 1) * 128], KRAW[:, c // 2, (c % 2) * 128:(c % 2) * 128 + 128], ident)
                mm.then_inc(sem["ntr_out"], 1)

                jobs = [0]

                def job():
                    j = jobs[0]
                    jobs[0] += 1
                    kind, i = JOBS[j]
                    if j >= 2:
                        pe.wait_ge(sem["job_evac"], NJ * l + j - 1)
                    else:
                        pe.wait_ge(sem["proj_evac"], N_PROJ * (l + 1))
                    if kind == "sum":
                        mm = ada_sum(j % 2, MPL(i))
                    elif kind == "part":
                        mm = ada_partial(j % 2, tile(("mix", l, 7 + [t_[:2] for t_ in JOB_TILES].index(("ada", i)))))
                    else:
                        hi, lo_ = next_quarter()[0]
                        for k in range(KC):
                            mm = three_passes(PS[:, j % 2, 0:T], (hi[:, k, :], lo_[:, k, :]), h_in(k), k == 0, k == KC - 1)
                    mm.then_inc(sem["job_out"], 1)

                job()
                job()

                pe.wait_ge(sem["xs_ready"], l + 1)
                for t in range(TT):
                    for c in range(2):
                        o = 256 * (t % 2) + 128 * c
                        pe.transpose(PS[:, 4 + t // 2, o:o + 128], XS[:, c, t * 128:(t + 1) * 128], ident)
                pe.transpose(PS[:, 5, 256:384], XS[:, 2, 0:128], ident).then_inc(sem["xtr_out"], 1)

                for _ in range(6):
                    job()
                pe.wait_ge(sem["nan_ready"], l + 1)
                pe.wait_ge(sem["xtr_evac"], l + 1)
                for t, b in ((0, 7), (1, 4), (2, 5)):
                    for c in range(4):
                        mm = pe.transpose(PS[:, b, c * 128:(c + 1) * 128], NAQK[:, t, c * 128:(c + 1) * 128], ident)
                    mm.then_inc(sem["ntr_out"], 1)
                units = [("p", 0), ("p", 1)] + [(t, h) for t in (1, 2) for h in range(4)]

                def na_scores(u):
                    if u >= 2:
                        pe.wait_ge(sem["s_read"], 10 * l + u - 1)
                    else:
                        pe.wait_ge(sem["proj_evac"], (l + 1) * N_PROJ)
                        pe.wait_ge(sem["ntr_evac"], 4 * (l + 1))
                    t, h = units[u]
                    b = 2 + u % 2
                    if t == "p":
                        lo = 64 * h
                        for c in range(2):
                            mm = pe.matmul(PS[:, b, c * 128:(c + 1) * 128], NAT[lo:lo + 64, c, 0:128], NAT[lo:lo + 64, 2 + c, 0:128], start=True, stop=True)
                    else:
                        lo, c = 64 * (h % 2), h // 2
                        q = NAT[lo:lo + 64, c, t * 128:(t + 1) * 128]
                        pe.matmul(PS[:, b, 0:256], q, NAT[lo:lo + 64, 2 + c, 128:384], start=True, stop=True)
                        mm = pe.matmul(PS[:, b, 256:384], q, KCT[lo:lo + 64, c, :], start=True, stop=True)
                    mm.then_inc(sem["s_out"], 1)

                def na_turn(u):
                    pe.wait_ge(sem["p_exp"], 10 * l + u + 1)
                    if u >= 2:
                        pe.wait_ge(sem["pt_evac"], 10 * l + u - 1)
                    for c in range(2 if units[u][0] == "p" else 3):
                        mm = pe.transpose(PS[:, 4 + u % 2, c * 128:(c + 1) * 128], ED[:, u % 2, c * 128:(c + 1) * 128], ident)
                    mm.then_inc(sem["pt_out"], 1)

                def na_out(u):
                    pe.wait_ge(sem["pt_evac"], 10 * l + u + 1)
                    if u >= 2:
                        pe.wait_ge(sem["o_evac"], 10 * l + u - 1)
                    t, h = units[u]
                    b = 6 + u % 2
                    if t == "p":
                        for c in range(2):
                            hh = 2 * c + h
                            mm = pe.matmul(PS[:, b, c * 64:c * 64 + 64], PTS[:, u % 2, c * 128:(c + 1) * 128], NV[:, 0, hh * 64:hh * 64 + 64], start=True, stop=True)
                    else:
                        vs = [NV[:, 1, h * 64:h * 64 + 64], NV[:, 2, h * 64:h * 64 + 64], VC[:, 0, h * 64:h * 64 + 64]]
                        for c in range(3):
                            mm = pe.matmul(PS[:, b, 0:64], PTS[:, u % 2, c * 128:(c + 1) * 128], vs[c], start=(c == 0), stop=(c == 2))
                    mm.then_inc(sem["o_out"], 1)

                for i in range(12):
                    if i < 10:
                        job()
                        na_scores(i)
                    if 1 <= i <= 10:
                        na_turn(i - 1)
                    if i >= 2:
                        na_out(i - 2)

                pe.wait_ge(sem["dfn_ready"], l + 1)
                pe.wait_ge(sem["s_read"], 10 * (l + 1))
                for t in range(TT):
                    for c in range(4):
                        mm = pe.transpose(PS[:, 2 + t, c * 128:(c + 1) * 128], DQK[:, t, c * 128:(c + 1) * 128], ident)
                    mm.then_inc(sem["dtr_out"], 1)
                dunits = [(t, h) for t in range(TT) for h in range(4)]

                def df_scores(u):
                    t, h = dunits[u]
                    if u >= 2:
                        pe.wait_ge(sem["d_exp"], 12 * l + u - 1)
                    else:
                        pe.wait_ge(sem["dtr_evac"], 3 * (l + 1))
                    for mp in range(2):
                        b = 2 + 2 * (u % 2) + mp
                        lo, c = 32 * ((2 * h + mp) % 4), (2 * h + mp) // 4
                        q = NAT[lo:lo + 32, c, t * 128:(t + 1) * 128]
                        if t == 0:
                            mm = pe.matmul(PS[:, b, 0:128], q, NAT[lo:lo + 32, 2 + c, 0:128], start=True, stop=True, tile_position=(lo, 0))
                        else:
                            pe.matmul(PS[:, b, 0:256], q, NAT[lo:lo + 32, 2 + c, 128:384], start=True, stop=True, tile_position=(lo, 0))
                            mm = pe.matmul(PS[:, b, 256:384], q, KCT[lo:lo + 32, 2 + c, :], start=True, stop=True, tile_position=(lo, 0))
                    mm.then_inc(sem["ds_out"], 1)

                def df_turn(u):
                    pe.wait_ge(sem["d_ready"], 12 * l + u + 1)
                    if u:
                        pe.wait_ge(sem["dpt_evac"], 12 * l + u)
                    else:
                        pe.wait_ge(sem["o_evac"], 10 * (l + 1))
                    for c in range(1 if dunits[u][0] == 0 else 3):
                        mm = pe.transpose(PS[:, 6, c * 128:(c + 1) * 128], ED[:, 2 * (u % 2), c * 128:(c + 1) * 128], ident)
                    mm.then_inc(sem["dpt_out"], 1)

                def df_out(u):
                    pe.wait_ge(sem["dpt_evac"], 12 * l + u + 1)
                    if u:
                        pe.wait_ge(sem["do_evac"], 12 * l + u)
                    t, h = dunits[u]
                    vs = [DV[:, 0, h * 64:h * 64 + 64]] if t == 0 else [DV[:, 1, h * 64:h * 64 + 64], DV[:, 2, h * 64:h * 64 + 64], VC[:, 1, h * 64:h * 64 + 64]]
                    for c, v in enumerate(vs):
                        mm = pe.matmul(PS[:, 7, 0:64], PTS[:, u % 2, c * 128:(c + 1) * 128], v, start=(c == 0), stop=(c == len(vs) - 1))
                    mm.then_inc(sem["do_out"], 1)

                for i in range(14):
                    if i < 12:
                        df_scores(i)
                        job()
                    if 1 <= i <= 12:
                        df_turn(i - 1)
                    if i >= 2:
                        df_out(i - 2)

                def scan_scores(kT, qT):
                    pe.matmul(PS[:, 2, 0:128], kT(0), qT(0, 1), start=True, stop=True)
                    pe.matmul(PS[:, 2, 128:384], kT(1), qT(1, 3), start=True, stop=True)
                    pe.matmul(PS[:, 3, 0:256], kT(2), qT(1, 3), start=True, stop=True).then_inc(sem["sT_out"], 1)

                def decay_row(kind, c):
                    h, d = c // 2, c % 2
                    if c >= 4:
                        pe.wait_ge(sem["e_ready"], 16 * l + 8 * kind + c - 3)
                    r = 32 * kind + 64 * d + h
                    pe.matmul(PS[:, 4 + c % 4, 0:T], ident[:, r:r + 1].broadcast_to([128, 128]), ROWS[:, 0, :], start=True, stop=True)\
                        .then_inc(sem["row_out"], 1)

                pe.wait_ge(sem["d_exp"], 12 * (l + 1))
                pe.wait_ge(sem["do_evac"], 12 * (l + 1))
                for c in range(8):
                    decay_row(0, c)
                    if c % 2 == 0:
                        h = c // 2
                        lo, ch = 64 * (h % 2), h // 2
                        if c:
                            job()
                            pe.wait_ge(sem["pm_ready"], 16 * l + c)
                        scan_scores(lambda s_: QKT[lo:lo + 64, 2 + ch, s_ * 128:(s_ + 1) * 128],
                                    lambda a, b: QKT[lo:lo + 64, ch, a * 128:b * 128])
                    if c % 2 or c == 0:
                        job()

                def over_keys(dst, pairs, v):
                    for i, (d, ks, off) in enumerate(pairs):
                        mm = pe.matmul(dst, PM[:, 2 * h + d, off:off + 128], v(d, ks), start=(i == 0), stop=(i == len(pairs) - 1))
                    return mm

                pe.wait_ge(sem["pm_ready"], 16 * l + 8)
                for i, (t, d, b, bq) in enumerate(((0, 0, 2, None), (0, 1, 3, None), (1, 0, 4, 5), (1, 1, 6, 7), (2, 0, 2, 3), (2, 1, 4, 5))):
                    if i >= 4:
                        pe.wait_ge(sem["num_evac"], 9 * l + i - 2)
                    for h in range(4):
                        mm = over_keys(PS[:, b, 65 * h:65 * h + 65], [(d, ks, off) for ks, off in SEEN[d][t]], lambda _, ks: V1[:, ks, h, :])
                    if bq is not None:
                        for ch in range(2):
                            mm = pe.matmul(PS[:, bq, 130 * ch:130 * ch + 130], QKT[:, ch, t * 128:(t + 1) * 128], C0[:, ch, d, :], start=True, stop=True)
                    mm.then_inc(sem["num_out"], 1)
                pe.wait_ge(sem["num_evac"], 9 * l + 4)
                for c in range(2):
                    mm = pe.transpose(PS[:, 6, c * 128:(c + 1) * 128], QKT[:, 2 + c, 0:128], ident)
                mm.then_inc(sem["kt_out"], 1)
                job()
                pe.wait_ge(sem["kw_ready"], 2 * l + 1)
                pe.wait_ge(sem["num_evac"], 9 * l + 5)
                for d in range(2):
                    for h in range(4):
                        mm = pe.matmul(PS[0:64, 7 if d == 0 else 2, 65 * h:65 * h + 65], KW[:, d, h, :], V1[:, 0, h, :], start=True, stop=True)
                mm.then_inc(sem["st_out"], 1)

                job()
                pe.wait_ge(sem["st_evac"], 3 * l + 2)
                pe.wait_ge(sem["num_evac"], 9 * l + 6)
                for c in range(8):
                    decay_row(1, c)
                    if c % 4 == 0:
                        lo = 64 * (c // 4)
                        if c:
                            job()
                            pe.wait_ge(sem["pm_ready"], 16 * l + 8 + c)
                        scan_scores(lambda s_: XS[lo:lo + 64, 2, s_ * 128:(s_ + 1) * 128],
                                    lambda a, b: XS[lo:lo + 64, 3, a * 128:b * 128])
                    if c >= 2 and c != 4:
                        job()
                pe.wait_ge(sem["pm_ready"], 16 * l + 16)
                for t, b, bq in ((0, 2, None), (1, 3, (4, 5)), (2, 6, (7, 2))):
                    for h in range(4):
                        mm = over_keys(PS[:, b, 64 * h:64 * h + 64], [(d, ks, off) for d in range(2) for ks, off in SEEN[d][t]],
                                       lambda d, ks: XDT[:, d, ks, h, :])
                    if bq is not None:
                        for g in range(2):
                            if t == 2 and g == 1:
                                pe.wait_ge(sem["num_evac"], 9 * l + 7)
                            mm = pe.matmul(PS[:, bq[g], 0:256], XS[64 * g:64 * g + 64, 3, t * 128:(t + 1) * 128], H0[64 * g:64 * g + 64, :], start=True, stop=True)
                    mm.then_inc(sem["num_out"], 1)
                job()
                pe.wait_ge(sem["kw_ready"], 2 * l + 2)
                pe.wait_ge(sem["num_evac"], 9 * l + 8)
                for d in range(2):
                    for h in range(4):
                        c = 4 * d + h
                        mm = pe.matmul(PS[0:64, 3, 64 * c:64 * c + 64], KW[:, d, h, :], BTM[:, 64 * (h // 2):64 * (h // 2) + 64], start=True, stop=True)
                mm.then_inc(sem["st_out"], 1)

                job()

                pe.wait_ge(sem["br_ready"], l + 1)
                pe.wait_ge(sem["st_evac"], 3 * (l + 1))
                pe.wait_ge(sem["num_evac"], 9 * (l + 1))
                for g in range(6):
                    t, half = g // 2, g % 2
                    srcs = (MO, NAQK) if half == 0 else (DQK, SZ)
                    for c in range(4):
                        mm = pe.transpose(PS[:, 2 + g, c * 128:(c + 1) * 128], srcs[c // 2][:, t, (c % 2) * 128:(c % 2) * 128 + 128], ident)
                    mm.then_inc(sem["brt_out"], 1)
                pe.wait_ge(sem["brt_evac"], 6 * (l + 1))
                pe.wait_ge(sem["brt_lo"], 6 * (l + 1))
                pe.wait_ge(sem["job_evac"], NJ * (l + 1))
                for dc in range(8):
                    if dc >= 2:
                        pe.wait_ge(sem["bp_evac"], 8 * l + dc - 1)
                    w = next_quarter()
                    for nb in range(4):
                        hi, lo_ = w[nb // 2]
                        for k in range(2):
                            kk = 2 * (nb % 2) + k
                            mm = three_passes(PS[:, 4 * (dc % 2) + nb, 0:T], (hi[:, kk, :], lo_[:, kk, :]),
                                              (BRT[:, 2 * nb + k, :], BRTL[:, 2 * nb + k, :]), k == 0, k == 1)
                    mm.then_inc(sem["bp_out"], 1)
                for dcs in ((0, 1), (2,), (3,), (4,), (5,), (6,), (7,)):
                    w = {dc: next_quarter()[0] for dc in dcs}
                    if dcs[0] in (0, 2):
                        pe.wait_ge(sem["bp_evac"], 8 * l + 7 + dcs[0] // 2)
                    if dcs[0] >= 4:
                        pe.wait_ge(sem["x1_ready"], 8 * l + dcs[0] - 3)
                    for k in range(KC):
                        if dcs[0] == 0:
                            pe.wait_ge(sem["mixl_ready"], 8 * l + k + 1)
                        for dc in dcs:
                            hi, lo_ = w[dc]
                            mm = three_passes(PS[:, 2 + dc % 4, 0:T], (hi[:, k, :], lo_[:, k, :]), (MIXH[:, k, :], MIX[:, k, :]), k == 0, k == KC - 1)
                            if k == KC - 1:
                                mm.then_inc(sem["wo_out"], 1)
                    if dcs[0] >= 2:
                        sum_squares(l, 1, dcs[0] - 2)
                sum_squares(l, 1, KC - 2)
                sum_squares(l, 1, KC - 1)
                if l < L - 1:
                    ada_early(l + 1, 0, [("mix", l, 27), ("mix", l, 28)])

                for k in range(KC):
                    pe.wait_ge(sem["h_ready"], 16 * l + 8 + k + 1)
                    mm = pe.matmul(PS[0:NE, 7, 0:T], wrt[:, k, :], hT[:, k, :], start=(k == 0), stop=(k == KC - 1))
                mm.then_inc(sem["rt_raw"], 1)
                pe.wait_ge(sem["x1_ready"], 8 * (l + 1))
                for g in range(6):
                    t, half = g // 2, g % 2
                    for c in range(4):
                        mm = pe.transpose(PS[:, g, c * 128:(c + 1) * 128], hT[:, 4 * half + c, t * 128:(t + 1) * 128], ident)
                    mm.then_inc(sem["h2t_out"], 1)
                    if g == 0:
                        pe.wait_ge(sem["rt_sb"], l + 1)
                        for t_ in range(TT):
                            mm = pe.transpose(PS[:, 7, 16 * t_:16 * t_ + 16], RRAW[0:NE, t_ * 128:(t_ + 1) * 128], ident[0:NE, 0:NE])
                        mm.then_inc(sem["rt_out"], 1)
                pe.wait_ge(sem["aff_ready"], l + 1)
                for t in range(TT):
                    mm = pe.transpose(PS[0:NE, 6, t * 128:(t + 1) * 128], AFF[:, t, :], ident)
                mm.then_inc(sem["afT"], 1)
                if l < L - 1:
                    pe.wait_ge(sem["h2t_evac"], 6 * (l + 1))
                    ada_early(l + 1, 2, [("mix", l, 29), ("mix", l, 30)])
                pe.wait_ge(sem["pos_ready"], l + 1)
                for t in range(TT):
                    mm = pe.transpose(PS[:, 7, 16 * t:16 * t + 16], WK[0:NE, t * 128:(t + 1) * 128], ident[0:NE, 0:NE])
                mm.then_inc(sem["posT"], 1)

                pe.wait_ge(sem["sel_ready"], 3 * (l + 1))
                pe.wait_ge(sem["h2t_lo"], 6 * (l + 1))
                pe.wait_ge(sem["h2t_evac"], 6 * (l + 1))
                if l < L - 1:
                    pe.wait_ge(sem["ada_taken"], EARLY * (l + 2))
                def gather(dst, q, a, b):
                    ts = (1, 2) if q % 2 == 0 else (0,)
                    for i, t in enumerate(ts):
                        for j, part in enumerate((H2MH, H2M)):
                            mm = pe.matmul(dst, rounded(part[:, t, 128 * (q // 2):128 * (q // 2) + 128]),
                                           rounded(SEL[:, t, a:b, :].rearrange("p a b -> p (a b)")),
                                           start=(i == 0 and j == 0), stop=(i == len(ts) - 1 and j == 1))
                    return mm

                for half in range(2):
                    for grp, ts in enumerate(((1, 2), (0,))):
                        for i, t in enumerate(ts):
                            for j, part in enumerate((H2MH, H2M)):
                                mm = pe.matmul(PS[0:64, 2 * grp + half, :], rounded(SEL[:, t, 0:2, :].rearrange("p a b -> p (a b)")),
                                               rounded(part[:, t, 512 * half:512 * half + 512]),
                                               start=(i == 0 and j == 0), stop=(i == len(ts) - 1 and j == 1))
                    mm.then_inc(sem["xf_out"], 1)
                for half in range(2):
                    pe.wait_ge(sem["xf_evac"], 2 * l + half + 1)
                    for c in range(4):
                        mm = pe.transpose(PS[:, half, 128 * c:128 * c + 128], XF[:, half, 128 * c:128 * c + 128], ident)
                    mm.then_inc(sem["xg_out"], 1)

                def pair_tiles(i):
                    return tile(("expert", l, i)), tile(("expert", l, i + 1))

                def project(dst, w2, x):
                    for k in range(KC):
                        for hf in range(2):
                            mm = pe.matmul(dst[64 * hf:64 * hf + 64, :], x(k), w2[hf][:, k, :], start=(k == 0), stop=(k == KC - 1),
                                           tile_position=(0, 64 * hf))
                    return mm

                def expert_a(e):
                    g = l * NE + e
                    if e >= 2:
                        pe.wait_ge(sem["hh_ready"], g - 1)
                    project(PS[:, 2 * (e % 2), :], pair_tiles(0 if e == 0 else 6 * e - 2),
                            lambda k: XG[:, k, e, :, :].rearrange("p a b -> p (a b)")).then_inc(sem["a_out"], 1)

                def expert_u(e):
                    project(PS[:, 2 * (e % 2) + 1, :], pair_tiles(2 if e == 0 else 6 * e + 2),
                            lambda k: XG[:, k, e, :, :].rearrange("p a b -> p (a b)")).then_inc(sem["u_out"], 1)

                def expert_down(e):
                    g = l * NE + e
                    pe.wait_ge(sem["hh_ready"], g + 1)
                    if e:
                        pe.wait_ge(sem["ht_evac"], g)
                    for c in range(4):
                        mm = pe.transpose(PS[:, 4, c * 128:(c + 1) * 128], HH[:, e % 2, c * 128:(c + 1) * 128], ident)
                    mm.then_inc(sem["ht_out"], 1)
                    pe.wait_ge(sem["ht_evac"], g + 1)
                    if e >= 2:
                        pe.wait_ge(sem["yd_evac"], g - 1)
                    project(PS[:, 5 + e % 2, :], pair_tiles(6 * e + 6 if e < NE - 1 else 6 * e + 4),
                            lambda k: HTT[:, e % 2, k % 4, 64 * (k // 4):64 * (k // 4) + 64]).then_inc(sem["yd_out"], 1)

                def combine(bank, n):
                    eb, dc = n // 8, n % 8
                    pe.wait_ge(sem["yd_evac"], NE * l + 4 * eb + 4)
                    pe.matmul(PS[:, bank, 0:128], YP[:, eb, dc * 128:(dc + 1) * 128], SGP[:, eb, :], start=True, stop=True)
                    return pe.matmul(PS[:, bank, 128:384], YS[:, eb, dc * 128:(dc + 1) * 128], SGT[:, eb, :], start=True, stop=True)

                def combine_early(n):
                    if n:
                        pe.wait_ge(sem["early_taken"], 24 * l + n)
                    combine(7, n).then_inc(sem["early_out"], 1)

                pe.wait_ge(sem["xg_evac"], 18 * l + 2)
                expert_a(0)
                expert_u(0)
                for q in range(16):
                    if q >= 4:
                        pe.wait_ge(sem["xg_evac"], 18 * l + 2 + q - 3)
                    gather(PS[:, 4 + q % 4, 0:448], q, 2, NE).then_inc(sem["xg_out"], 1)
                pe.wait_ge(sem["xg_evac"], 18 * (l + 1))
                pe.wait_ge(sem["selg_ready"], l + 1)
                for i in range(3):
                    for j in range(4):
                        if i < 2:
                            eb, t = 2 * i + j // 2, 1 + j % 2
                        else:
                            eb, t = j, 0
                        mm = pe.transpose(PS[:, 4 + i, j * 128:(j + 1) * 128], SELG[:, t, 4 * eb:4 * eb + 4, :].rearrange("p a b -> p (a b)"), ident)
                    mm.then_inc(sem["sgt_out"], 1)
                for e in range(1, NE):
                    units = COMBINED.get(e, ())
                    expert_a(e)
                    if units:
                        combine_early(units[0])
                    if e == 1:
                        pe.wait_ge(sem["sgt_evac"], 3 * (l + 1))
                    expert_down(e - 1)
                    if units:
                        combine_early(units[1])
                    expert_u(e)
                    if len(units) > 2:
                        combine_early(units[2])
                expert_down(NE - 1)

                for dc in range(8):
                    if dc >= 4:
                        pe.wait_ge(sem["x_ready"], 8 * l + dc - 3)
                    mm = combine(dc % 4, 24 + dc)
                    mm.then_inc(sem["cb_out"], 1)
                    if dc >= 2 and l < L - 1:
                        sum_squares(l + 1, 0, dc - 2)
                if l < L - 1:
                    sum_squares(l + 1, 0, KC - 2)
                    sum_squares(l + 1, 0, KC - 1)
            for g in range(6):
                h, t = g // 3, g % 3
                pe.wait_ge(sem["x_ready"], 8 * (L - 1) + 4 * (h + 1))
                for c in range(4):
                    mm = pe.transpose(PS[:, (4, 5, 7, 0, 1, 2)[g], c * 128:(c + 1) * 128], xT[:, 4 * h + c, t * 128:(t + 1) * 128], ident)
                mm.then_inc(sem["yt_out"], 1)

        @block.scalar
        def _(act):
            def copy(dst, src, scale=1.0):
                return act.activation(dst, src, ACT.Copy, scale=scale)

            act.dma_start(small[:, 0:16], dr["cvec"]).then_inc(par_in[2], 16)
            act.dma_start(cst[:, :], dr["consts"]).then_inc(par_in[0], 16)
            act.dma_start(XIN[:, 0, :], dr["x_prompt"][0]).then_inc(par_in[0], 16)
            act.dma_start(XIN[:, 1:3, :], dr["x_sample"][0].rearrange("(t p) d -> p t d", p=128)).then_inc(par_in[0], 16)
            act.wait_ge(par_in[2], 16)
            act.activation(small[:, 16:32], small[:, 0:16], ACT.Tanh, scale=0.5).then_inc(sem["tanh_out"], 1)
            for g in range(6):
                t, h = g // 2, g % 2
                act.wait_ge(sem["xT_out"], g + 1)
                ins = copy(xT[:, 4 * h:4 * h + 4, t * 128:(t + 1) * 128], PS[:, g, :].rearrange("p (a b) -> p a b", a=4))
                ins.then_inc(sem["xT_evac"], 1)
            act.wait_ge(sem["xT_evac"], 6)

            def squares(k):
                act.activation(hT[:, k, :], xT[:, k, :], ACT.Square).then_inc(sem["sq_ready"], 1)

            def root(layer, which):
                act.wait_ge(sem["ss_ready"], 2 * layer + which + 1)
                act.activation(RSTD, PS[:, 6, 0:T], ACT.Sqrt, scale=1.0 / D, bias=K("eps")).then_inc(sem["rms_ready"], 1)

            def modulate(layer, which):
                for k in range(KC):
                    act.wait_ge(sem["hx_ready"], 16 * layer + 8 * which + k + 1)
                    for g, (a, b) in enumerate(((0, 128), (128, 384))):
                        ins = act.activation(hT[:, k, a:b], hT[:, k, a:b], ACT.Identity, scale=amp[:, which, k, g:g + 1],
                                             bias=mod[:, 24 * which + k, g:g + 1])
                    ins.then_inc(sem["h_ready"], 1)

            def ada_early(layer, i):
                for j in range(i, i + 2):
                    act.wait_ge(sem["ada_part"], EARLY * layer + j + 1)
                    copy(MPE[:, j % 2, :], PS[:, j % 2, :]).then_inc(sem["ada_evac"], 1)
                for j in range(i, i + 2):
                    act.wait_ge(sem["ada_sel"], EARLY * layer + j + 1)
                    copy(mod[:, 4 * j:4 * j + 4, :], PS[:, j % 2, 0:8].rearrange("p (a b) -> p a b", a=4)).then_inc(sem["ada_taken"], 1)

            for k in range(KC):
                squares(k)
            root(0, 0)
            ada_early(0, 0)
            ada_early(0, 2)
            for l in range(L):
                split = [0]

                def high_parts(until):
                    while split[0] < until:
                        q = split[0]
                        split[0] += 1
                        for i in tiles_begun(q):
                            slot, v = LANDING[("mix", l, i)]
                            act.wait_ge(landed[slot], v)
                        if q >= 4:
                            name, v = quarter_end(l, q - 4)
                            act.wait_ge(sem[name], v)
                        elif l:
                            act.wait_ge(sem["yd_out"], NE * l)
                        else:
                            act.wait_ge(sem["ada_part"], EARLY)
                        for w, hi in quarter(q):
                            ins = copy(rounded(hi), w)
                        ins.then_inc(sem["hi_ready"], 1)

                act.wait_ge(par_in[1], 80 * (l + 1))
                copy(rounded(WSMH), wsm[:, :, :]).then_inc(sem["wsm_hi"], 1)
                if l:
                    high_parts(1)
                modulate(l, 0)
                high_parts(4)

                j = [0]

                def proj(dsts):
                    j[0] += 1
                    act.wait_ge(sem["proj_out"], l * N_PROJ + j[0])
                    b = (0, 1, 2, 3, 7)[(j[0] - 1) % 5]
                    for i, (dst, lo, hi, scale) in enumerate(dsts):
                        src = PS[:, b, lo:hi]
                        if len(dst.shape) == 3:
                            src = src.rearrange("p (a b) -> p a b", a=dst.shape[1])
                        ins = copy(dst, src, scale)
                    ins.then_inc(sem["proj_evac"], 1)

                def proj_tokens(i, dsts):
                    before, after = {5: (Q_GATE, Q_GATE + 2), 6: (Q_GATE + 2, Q_GATE + 4)}.get(i, (4 * i + 7, 4 * i + 8))
                    high_parts(before)
                    for t in range(TT):
                        proj(dsts(t))
                    high_parts(after)

                for c in range(4):
                    proj([(QKT[:, c, :], 0, T, 1.0 if c < 2 else 0.125)])
                    high_parts(5 + c)
                proj_tokens(1, lambda t: [(NAQK[:, t, :], 0, 512, 1.0)])
                act.wait_ge(sem["gact_in"], l + 1)
                act.activation(GL, GA, ACT.Exp, scale=-1.0).then_inc(sem["gact_e"], 1)
                act.wait_ge(sem["gact_e"], l + 1)
                act.activation(GL, GL, ACT.Ln, bias=1.0)
                act.activation(AEXP, RP("a_log"), ACT.Exp).then_inc(sem["gact_out"], 1)
                for c in range(4):
                    proj([(XB[:, c, 2:130], 0, 128, 1.0), (XB[:, c, 134:390], 128, T, 1.0)])
                    high_parts(13 + c)
                proj_tokens(3, lambda t: [(V1[:, t, :, 0:64], 0, 256, 1.0), (MO[:, t, :], 256, 512, 1.0)])
                proj_tokens(4, lambda t: [(NV[:, t, :], 0, 256, 1.0), (DQK[:, t, 0:256], 256, 512, 1.0)])
                act.wait_ge(sem["tmT"], l + 1)
                for i in range(3):
                    ins = copy(TM[:, i, :], PS[:, 4 + i, 0:T])
                ins.then_inc(sem["tm_evac"], 1)
                proj_tokens(5, lambda t: [(DQK[:, t, 256:512], 0, 256, 1.0), (DV[:, t, :], 256, 512, 1.0)])
                proj_tokens(6, lambda t: [(SZ[:, t, :], 0, 256, 1.0)])
                act.wait_ge(sem["tm_ready"], l + 1)
                act.activation(WPT, WPT, ACT.Exp)
                act.activation(EMT, EMT, ACT.Exp)
                act.activation(LAM[:, 0:2], LAM[:, 0:2], ACT.Exp).then_inc(sem["tm_exp"], 1)
                act.wait_ge(sem["ntr_out"], 4 * l + 1)
                copy(KCT, PS[:, 6, :].rearrange("p (a b) -> p a b", a=4)).then_inc(sem["ntr_evac"], 1)
                act.wait_ge(sem["conv_ready"], l + 1)
                for c in range(4):
                    ins = act.activation(XS[:, c, 0:128], CV[:, c, 2:130], ACT.Tanh, scale=0.5)
                    ins = act.activation(XS[:, c, 128:384], CV[:, c, 134:390], ACT.Tanh, scale=0.5)
                ins.then_inc(sem["silu_t"], 1)
                act.wait_ge(sem["xtr_out"], l + 1)
                copy(XTM[:, 0:2, :], PS[:, 4, :].rearrange("p (a b) -> p a b", a=2))
                copy(XTM[:, 2, :], PS[:, 5, 0:256])
                copy(BTM, PS[:, 5, 256:384]).then_inc(sem["xtr_evac"], 1)

                jobs = [0]

                def take_job():
                    j = jobs[0]
                    jobs[0] += 1
                    kind, i = JOBS[j]
                    act.wait_ge(sem["job_out"], NJ * l + j + 1)
                    if kind == "part":
                        ins = copy(MPL(i), PS[:, j % 2, :].rearrange("p (a b) -> p a b", a=2))
                    elif kind == "sum":
                        ins = copy(mod[:, 4 * (EARLY + i):4 * (EARLY + i) + 4, :], PS[:, j % 2, 0:8].rearrange("p (a b) -> p a b", a=4))
                    else:
                        if 8 <= i:
                            act.wait_ge(spilled[i % 8], 16 * (SPILLED // 8 * l + i // 8))
                        ins = act.activation(GATES[:, i % 8, :], PS[:, j % 2, 0:T], ACT.Tanh, scale=0.5)
                    ins.then_inc(sem["job_evac"], 1)
                    if j and JOBS[j - 1][0] == "gate" and JOBS[j - 1][1] < SPILLED:
                        g = JOBS[j - 1][1]
                        act.wait_ge(sem["job_evac"], NJ * l + j)
                        act.dma_start(spill[l, g % 8, :, g // 8, :], GATES[:, g % 8, :]).then_inc(spilled[g % 8], 16)
                    high_parts(AHEAD[j])

                for _ in range(8):
                    take_job()
                for i, b in enumerate((7, 4, 5)):
                    act.wait_ge(sem["ntr_out"], 4 * l + i + 2)
                    copy(NAT[:, :, i * 128:(i + 1) * 128], PS[:, b, :].rearrange("p (a b) -> p a b", a=4)).then_inc(sem["ntr_evac"], 1)

                def na_exp(u):
                    act.wait_ge(sem["s_read"], 10 * l + u + 1)
                    if u < 2:
                        for c in range(2):
                            ins = act.activation(ED[:, u, c * 128:(c + 1) * 128], ED[:, 2 + u, c * 128:(c + 1) * 128], ACT.Exp,
                                                 bias=SMX[:, u, c:c + 1], accum_out=SSUM[:, u, c:c + 1])
                    else:
                        ins = act.activation(ED[:, u % 2, :], ED[:, 2 + u % 2, :], ACT.Exp, bias=SMX[:, u % 2, 0:1], accum_out=SSUM[:, u % 2, 0:1])
                    ins.then_inc(sem["p_exp"], 1)

                def na_turned(u):
                    act.wait_ge(sem["pt_out"], 10 * l + u + 1)
                    w = 256 if u < 2 else 384
                    copy(PTS[:, u % 2, 0:w], PS[:, 4 + u % 2, 0:w]).then_inc(sem["pt_evac"], 1)

                for i in range(11):
                    if i < 10:
                        if i >= 2:
                            act.wait_ge(sem["o_evac"], 10 * l + i - 1)
                        na_exp(i)
                        take_job()
                    if i >= 1:
                        na_turned(i - 1)
                for t in range(TT):
                    act.wait_ge(sem["dtr_out"], 3 * l + t + 1)
                    copy(NAT[:, :, t * 128:(t + 1) * 128], PS[:, 2 + t, :].rearrange("p (a b) -> p a b", a=4)).then_inc(sem["dtr_evac"], 1)

                def df_exp(u):
                    act.wait_ge(sem["d_max"], 12 * l + u + 1)
                    w = 128 if u < 4 else 384
                    for mp in range(2):
                        ins = act.activation(ED[:, 2 * (u % 2) + mp, 0:w], PS[:, 2 + 2 * (u % 2) + mp, 0:w], ACT.Exp,
                                             scale=32 ** -0.5, bias=DMX[:, u % 2, mp:mp + 1], accum_out=DSUM[:, u % 2, mp:mp + 1])
                    ins.then_inc(sem["d_exp"], 1)

                def df_turned(u):
                    act.wait_ge(sem["dpt_out"], 12 * l + u + 1)
                    w = 128 if u < 4 else 384
                    copy(PTS[:, u % 2, 0:w], PS[:, 6, 0:w]).then_inc(sem["dpt_evac"], 1)

                for i in range(13):
                    if i < 12:
                        df_exp(i)
                        take_job()
                    if i >= 1:
                        df_turned(i - 1)

                def combos(kind):
                    for c in range(8):
                        act.wait_ge(sem["e_ready"], 16 * l + 8 * kind + c + 1)
                        i = c % 2
                        act.activation(EDf[:, 512 * i:512 * i + 512], EDf[:, 512 * i:512 * i + 512], ACT.Exp).then_inc(sem["e_exp"], 1)
                        if kind == 0 or c >= 2:
                            take_job()

                combos(0)
                act.activation(W1[:, 0:768].rearrange("p (a b) -> p a b", a=TT), MO[:, :, :], ACT.Tanh, scale=0.5)
                act.activation(W1[:, 768:1536].rearrange("p (a b) -> p a b", a=TT), SZ[:, :, :], ACT.Tanh, scale=0.5).then_inc(sem["tanh_out"], 1)
                take_job()
                act.wait_ge(sem["st_out"], 2 * l + 1)
                for d in range(2):
                    copy(CN_OUT[0:64, d, :, :], PS[0:64, 7 if d == 0 else 2, 0:260].rearrange("p (a b) -> p a b", a=4)).then_inc(sem["st_evac"], 1)
                take_job()
                combos(1)
                take_job()
                act.wait_ge(sem["st_out"], 2 * l + 2)
                copy(SS_OUT[0:64, :, :], PS[0:64, 3, :].rearrange("p (a b) -> p a b", a=8)).then_inc(sem["st_evac"], 1)
                take_job()
                for g in range(6):
                    t, half = g // 2, g % 2
                    act.wait_ge(sem["brt_out"], 6 * l + g + 1)
                    copy(rounded(BRT[:, 4 * half:4 * half + 4, t * 128:(t + 1) * 128]), PS[:, 2 + g, :].rearrange("p (a b) -> p a b", a=4)).then_inc(sem["brt_evac"], 1)
                for slot in spilled:
                    act.wait_ge(slot, 16 * (SPILLED // 8) * (l + 1))
                for dc in range(8):
                    if dc == 0:
                        act.wait_ge(sem["br_ready"], l + 1)
                    if dc == 2:
                        act.wait_ge(sem["tokens_free"], l + 1)
                    if dc >= 4:
                        act.wait_ge(sem["mix_ready"], 8 * l + dc - 3)
                    act.dma_start(GT[dc % 4], spill[l, dc]).then_inc(gate_in[dc % 4], 16)
                    if dc >= 4:
                        high_parts(Q_BRANCH + dc + 1)
                for dc in range(4, 8):
                    high_parts(Q_BRANCH + dc + 5)
                for k in range(KC):
                    if k < 4:
                        high_parts(Q_OUT + k + 5)
                    act.wait_ge(sem["x1_ready"], 8 * l + k + 1)
                    squares(k)
                root(l, 1)
                if l < L - 1:
                    ada_early(l + 1, 0)
                modulate(l, 1)

                for t in range(TT):
                    act.wait_ge(sem["rt_max"], l + 1)
                    ins = act.activation(AFF[:, t, :], PS[:, 7, 16 * t:16 * t + 16], ACT.Exp, bias=RMX[:, t:t + 1], accum_out=RSUM[:, t:t + 1])
                ins.then_inc(sem["rt_exp"], 1)
                for g in range(6):
                    t, half = g // 2, g % 2
                    act.wait_ge(sem["h2t_out"], 6 * l + g + 1)
                    copy(rounded(H2MH[:, t, 512 * half:512 * half + 512]), PS[:, g, :])
                    copy(H2M[:, t, 512 * half:512 * half + 512], PS[:, g, :]).then_inc(sem["h2t_evac"], 1)
                if l < L - 1:
                    ada_early(l + 1, 2)
                for half in range(2):
                    act.wait_ge(sem["xf_out"], 2 * l + half + 1)
                    copy(XF[0:64, half, :], PS[0:64, half, :])
                    copy(XF[64:128, half, :], PS[0:64, 2 + half, :]).then_inc(sem["xf_evac"], 1)
                for half in range(2):
                    act.wait_ge(sem["xg_out"], 18 * l + half + 1)
                    for grp in range(2):
                        src = PS[:, half, :].rearrange("p (d g n) -> p d g n", d=4, g=2)[:, :, grp, :]
                        ins = copy(XG[:, 4 * half:4 * half + 4, 0:2, grp, :], src.rearrange("p d (e s) -> p d e s", e=2))
                    ins.then_inc(sem["xg_evac"], 1)

                def tanh_a(e):
                    g = l * NE + e
                    act.wait_ge(sem["a_out"], g + 1)
                    if e:
                        act.wait_ge(sem["hh_ready"], g)
                    act.activation(TH, PS[:, 2 * (e % 2), :], ACT.Tanh, scale=0.5).then_inc(sem["a_tanh"], 1)

                def down_side(e):
                    g = l * NE + e
                    act.wait_ge(sem["ht_out"], g + 1)
                    if e >= 2:
                        act.wait_ge(sem["yd_out"], g - 1)
                    copy(HTT[:, e % 2, :, :], PS[:, 4, :].rearrange("p (a b) -> p a b", a=4)).then_inc(sem["ht_evac"], 1)

                def take_y(e):
                    g = l * NE + e
                    act.wait_ge(sem["yd_out"], g + 1)
                    b, eb, o = 5 + e % 2, e // 4, 32 * (e % 4)
                    copy(YS[o:o + 32, eb, 0:512], PS[0:32, b, :])
                    copy(YP[o:o + 32, eb, 0:512], PS[32:64, b, :])
                    copy(YS[o:o + 32, eb, 512:1024], PS[64:96, b, :])
                    copy(YP[o:o + 32, eb, 512:1024], PS[96:128, b, :]).then_inc(sem["yd_evac"], 1)

                tanh_a(0)
                for q in range(16):
                    act.wait_ge(sem["xg_out"], 18 * l + 2 + q + 1)
                    copy(XG[:, q // 2, 2:NE, q % 2, :], PS[:, 4 + q % 4, 0:448].rearrange("p (a b) -> p a b", b=32)).then_inc(sem["xg_evac"], 1)
                for i in range(3):
                    act.wait_ge(sem["sgt_out"], 3 * l + i + 1)
                    if i < 2:
                        ins = copy(SGT[:, 2 * i:2 * i + 2, :], PS[:, 4 + i, :].rearrange("p (a b) -> p a b", a=2))
                    else:
                        ins = copy(SGP, PS[:, 6, :].rearrange("p (a b) -> p a b", a=4))
                    ins.then_inc(sem["sgt_evac"], 1)
                for e in range(1, NE):
                    tanh_a(e)
                    down_side(e - 1)
                    take_y(e - 1)
                down_side(NE - 1)
                take_y(NE - 1)
                if l < L - 1:
                    for k in range(KC):
                        act.wait_ge(sem["x_ready"], 8 * l + k + 1)
                        squares(k)
                    root(l + 1, 0)
            for g in range(6):
                h, t = g // 3, g % 3
                act.wait_ge(sem["yt_out"], g + 1)
                copy(YOUT[:, t, 512 * h:512 * h + 512], PS[:, (4, 5, 7, 0, 1, 2)[g], :]).then_inc(sem["yt_evac"], 1)

        @block.vector
        def _(dve):
            steps = [0]

            def step():
                steps[0] += 1
                return steps[0]

            TTo, TS, STT = dve.tensor_tensor, dve.tensor_scalar, dve.scalar_tensor_tensor

            dve.memset(c32[:, :, :], 0.0).then_inc(dve_step, 1)
            dve.wait_ge(dve_step, step())
            dve.wait_ge(sem["tanh_out"], 1)
            dve.wait_ge(par_in[2], 16)
            TS(small[:, 32:48], small[:, 0:16], 0.5, None, ALU.mult).then_inc(dve_step, 1)
            dve.wait_ge(dve_step, step())
            STT(c32[:, :, 0:2], small[:, 16:32].rearrange("p (a b) -> p a b", a=8), 1.0, small[:, 32:48].rearrange("p (a b) -> p a b", a=8),
                ALU.add, ALU.mult).then_inc(sem["c_ready"], 1)
            dve.wait_ge(sem["c_ready"], 1)
            dve.wait_ge(sem["xT_evac"], 6)
            for l in range(L):
                lam_init = 0.8 - 0.6 * math.exp(-0.3 * l)
                dve.wait_ge(par_in[1], 80 * (l + 1))
                dve.wait_ge(sem["ada_taken"], EARLY * (l + 1))
                TTo(mod[:, 0:16, :], mod[:, 0:16, :], over(CP("b_ada")[:, 0:16], 2, 2), ALU.add).then_inc(dve_step, 1)
                dve.wait_ge(dve_step, step())
                STT(amp[:, 0, :, :], mod[:, 8:16, :], 1.0, over(CP("norm1"), 2, 2), ALU.add, ALU.mult).then_inc(dve_step, 1)
                dve.wait_ge(dve_step, step())

                def modulated(which):
                    dve.wait_ge(sem["rms_ready"], 2 * l + which + 1)
                    dve.reciprocal(RSTD, RSTD).then_inc(dve_step, 1)
                    dve.wait_ge(dve_step, step())
                    for k in range(KC):
                        TTo(hT[:, k, :], xT[:, k, :], RSTD, ALU.mult).then_inc(sem["hx_ready"], 1)
                    dve.wait_ge(sem["hx_ready"], 16 * l + 8 * (which + 1))

                dve.wait_ge(sem["wsm_hi"], l + 1)
                TTo(rounded(wsm[:, :, :]), wsm[:, :, :], rounded(WSMH), ALU.subtract).then_inc(sem["wsm_lo"], 1)

                modulated(0)
                dve.wait_ge(sem["x_stored"], 16 * (l + 1))
                for k in range(KC):
                    dve.wait_ge(sem["h_ready"], 16 * l + k + 1)
                    dve.tensor_copy(rounded(HH_IN[:, k, :]), hT[:, k, :]).then_inc(sem["xh_ready"], 1)
                    if k % 2:
                        dve.wait_ge(sem["xh_ready"], 8 * l + k + 1)
                        TTo(rounded(hT[:, k, :]), hT[:, k, :], rounded(HH_IN[:, k, :]), ALU.subtract).then_inc(sem["hl_odd"], 1)
                dve.memset(TM[:, 0:2, :], 0.0)
                dve.memset(V1[:, :, :, 64:65], 1.0)
                for a in (0, 130, 132, 390):
                    ins = dve.memset(XB[:, :, a:a + 2], 0.0)
                ins.then_inc(dve_step, 1)
                dve.wait_ge(dve_step, step())

                dve.wait_ge(sem["gpre_raw"], l + 1)
                dve.tensor_copy(GRAW[0:24, :], PS[0:24, 7, 0:T]).then_inc(sem["gpre_sb"], 1)
                dve.wait_ge(sem["gpre_out"], l + 1)
                g3 = PS[:, 7, 0:72].rearrange("p (a b) -> p a b", a=TT)
                TTo(G1, g3, over(rowp[:, 0:24], 1, TT), ALU.add).then_inc(dve_step, 1)
                dve.wait_ge(dve_step, step())
                STT(GA, G1, -1.0, G1, ALU.mult, ALU.max).then_inc(sem["gact_in"], 1)
                lam = RP("lambda").rearrange("p (a b c) -> p a b c", a=2, b=2)
                TTo(SS[:, 0:64].rearrange("p (a b) -> p a b", a=2), lam[:, :, 0, :], lam[:, :, 1, :], ALU.mult).then_inc(dve_step, 1)
                dve.wait_ge(dve_step, step())
                dve.tensor_reduce(LAM[:, 0:2], SS[:, 0:64].rearrange("p (a b) -> p a b", a=2), AX.X, ALU.add).then_inc(dve_step, 1)
                dve.wait_ge(dve_step, step())
                dve.wait_ge(sem["gact_out"], l + 1)
                gf = TM[:, 0, :].rearrange("p (t d k h) -> p t d k h", t=TT, d=2, k=2)
                gi = TM[:, 1, :].rearrange("p (t d k h) -> p t d k h", t=TT, d=2, k=2)
                STT(DTM, G1[:, :, 16:24], 0.0, GL[:, :, 16:24], ALU.max, ALU.add).then_inc(dve_step, 1)
                dve.wait_ge(dve_step, step())
                for d in range(2):
                    STT(gf[:, :, d, 0, 0:4], G1[:, :, 8 * d + 4:8 * d + 8], 0.0, GL[:, :, 8 * d + 4:8 * d + 8], ALU.min, ALU.subtract)
                    dve.tensor_copy(gi[:, :, d, 0, 0:4], G1[:, :, 8 * d:8 * d + 4])
                    ins = STT(gf[:, :, d, 1, 0:4], DTM[:, :, 4 * d:4 * d + 4], -1.0, over(AEXP[:, 4 * d:4 * d + 4], 1, TT), ALU.mult, ALU.mult)
                ins.then_inc(sem["gtm_ready"], 1)
                dve.wait_ge(sem["gtm_ready"], l + 1)
                dve.wait_ge(sem["proj_evac"], l * N_PROJ + 11)
                for c in range(4):
                    for jj in range(5):
                        wv = CP("conv_w")[:, 5 * c + jj:5 * c + jj + 1]
                        src = XB[:, c, jj:jj + 388]
                        if jj == 0:
                            ins = TS(CV[:, c, 2:390], src, wv, CP("conv_b")[:, c:c + 1], ALU.mult, ALU.add)
                        else:
                            ins = STT(CV[:, c, 2:390], src, wv, CV[:, c, 2:390], ALU.mult, ALU.add)
                        if jj < 4:
                            ins.then_inc(dve_step, 1)
                            dve.wait_ge(dve_step, step())
                ins.then_inc(sem["conv_ready"], 1)
                dve.wait_ge(sem["conv_ready"], l + 1)

                dve.wait_ge(sem["growT"], l + 1)
                segs = ((0, 128), (128, 384))
                for lo, rev in ((0, False), (64, True)):
                    for a, b in segs:
                        def run(v):
                            v = v[lo:lo + 64, a:b]
                            return v[:, ::-1] if rev else v
                        ins = dve.tensor_tensor_scan(run(ROWS[:, 2, :]), run(PS[:, 4, 0:T]), zeros[lo:lo + 64, :].broadcast_to([64, b - a]), 0.0, ALU.add, ALU.add)
                TS(NM0, CP("m0"), -1.0, None, ALU.mult)
                ins.then_inc(dve_step, 1)
                dve.wait_ge(dve_step, step())
                TTo(ROWS[:, 1, :], ROWS[:, 2, :], PS[:, 5, 0:T], ALU.subtract)
                dve.tensor_copy(ROWS[:, 0, :], ROWS[:, 2, :]).then_inc(dve_step, 1)
                dve.wait_ge(dve_step, step())
                for lo, rev in ((0, False), (64, True)):
                    for i, (a, b) in enumerate(segs):
                        def run(v):
                            v = v[lo:lo + 4, a:b]
                            return v[:, ::-1] if rev else v
                        ins = dve.tensor_tensor_scan(run(ROWS[:, 0, :]), run(ROWS[:, 1, :]), run(ROWS[:, 1, :]),
                                                     NM0[lo:lo + 4, :] if i else 0.0, ALU.min, ALU.min)
                ins.then_inc(sem["rows_ready"], 1)
                dve.wait_ge(sem["rows_ready"], l + 1)
                TTo(MOUT[0:4, 0:1], ROWS[0:4, 2, 127:128], ROWS[0:4, 0, 127:128], ALU.subtract)
                TTo(MOUT[64:68, 1:2], ROWS[64:68, 2, 0:1], ROWS[64:68, 0, 0:1], ALU.subtract).then_inc(sem["m_out"], 1)
                dve.wait_ge(sem["tm_evac"], l + 1)
                tmr, tmn, tmb = (TM[:, i, :].rearrange("p (t d k h) -> p t d k h", t=TT, d=2, k=2) for i in range(3))
                m0 = RP("m0").rearrange("p (d k h) -> p d k h", d=2, k=2)
                for k in range(2):
                    for d in range(2):
                        TTo(WPT[:, :, 8 * k + 4 * d:8 * k + 4 * d + 4], tmr[:, :, d, k, 0:4], over(m0[:, d, k, 0:4], 1, TT), ALU.add)
                for d in range(2):
                    ins = TTo(EMT[:, :, 4 * d:4 * d + 4], tmr[:, :, d, 0, 0:4], tmb[:, :, d, 0, 0:4], ALU.subtract)
                ins.then_inc(sem["tm_ready"], 1)

                dve.wait_ge(sem["silu_t"], l + 1)
                TS(CV[:, :, 2:390], CV[:, :, 2:390], 0.5, None, ALU.mult).then_inc(dve_step, 1)
                dve.wait_ge(dve_step, step())
                STT(XS[:, :, 0:128], XS[:, :, 0:128], 1.0, CV[:, :, 2:130], ALU.add, ALU.mult)
                STT(XS[:, :, 128:384], XS[:, :, 128:384], 1.0, CV[:, :, 134:390], ALU.add, ALU.mult).then_inc(sem["xs_ready"], 1)

                dve.wait_ge(sem["xs_ready"], l + 1)
                sq = W1.rearrange("p (a b) -> p a b", a=TT)
                dve.wait_ge(sem["proj_evac"], l * N_PROJ + 20)
                TTo(sq, NAQK[:, :, :], NAQK[:, :, :], ALU.mult).then_inc(dve_step, 1)
                dve.wait_ge(dve_step, step())
                dve.tensor_reduce(SS[:, 0:24], W1.rearrange("p (a b) -> p a b", b=64), AX.X, ALU.add).then_inc(dve_step, 1)
                dve.wait_ge(dve_step, step())
                TTo(sq, DQK[:, :, :], DQK[:, :, :], ALU.mult).then_inc(dve_step, 1)
                dve.wait_ge(dve_step, step())
                dve.tensor_reduce(SS[:, 24:72], W1.rearrange("p (a b) -> p a b", b=32), AX.X, ALU.add).then_inc(dve_step, 1)
                dve.wait_ge(dve_step, step())
                TS(SS[:, 0:24], SS[:, 0:24], 1.0 / 64, EPS, ALU.mult, ALU.add)
                TS(SS[:, 24:72], SS[:, 24:72], 1.0 / 32, EPS, ALU.mult, ALU.add).then_inc(sem["pool_in"], 1)
                dve.wait_ge(sem["pool_out"], 4 * l + 1)
                na = NAQK.rearrange("p t (g c) -> p (t g) c", c=64)
                TTo(na, na, over(RS[:, 0:24], 2, 64), ALU.mult).then_inc(dve_step, 1)
                dve.wait_ge(dve_step, step())
                for i, name in enumerate(("na_qn", "na_kn")):
                    ins = [TTo(NAQK[:, t, 256 * i:256 * i + 256].rearrange("p (g c) -> p g c", c=64), NAQK[:, t, 256 * i:256 * i + 256].rearrange("p (g c) -> p g c", c=64),
                               over(RP(name), 1, 4), ALU.mult) for t in range(TT)][-1]
                ins.then_inc(sem["nan_ready"], 1)
                df = DQK.rearrange("p t (g c) -> p (t g) c", c=32)
                TTo(df, df, over(RS[:, 24:72], 2, 32), ALU.mult).then_inc(dve_step, 1)
                dve.wait_ge(dve_step, step())
                for i, name in enumerate(("diff_qn", "diff_kn")):
                    for t in range(TT):
                        v = DQK[:, t, 256 * i:256 * i + 256].rearrange("p (g c) -> p g c", c=32)
                        ins = TTo(v, v, over(RP(name), 1, 8), ALU.mult)
                ins.then_inc(dve_step, 1)
                dve.wait_ge(dve_step, step())
                for t in range(2):
                    x4 = DQK[:, 1 + t, :].rearrange("p (g c) -> p g c", c=32)
                    cos = over(K("cos")[:, 32 * t:32 * t + 32], 1, 16)
                    TTo(W1[:, 512 * t:512 * t + 512].rearrange("p (g c) -> p g c", c=32), x4, cos, ALU.mult).then_inc(dve_step, 1)
                    dve.wait_ge(dve_step, step())
                    sin = K("sin")[:, 32 * t:32 * t + 32].rearrange("p (a b c) -> p a b c", a=2, b=2)
                    x5 = DQK[:, 1 + t, :].rearrange("p (g a b c) -> p g a b c", g=16, a=2, b=2)
                    w5 = W2[:, 512 * t:512 * t + 512].rearrange("p (g a b c) -> p g a b c", g=16, a=2, b=2)
                    for b in range(2):
                        ins = TTo(w5[:, :, :, b, :], x5[:, :, :, 1 - b, :], over(sin[:, :, b, :], 1, 16), ALU.mult)
                    ins.then_inc(dve_step, 1)
                    dve.wait_ge(dve_step, step())
                    ins = TTo(DQK[:, 1 + t, :], W1[:, 512 * t:512 * t + 512], W2[:, 512 * t:512 * t + 512], ALU.add)
                dve.wait_ge(sem["tm_exp"], l + 1)
                TTo(LAM[:, 2:3], LAM[:, 1:2], LAM[:, 0:1], ALU.subtract).then_inc(dve_step, 1)
                dve.wait_ge(dve_step, step())
                TS(LAM[:, 3:4], LAM[:, 2:3], -lam_init, None, ALU.add).then_inc(sem["dfn_ready"], 1)
                dve.wait_ge(sem["dfn_ready"], l + 1)

                dve.wait_ge(sem["bm_loaded"], 256 * (l + 1))
                win = over(K("win"), 1, 16)
                for t in range(2):
                    v = BM[:, t, :, :].rearrange("p h (r c) -> p (h r) c", c=64)
                    w_ = W1[:, 0:1024].rearrange("p (a b) -> p a b", a=16)
                    TTo(w_, v[:, :, ::-1], win, ALU.add).then_inc(dve_step, 1)
                    dve.wait_ge(dve_step, step())
                    dve.tensor_copy(v, w_).then_inc(dve_step, 1)
                    dve.wait_ge(dve_step, step())

                na_s = 64 ** -0.5

                def na_in(u):
                    dve.wait_ge(sem["s_out"], 10 * l + u + 1)
                    if u >= 2:
                        dve.wait_ge(sem["p_exp"], 10 * l + u - 1)
                    i = u % 2
                    if u < 2:
                        TS(ED[:, 2 + i, 0:256], PS[:, 2 + i, 0:256], na_s, None, ALU.mult).then_inc(dve_step, 1)
                        dve.wait_ge(dve_step, step())
                        dve.tensor_reduce(SMX[:, i, :], ED[:, 2 + i, 0:256].rearrange("p (a b) -> p a b", a=2), AX.X, ALU.max, negate=True)\
                            .then_inc(sem["s_read"], 1)
                    else:
                        t, h = (u - 2) // 4, (u - 2) % 4
                        TS(ED[:, 2 + i, 256:384], PS[:, 2 + i, 256:384], na_s, None, ALU.mult)
                        STT(ED[:, 2 + i, 0:256], PS[:, 2 + i, 0:256], na_s, BM[:, t, h, :], ALU.mult, ALU.add).then_inc(dve_step, 1)
                        dve.wait_ge(dve_step, step())
                        dve.tensor_reduce(SMX[:, i, 0:1], ED[:, 2 + i, :], AX.X, ALU.max, negate=True).then_inc(sem["s_read"], 1)

                def na_take(u):
                    dve.wait_ge(sem["o_out"], 10 * l + u + 1)
                    i = u % 2
                    dve.wait_ge(sem["p_exp"], 10 * l + u + 1)
                    dve.reciprocal(SREC[:, i, :] if u < 2 else SREC[:, i, 0:1], SSUM[:, i, :] if u < 2 else SSUM[:, i, 0:1]).then_inc(dve_step, 1)
                    dve.wait_ge(dve_step, step())
                    if u < 2:
                        for c in range(2):
                            h = 2 * c + i
                            ins = TS(NAQK[:, 0, h * 64:h * 64 + 64], PS[:, 6 + i, c * 64:c * 64 + 64], SREC[:, i, c:c + 1], None, ALU.mult)
                    else:
                        t, h = 1 + (u - 2) // 4, (u - 2) % 4
                        ins = TS(NAQK[:, t, h * 64:h * 64 + 64], PS[:, 6 + i, 0:64], SREC[:, i, 0:1], None, ALU.mult)
                    ins.then_inc(sem["o_evac"], 1)

                for i in range(12):
                    if i < 10:
                        na_in(i)
                    if i >= 2:
                        na_take(i - 2)

                def df_max(u):
                    dve.wait_ge(sem["ds_out"], 12 * l + u + 1)
                    if u >= 2:
                        dve.wait_ge(sem["dpt_out"], 12 * l + u - 1)
                    i, w = u % 2, (128 if u < 4 else 384)
                    dve.tensor_reduce(SMX[:, i, :], PS[:, 2 + 2 * i:4 + 2 * i, 0:w], AX.X, ALU.max, negate=True).then_inc(dve_step, 1)
                    dve.wait_ge(dve_step, step())
                    TS(DMX[:, i, :], SMX[:, i, :], 32 ** -0.5, None, ALU.mult).then_inc(sem["d_max"], 1)

                def df_mix(u):
                    dve.wait_ge(sem["d_exp"], 12 * l + u + 1)
                    i, w = u % 2, (128 if u < 4 else 384)
                    dve.reciprocal(DREC[:, i, :], DSUM[:, i, :]).then_inc(dve_step, 1)
                    dve.wait_ge(dve_step, step())
                    TS(ED[:, 2 * i, 0:w], ED[:, 2 * i, 0:w], DREC[:, i, 0:1], None, ALU.mult)
                    TTo(DREC[:, i, 1:2], DREC[:, i, 1:2], LAM[:, 3:4], ALU.mult).then_inc(dve_step, 1)
                    dve.wait_ge(dve_step, step())
                    STT(ED[:, 2 * i, 0:w], ED[:, 2 * i + 1, 0:w], DREC[:, i, 1:2], ED[:, 2 * i, 0:w], ALU.mult, ALU.add).then_inc(sem["d_ready"], 1)

                def df_take(u):
                    dve.wait_ge(sem["do_out"], 12 * l + u + 1)
                    t, h = u // 4, u % 4
                    dve.tensor_copy(DQK[:, t, h * 64:h * 64 + 64], PS[:, 7, 0:64]).then_inc(sem["do_evac"], 1)

                for i in range(14):
                    if i < 12:
                        df_max(i)
                    if 1 <= i <= 12:
                        df_mix(i - 1)
                    if i >= 2:
                        df_take(i - 2)

                def head_norm(src, n, c, scale, eps, power, lo):
                    w_ = W2[:, 0:n * c].rearrange("p (a b) -> p a b", a=n)
                    TTo(w_, src, src, ALU.mult).then_inc(dve_step, 1)
                    dve.wait_ge(dve_step, step())
                    dve.tensor_reduce(SS[:, 0:n], w_, AX.X, ALU.add).then_inc(dve_step, 1)
                    dve.wait_ge(dve_step, step())
                    TS(SS[:, 0:n], SS[:, 0:n], scale, eps, ALU.mult, ALU.add).then_inc(sem["pool_in"], 1)
                    dve.wait_ge(sem["pool_out"], power)

                dve.wait_ge(sem["do_evac"], 12 * (l + 1))
                dve.tensor_copy(W1[:, 0:768].rearrange("p (a b) -> p a b", a=TT), DQK[:, :, 0:256]).then_inc(dve_step, 1)
                dve.wait_ge(dve_step, step())
                o3 = W1[:, 0:768].rearrange("p (a b) -> p a b", b=64)
                head_norm(o3, 12, 64, 1.0 / 64, EPS, 4 * l + 2, 0)
                TTo(o3, o3, over(RS[:, 0:12], 2, 64), ALU.mult).then_inc(dve_step, 1)
                dve.wait_ge(dve_step, step())
                for t in range(TT):
                    ins = STT(DQK[:, t, 0:256].rearrange("p (a b) -> p a b", a=4), W1[:, 256 * t:256 * t + 256].rearrange("p (a b) -> p a b", a=4), 1.0 - lam_init,
                              over(RP("diff_norm"), 1, 4), ALU.mult, ALU.mult)
                ins.then_inc(dve_step, 1)
                dve.wait_ge(dve_step, step())

                def decays(kind):
                    def exponent(c):
                        h, d = c // 2, c % 2
                        k = 16 * l + 8 * kind + c
                        dve.wait_ge(sem["row_out"], k + 1)
                        if c >= 2:
                            dve.wait_ge(sem["pm_ready"], k - 1)
                        row = PS[:, 4 + c % 4, :]
                        e = EDf[:, 512 * (c % 2):512 * (c % 2) + 512]
                        bias = [tmn[:, t, d, kind, h:h + 1] for t in range(TT)]
                        M = K("mask")
                        STT(e[:, 0:128], row[:, 0:128], bias[0], M[:, 0:128] if d == 0 else M[:, 256:384], ALU.subtract, ALU.add)
                        if d == 0:
                            STT(e[:, 128:384], row[:, 128:384], bias[1], M[:, 0:256], ALU.subtract, ALU.add)
                            ins = STT(e[:, 384:512], row[:, 256:384], bias[2], M[:, 0:128], ALU.subtract, ALU.add)
                        else:
                            STT(e[:, 128:256], row[:, 128:256], bias[1], M[:, 256:384], ALU.subtract, ALU.add)
                            ins = STT(e[:, 256:512], row[:, 128:384], bias[2], M[:, 128:384], ALU.subtract, ALU.add)
                        ins.then_inc(sem["e_ready"], 1)

                    def scored(c):
                        h, d = c // 2, c % 2
                        k = 16 * l + 8 * kind + c
                        dve.wait_ge(sem["e_exp"], k + 1)
                        dve.wait_ge(sem["sT_out"], 6 * l + (h + 1 if kind == 0 else 5 + h // 2))
                        e = EDf[:, 512 * (c % 2):512 * (c % 2) + 512]
                        dve.tensor_copy(WS[:, 8 * kind + 4 * d + h:8 * kind + 4 * d + h + 1], e[:, 127:128] if d == 0 else e[:, 0:1])
                        if d == 0:
                            TTo(PM[:, c, 0:384], e[:, 0:384], PS[:, 2, 0:384], ALU.mult)
                            ins = TTo(PM[:, c, 384:512], e[:, 384:512], PS[:, 3, 128:256], ALU.mult)
                        else:
                            TTo(PM[:, c, 0:256], e[:, 0:256], PS[:, 2, 0:256], ALU.mult)
                            ins = TTo(PM[:, c, 256:512], e[:, 256:512], PS[:, 3, 0:256], ALU.mult)
                        ins.then_inc(sem["pm_ready"], 1)

                    exponent(0)
                    for c in range(1, 8):
                        exponent(c)
                        scored(c - 1)
                    scored(7)

                decays(0)
                for i, (t, d, b, bq) in enumerate(((0, 0, 2, None), (0, 1, 3, None), (1, 0, 4, 5), (1, 1, 6, 7), (2, 0, 2, 3), (2, 1, 4, 5))):
                    dve.wait_ge(sem["num_out"], 9 * l + i + 1)
                    dst = NUM[:, 2 * t + d, :, :]
                    src = PS[:, b, 0:260].rearrange("p (a b) -> p a b", a=4)
                    if bq is None:
                        ins = dve.tensor_copy(dst, src)
                    else:
                        qc = PS[:, bq, 0:260].rearrange("p (a b) -> p a b", a=4)
                        TTo(dst, qc, over(WPT[:, t, 4 * d:4 * d + 4], 2, 65), ALU.mult).then_inc(dve_step, 1)
                        dve.wait_ge(dve_step, step())
                        ins = TTo(dst, dst, src, ALU.add)
                    ins.then_inc(sem["num_evac"], 1)
                dve.wait_ge(sem["kt_out"], l + 1)
                for d in range(2):
                    ins = TTo(KW[:, d, :, :], PS[:, 6, 0:256].rearrange("p (a b) -> p a b", a=4), over(WS[:, 4 * d:4 * d + 4], 2, 64), ALU.mult)
                ins.then_inc(sem["kw_ready"], 1)
                dve.wait_ge(st_dma["nav"], 16 * (l + 1))
                dve.wait_ge(st_dma["dv"], 16 * (l + 1))
                for d in range(2):
                    for t in range(TT):
                        ins = TTo(XDT[:, d, t, :, :], XTM[:, t, :].rearrange("p (a b) -> p a b", a=4), over(DTM[:, t, 4 * d:4 * d + 4], 2, 64), ALU.mult)
                ins.then_inc(dve_step, 1)
                dve.wait_ge(dve_step, step())
                dve.wait_ge(sem["num_evac"], 9 * l + 6)
                den = NUM[:, :, :, 64:65].rearrange("p a b c -> p (a b c)")
                emt = EMT.rearrange("p a b -> p (a b)")
                STT(SS[:, 0:24], den, -1.0, den, ALU.mult, ALU.max).then_inc(dve_step, 1)
                dve.wait_ge(dve_step, step())
                TTo(SS[:, 0:24], SS[:, 0:24], emt, ALU.max).then_inc(dve_step, 1)
                dve.wait_ge(dve_step, step())
                dve.reciprocal(SS[:, 0:24], SS[:, 0:24]).then_inc(dve_step, 1)
                dve.wait_ge(dve_step, step())
                hn = W2.rearrange("p (a b) -> p a b", a=24)
                TTo(hn, NUM[:, :, :, 0:64].rearrange("p a b c -> p (a b) c"), over(SS[:, 0:24], 2, 64), ALU.mult).then_inc(dve_step, 1)
                dve.wait_ge(dve_step, step())
                hs = NUM.rearrange("p a b c -> p (a b c)")[:, 0:768].rearrange("p (a b) -> p a b", b=64)
                h2 = W2.rearrange("p (t d h c) -> p t d (h c)", t=TT, d=2, h=4)
                hs3 = NUM.rearrange("p a b c -> p (a b c)")[:, 0:768].rearrange("p (t c) -> p t c", t=TT)
                TTo(hs3, h2[:, :, 0, :], h2[:, :, 1, :], ALU.add).then_inc(dve_step, 1)
                dve.wait_ge(dve_step, step())
                head_norm(hs, 12, 64, 4.0 / 64, 4 * EPS, 4 * l + 3, 0)
                TTo(hs, hs, over(RS[:, 0:12], 2, 64), ALU.mult).then_inc(dve_step, 1)
                dve.wait_ge(dve_step, step())
                TTo(hs3, hs3, over(RP("mlstm_norm"), 1, TT), ALU.mult).then_inc(dve_step, 1)
                dve.wait_ge(dve_step, step())
                dve.wait_ge(sem["tanh_out"], 1 + (l + 1))
                STT(MO[:, :, :], W1[:, 0:768].rearrange("p (a b) -> p a b", a=TT), 1.0, hs3, ALU.add, ALU.mult).then_inc(dve_step, 1)
                dve.wait_ge(dve_step, step())

                decays(1)
                Y = NUM.rearrange("p a b c -> p (a b c)")[:, 0:768].rearrange("p (t c) -> p t c", t=TT)
                for t, b, bq in ((0, 2, None), (1, 3, (4, 5)), (2, 6, (7, 2))):
                    dve.wait_ge(sem["num_out"], 9 * l + 7 + t)
                    y4 = Y[:, t, :].rearrange("p (a b) -> p a b", a=4)
                    TTo(y4, XTM[:, t, :].rearrange("p (a b) -> p a b", a=4), over(RP("ssm_d"), 2, 64), ALU.mult).then_inc(dve_step, 1)
                    dve.wait_ge(dve_step, step())
                    if bq is not None:
                        for g in range(2):
                            qc = PS[:, bq[g], 0:256].rearrange("p (a b c) -> p a b c", a=2, b=2)
                            for d in range(2):
                                w_ = W2[:, 256 * g + 128 * d:256 * g + 128 * d + 128].rearrange("p (b c) -> p b c", b=2)
                                ins = TTo(w_, qc[:, d, :, :], over(WPT[:, t, 8 + 4 * d + 2 * g:8 + 4 * d + 2 * g + 2], 2, 64), ALU.mult)
                        ins.then_inc(dve_step, 1)
                        dve.wait_ge(dve_step, step())
                        for d in range(2):
                            w_ = W2[:, 0:512].rearrange("p (g d c) -> p g d c", g=2, d=2)[:, :, d, :]
                            y3 = Y[:, t, :].rearrange("p (g c) -> p g c", g=2)
                            TTo(y3, y3, w_, ALU.add).then_inc(dve_step, 1)
                            dve.wait_ge(dve_step, step())
                    TTo(Y[:, t, :], Y[:, t, :], PS[:, b, 0:256], ALU.add).then_inc(sem["num_evac"], 1)
                for d in range(2):
                    ins = TTo(KW[:, d, :, :], XDT[:, d, 0, :, :], over(WS[:, 8 + 4 * d:12 + 4 * d], 2, 64), ALU.mult)
                ins.then_inc(sem["kw_ready"], 1)
                dve.wait_ge(sem["num_evac"], 9 * (l + 1))
                STT(SZ[:, :, :], W1[:, 768:1536].rearrange("p (a b) -> p a b", a=TT), 1.0, SZ[:, :, :], ALU.add, ALU.mult).then_inc(dve_step, 1)
                dve.wait_ge(dve_step, step())
                TTo(Y, Y, SZ[:, :, :], ALU.mult).then_inc(dve_step, 1)
                dve.wait_ge(dve_step, step())
                head_norm(Y, 3, 256, 1.0 / 256, 4 * EPS, 4 * (l + 1), 0)
                TTo(Y, Y, over(RS[:, 0:3], 2, 256), ALU.mult).then_inc(dve_step, 1)
                dve.wait_ge(dve_step, step())
                TTo(SZ[:, :, :], Y, over(RP("ssm_norm"), 1, TT), ALU.mult).then_inc(sem["br_ready"], 1)

                dve.wait_ge(sem["job_evac"], NJ * l + JOBS.index(("sum", 7)) + 1)
                TTo(mod[:, 16:48, :], mod[:, 16:48, :], over(CP("b_ada")[:, 16:48], 2, 2), ALU.add).then_inc(dve_step, 1)
                dve.wait_ge(dve_step, step())
                STT(amp[:, 1, :, :], mod[:, 32:40, :], 1.0, over(CP("norm2"), 2, 2), ALU.add, ALU.mult)
                TS(mod[:, 16:24, :], mod[:, 16:24, :], 0.5, None, ALU.mult)
                TS(mod[:, 40:48, :], mod[:, 40:48, :], 0.5, None, ALU.mult).then_inc(dve_step, 1)
                dve.wait_ge(dve_step, step())
                for g in range(6):
                    t, half = g // 2, g % 2
                    dve.wait_ge(sem["brt_evac"], 6 * l + g + 1)
                    o = (slice(None), slice(4 * half, 4 * half + 4), slice(t * 128, (t + 1) * 128))
                    TTo(rounded(BRTL[o]), PS[:, 2 + g, :].rearrange("p (a b) -> p a b", a=4), rounded(BRT[o]), ALU.subtract).then_inc(sem["brt_lo"], 1)
                dve.wait_ge(sem["brt_evac"], 6 * (l + 1))
                for name, k in (("nak", 1), ("nav", 1), ("dk", 1), ("dv", 1), ("C", 2), ("n", 2), ("ssm", 1)):
                    dve.wait_ge(st_dma[name], 16 * k * (l + 1))
                dve.memset(TMPB[:, 0, 0:1], 0.0).then_inc(sem["tokens_free"], 1)
                dve.wait_ge(sem["tokens_free"], l + 1)
                for dc in range(8):
                    dve.wait_ge(sem["bp_out"], 8 * l + dc + 1)
                    dve.wait_ge(gate_in[dc % 4], 16 * (2 * l + dc // 4 + 1))
                    b = 4 * (dc % 2)
                    STT(TMPB[:, 0:3, :], GT[dc % 4], 1.0, PS[:, b:b + 3, 0:T], ALU.add, ALU.mult)
                    STT(TMPB[:, 3, :], GATES[:, dc, :], 1.0, PS[:, b + 3, 0:T], ALU.add, ALU.mult).then_inc(sem["bp_evac"], 1)
                    dve.wait_ge(sem["bp_evac"], 8 * l + dc + 1)
                    TTo(TMPB[:, 0:2, :], TMPB[:, 0:2, :], TMPB[:, 2:4, :], ALU.add).then_inc(dve_step, 1)
                    dve.wait_ge(dve_step, step())
                    TTo(MIX[:, dc, :], TMPB[:, 0, :], TMPB[:, 1, :], ALU.add).then_inc(dve_step, 1)
                    dve.wait_ge(dve_step, step())
                    dve.tensor_copy(rounded(MIXH[:, dc, :]), MIX[:, dc, :]).then_inc(sem["mix_ready"], 1)
                    dve.wait_ge(sem["mix_ready"], 8 * l + dc + 1)
                for dc in range(8):
                    if dc == 0:
                        dve.wait_ge(sem["x_back"], 16 * (l + 1))
                    dve.wait_ge(sem["wo_out"], 8 * l + dc + 1)
                    for g, (a, b) in enumerate(segs):
                        ins = STT(xT[:, dc, a:b], PS[:, 2 + dc % 4, a:b], mod[:, 16 + dc, g:g + 1], xT[:, dc, a:b], ALU.mult, ALU.add)
                    ins.then_inc(sem["x1_ready"], 1)
                dve.wait_ge(sem["x1_ready"], 8 * (l + 1))
                modulated(1)

                dve.wait_ge(sem["rt_raw"], l + 1)
                dve.tensor_copy(RRAW[0:NE, :], PS[0:NE, 7, 0:T]).then_inc(sem["rt_sb"], 1)
                dve.wait_ge(sem["rt_out"], l + 1)
                dve.tensor_reduce(RMX, PS[:, 7, 0:48].rearrange("p (a b) -> p a b", a=TT), AX.X, ALU.max, negate=True).then_inc(sem["rt_max"], 1)
                dve.wait_ge(sem["rt_exp"], l + 1)
                dve.reciprocal(RSUM, RSUM).then_inc(dve_step, 1)
                dve.wait_ge(dve_step, step())
                TTo(AFF, AFF, over(RSUM, 2, NE), ALU.mult).then_inc(sem["aff_ready"], 1)
                dve.wait_ge(sem["afT"], l + 1)
                dve.tensor_copy(WK[0:NE, :], PS[0:NE, 6, 0:T]).then_inc(dve_step, 1)
                dve.wait_ge(dve_step, step())
                for (a, b), rounds in zip(segs, (2, 4)):
                    for _ in range(rounds):
                        dve.max(TOP[0:NE, :], WK[0:NE, a:b]).then_inc(dve_step, 1)
                        dve.wait_ge(dve_step, step())
                        dve.match_replace(WK[0:NE, a:b], TOP[0:NE, :], WK[0:NE, a:b], -1.0).then_inc(dve_step, 1)
                        dve.wait_ge(dve_step, step())
                TS(MSK[0:NE, :], WK[0:NE, :], 0.0, None, ALU.is_lt).then_inc(dve_step, 1)
                dve.wait_ge(dve_step, step())
                for a, b in segs:
                    ins = dve.tensor_tensor_scan(AFT[0:NE, a:b], MSK[0:NE, a:b], zeros[0:NE, :].broadcast_to([NE, b - a]), 0.0, ALU.add, ALU.add)
                ins.then_inc(dve_step, 1)
                dve.wait_ge(dve_step, step())
                TTo(WK[0:NE, :], AFT[0:NE, :], MSK[0:NE, :], ALU.mult).then_inc(sem["pos_ready"], 1)
                dve.wait_ge(sem["posT"], l + 1)
                TS(POS, PS[:, 7, 0:48].rearrange("p (a b) -> p a b", a=TT), -1.0, None, ALU.add).then_inc(dve_step, 1)
                dve.wait_ge(dve_step, step())
                for t in range(TT):
                    TTo(rounded(SEL[:, t, :, :]), over(K("iota"), 1, NE), over(POS[:, t, :], 2, 32), ALU.is_equal).then_inc(sem["sel_ready"], 1)
                dve.wait_ge(sem["sel_ready"], 3 * (l + 1))
                for t in range(TT):
                    ins = TTo(SELG[:, t, :, :], rounded(SEL[:, t, :, :]), over(AFF[:, t, :], 2, 32), ALU.mult)
                ins.then_inc(sem["selg_ready"], 1)

                def add_back(bank, dc, signal):
                    for g, (a, b) in enumerate(segs):
                        ins = STT(xT[:, dc, a:b], PS[:, bank, a:b], mod[:, 40 + dc, g:g + 1], xT[:, dc, a:b], ALU.mult, ALU.add)
                    ins.then_inc(sem[signal], 1)

                def add_early(n):
                    dve.wait_ge(sem["early_out"], 24 * l + n + 1)
                    if n >= 8:
                        dve.wait_ge(sem["early_taken"], 24 * l + n - 7)
                    add_back(7, n % 8, "early_taken")

                for e in range(NE):
                    g = l * NE + e
                    units = COMBINED.get(e, ())
                    for n in units[:2]:
                        add_early(n)
                    dve.wait_ge(sem["a_tanh"], g + 1)
                    if e == 0:
                        dve.wait_ge(sem["sgt_evac"], 3 * (l + 1))
                    if e >= 2:
                        dve.wait_ge(sem["ht_out"], g - 1)
                    STT(SA, TH, 1.0, PS[:, 2 * (e % 2), :], ALU.add, ALU.mult).then_inc(dve_step, 1)
                    dve.wait_ge(dve_step, step())
                    dve.wait_ge(sem["u_out"], g + 1)
                    TTo(HH[:, e % 2, :], SA, PS[:, 2 * (e % 2) + 1, :], ALU.mult).then_inc(sem["hh_ready"], 1)
                    for n in units[2:]:
                        add_early(n)
                dve.wait_ge(sem["early_taken"], 24 * (l + 1))
                for dc in range(8):
                    dve.wait_ge(sem["cb_out"], 8 * l + dc + 1)
                    add_back(dc % 4, dc, "x_ready")


_WEIGHTS = ["w_ada", "w_in", "w_branch", "w_out", "w_router", "w_gate", "w_up", "w_down"]
_PLAIN = ["x_prompt", "x_sample", "cache_na_k", "cache_na_v", "cache_diff_k", "cache_diff_v"] + _WEIGHTS
_OUTS = [(1, 128, 1024), (1, 256, 1024), (1, 2, 128, 4, 64), (1, 2, 128, 4, 64), (1, 2, 128, 4, 64), (1, 2, 128, 4, 64),
         (1, 2, 2, 4, 64, 64), (1, 2, 2, 4, 64), (1, 2, 2, 4), (1, 2, 2, 4, 64, 64)]


def laid_out(i):
    a = {k: np.asarray(v) for k, v in i.items()}
    f = np.float32
    rows = {"gate_b": a["mlstm_gate_b"].reshape(L, 16), "dt_bias": a["ssm_dt_bias"].reshape(L, 8), "a_log": a["ssm_a_log"].reshape(L, 8),
            "ssm_d": a["ssm_d"], "na_qn": a["na_qnorm_w"], "na_kn": a["na_knorm_w"], "diff_qn": a["diff_qnorm_w"],
            "diff_kn": a["diff_knorm_w"], "diff_norm": a["diff_norm_w"], "mlstm_norm": a["mlstm_norm_w"], "ssm_norm": a["ssm_norm_w"],
            "lambda": a["diff_lambda"].reshape(L, 128)}
    m0 = np.zeros((L, 2, 2, 32), f)
    m0[:, :, 0, 0:4] = a["state_mlstm_m"][0]
    rows["m0"] = m0.reshape(L, 128)
    rowp = np.zeros((L, NROW), f)
    for n, v in rows.items():
        rowp[:, ROW[n][0]:ROW[n][0] + ROW[n][1]] = v
    cols = {"norm1": a["norm1_w"].reshape(L, 8, 128), "norm2": a["norm2_w"].reshape(L, 8, 128), "b_ada": a["b_ada"].reshape(L, 48, 128),
            "conv_w": a["ssm_conv_w"].reshape(L, 5, 4, 128).transpose(0, 2, 1, 3).reshape(L, 20, 128),
            "conv_b": a["ssm_conv_b"].reshape(L, 4, 128), "m0": m0.reshape(L, 1, 128)}
    colp = np.zeros((L, 128, NCOL), f)
    for n, v in cols.items():
        colp[:, :, COL[n][0]:COL[n][0] + COL[n][1]] = v.transpose(0, 2, 1)
    cn = np.concatenate([a["state_mlstm_C"][0], a["state_mlstm_n"][0][..., None]], -1)
    cn = cn.reshape(L, 2, 2, 2, 64, 65).transpose(0, 3, 4, 2, 1, 5)
    c0n = np.zeros((L, 2, 64, 2, 2, 2, 65), f)
    for h in range(2):
        c0n[:, h, :, :, :, h] = cn[:, h]
    c0n = c0n.reshape(L, 128, 520)
    h0t = a["state_ssm"][0].reshape(L, 2, 2, 2, 64, 64).transpose(0, 2, 5, 1, 3, 4).reshape(L, 128, 256)
    cvec = np.stack([a["c_ctx"].reshape(8, 128), a["c"][0].reshape(8, 128)], -1).transpose(1, 0, 2).reshape(128, 16)
    rpb_rev = a["na_rpb"][:, :, :, ::-1].reshape(L * 4 * 15 * 31)
    return {"rowp": rowp, "colp": colp, "c0n": c0n, "h0t": h0t, "cvec": cvec, "rpb_rev": rpb_rev, "consts": constants()}


def kernel(**inputs):
    import concourse.bacc as _bacc
    from concourse.bass_utils import run_bass_kernel_spmd as _run

    nc = _bacc.Bacc("TRN2", target_bir_lowering=False, num_devices=1)
    arrays, dr = {}, {}
    given = {n: inputs[n] for n in _PLAIN}
    given.update(laid_out(inputs))
    for name, v in given.items():
        v = np.ascontiguousarray(v)
        arrays[f"in_{name}"] = v
        dr[name] = nc.dram_tensor(f"in_{name}", v.shape, F32, kind="ExternalInput").ap()
    outs = [nc.dram_tensor(f"out_{i}", shape, F32, kind="ExternalOutput").ap() for i, shape in enumerate(_OUTS)]
    trunk_program(nc, dr, outs)
    r = _run(nc, [arrays], core_ids=[0])
    return tuple(r.results[0][f"out_{i}"] for i in range(len(_OUTS)))
```
